# Optimizing a Trainium2 kernel written in Bass

```python
import jax, jax.numpy as jnp
from jax import lax
import numpy as np

D_MODEL = 1024
BATCH = 1
SEQ = 1024
DEPTH = 2
DEC_BATCH = 8
DEC_SEQ = 1
PAST_LEN = 1024
PAGE_SIZE = 128

HEAD_DIM = 64
N_A_HEADS = 8
A_WIDTH = N_A_HEADS * HEAD_DIM
N_Q_HEADS = 8
N_KV_HEADS = 2
GQA_GROUP = N_Q_HEADS // N_KV_HEADS
B_WIDTH = N_Q_HEADS * HEAD_DIM
KV_WIDTH = N_KV_HEADS * HEAD_DIM
MIX_WIDTH = A_WIDTH + B_WIDTH
DECAY_LORA = 64
AAA_LORA = 64
GATE_LORA = 160
A_PROJ = 3 * A_WIDTH + DECAY_LORA + AAA_LORA + GATE_LORA
B_PROJ = B_WIDTH + 2 * KV_WIDTH
IN_PROJ = A_PROJ + B_PROJ
WINDOW = 128
BLOCK = WINDOW
WIN_BUF = min(WINDOW, PAST_LEN)
D_FF = -(-8 * D_MODEL // (3 * 256)) * 256
ROPE_THETA = 10000.0
NORM_EPS = 1e-5
LNX_EPS = 64e-5
ATTN_SCALE = HEAD_DIM ** -0.5

kernel_name = "hybrid_rwkv7_swa_sink_decoder_step"

F32 = jnp.float32

def rmsnorm(x, g):
    xf = x.astype(F32)
    y = xf * lax.rsqrt(jnp.mean(xf * xf, axis=-1, keepdims=True) + NORM_EPS)
    return (y * g.astype(F32)).astype(x.dtype)

def rope(x, positions):
    half = HEAD_DIM // 2
    inv = ROPE_THETA ** (-jnp.arange(half, dtype=F32) / half)
    ang = positions.astype(F32)[:, None] * inv[None, :]
    cos = jnp.cos(ang)[:, None, :]
    sin = jnp.sin(ang)[:, None, :]
    xf = x.astype(F32)
    x1, x2 = xf[..., :half], xf[..., half:]
    return jnp.concatenate([x1 * cos - x2 * sin, x2 * cos + x1 * sin], axis=-1).astype(x.dtype)

def sink_softmax(s, mask, sink):
    s = jnp.where(mask, s, -jnp.inf)
    m = jnp.maximum(jnp.max(s, axis=-1, keepdims=True), sink)
    p = jnp.exp(s - m)
    return p / (jnp.sum(p, axis=-1, keepdims=True) + jnp.exp(sink - m))

def rwkv7_scan(r, decay, k, v, a_, b_, S0):
    def step(S, inp):
        r_t, w_t, k_t, v_t, a_t, b_t = inp
        sa = jnp.einsum('bhij,bhj->bhi', S, a_t)
        S = S * w_t[:, :, None, :] + sa[..., None] * b_t[:, :, None, :] + v_t[..., None] * k_t[:, :, None, :]
        y = jnp.einsum('bhij,bhj->bhi', S, r_t)
        return S, y
    seq = tuple(jnp.swapaxes(t, 0, 1) for t in (r, decay, k, v, a_, b_))
    S, y = lax.scan(step, S0, seq)
    return jnp.swapaxes(y, 0, 1), S

def rwkv7_mix(pa, shift_prev, S0, W, l):
    Bn, T, _ = pa.shape
    prev = jnp.concatenate([shift_prev[:, None].astype(pa.dtype), pa[:, :-1]], axis=1)
    xs = pa + W['mu'][l] * (prev - pa)
    r, k, v, wlo, alo, glo = jnp.split(
        xs, [A_WIDTH, 2 * A_WIDTH, 3 * A_WIDTH, 3 * A_WIDTH + DECAY_LORA, 3 * A_WIDTH + DECAY_LORA + AAA_LORA], axis=-1)
    w = -jax.nn.softplus(-(W['w0'][l] + jnp.tanh(wlo) @ W['w_decay_up'][l]).astype(F32)) - 0.5
    decay = jnp.exp(-jnp.exp(w))
    a = jax.nn.sigmoid((W['a0'][l] + alo @ W['w_a_up'][l]).astype(F32))
    g = jax.nn.sigmoid(glo) @ W['w_g_up'][l]
    hs = lambda t: t.reshape(Bn, T, N_A_HEADS, HEAD_DIM)
    kk = hs((k * W['k_k'][l]).astype(F32))
    kk = kk / jnp.maximum(jnp.sqrt(jnp.sum(kk * kk, axis=-1, keepdims=True)), 1e-12)
    k_mod = k.astype(F32) * (1.0 + (a - 1.0) * W['k_a'][l].astype(F32))
    rh, kh, vh, ah, dh = hs(r.astype(F32)), hs(k_mod), hs(v.astype(F32)), hs(a), hs(decay)
    y, S = rwkv7_scan(rh, dh, kh, vh, -kk, kk * ah, S0.astype(F32))
    mean = jnp.mean(y, axis=-1, keepdims=True)
    var = jnp.mean(jnp.square(y - mean), axis=-1, keepdims=True)
    yn = ((y - mean) * lax.rsqrt(var + LNX_EPS)).reshape(Bn, T, A_WIDTH)
    yn = yn * W['lnx_g'][l].astype(F32) + W['lnx_b'][l].astype(F32)
    bonus = (jnp.sum(rh * kh * W['r_k'][l].astype(F32), axis=-1, keepdims=True) * vh).reshape(Bn, T, A_WIDTH)
    out = (yn + bonus) * g.astype(F32)
    return out.astype(pa.dtype), pa[:, -1], S

def swa_banded(q, k, v, sink):
    Bn, T = q.shape[0], q.shape[1]
    nb = T // BLOCK
    qb = q.reshape(Bn, nb, BLOCK, N_KV_HEADS, GQA_GROUP, HEAD_DIM)

    def band(t):
        tb = t.reshape(Bn, nb, BLOCK, N_KV_HEADS, HEAD_DIM)
        prev = jnp.concatenate([jnp.zeros_like(tb[:, :1]), tb[:, :-1]], axis=1)
        return jnp.concatenate([prev, tb], axis=2)

    kb, vb = band(k), band(v)
    s = jnp.einsum('bnqkgd,bnskd->bnkgqs', qb, kb).astype(F32) * ATTN_SCALE
    i = jnp.arange(BLOCK)
    j = jnp.arange(2 * BLOCK)
    n = jnp.arange(nb)
    diff = i[:, None] - j[None, :] + BLOCK
    kpos = n[:, None] * BLOCK - BLOCK + j[None, :]
    mask = ((diff >= 0) & (diff < WINDOW))[None] & (kpos >= 0)[:, None, :]
    mask = mask[None, :, None, None]
    p = sink_softmax(s, mask, sink[None, None, :, :, None, None])
    o = jnp.einsum('bnkgqs,bnskd->bnqkgd', p.astype(vb.dtype), vb)
    return o.reshape(Bn, T, B_WIDTH)

def swa_step(q, k, v, kbuf, vbuf, sink, positions):
    Bn, T = q.shape[0], q.shape[1]
    kc = jnp.concatenate([kbuf.astype(k.dtype), k], axis=1)
    vc = jnp.concatenate([vbuf.astype(v.dtype), v], axis=1)
    qg = q.reshape(Bn, T, N_KV_HEADS, GQA_GROUP, HEAD_DIM)
    s = jnp.einsum('btkgd,bskd->bkgts', qg, kc).astype(F32) * ATTN_SCALE
    kpos = positions[0] - WIN_BUF + jnp.arange(WIN_BUF + T)
    diff = positions[:, None] - kpos[None, :]
    mask = ((diff >= 0) & (diff < WINDOW))[None, None, None]
    p = sink_softmax(s, mask, sink[None, :, :, None, None])
    o = jnp.einsum('bkgts,bskd->btkgd', p.astype(vc.dtype), vc).reshape(Bn, T, B_WIDTH)
    return o, kc[:, -WIN_BUF:], vc[:, -WIN_BUF:]

def decoder_layer(x, l, positions, shift_prev, S0, kbuf, vbuf, W):
    Bn, T, _ = x.shape
    h = rmsnorm(x, W['attn_norm'][l])
    proj = h @ W['w_in'][l]
    pa, pb = proj[..., :A_PROJ], proj[..., A_PROJ:]
    ya, new_shift, S_new = rwkv7_mix(pa, shift_prev, S0, W, l)
    q = pb[..., :B_WIDTH].reshape(Bn, T, N_Q_HEADS, HEAD_DIM)
    k = pb[..., B_WIDTH:B_WIDTH + KV_WIDTH].reshape(Bn, T, N_KV_HEADS, HEAD_DIM)
    v = pb[..., B_WIDTH + KV_WIDTH:].reshape(Bn, T, N_KV_HEADS, HEAD_DIM)
    q = rope(q, positions)
    k = rope(k, positions)
    sink = W['sinks'][l].reshape(N_KV_HEADS, GQA_GROUP).astype(F32)
    if kbuf is None:
        yb = swa_banded(q, k, v, sink)
        new_k, new_v = k[:, T - WIN_BUF:], v[:, T - WIN_BUF:]
    else:
        yb, new_k, new_v = swa_step(q, k, v, kbuf, vbuf, sink, positions)
    mixed = jnp.concatenate([ya, yb.astype(ya.dtype)], axis=-1) @ W['w_out'][l]
    x = x + mixed
    h2 = rmsnorm(x, W['ffn_norm'][l])
    x = x + (jax.nn.silu(h2 @ W['w_gate'][l]) * (h2 @ W['w_up'][l])) @ W['w_down'][l]
    return x, new_shift, S_new, new_k, new_v

def setup_inputs(seed: int = 0) -> dict:
    key = jax.random.key(seed)
    ks = iter(jax.random.split(key, 32))
    nrm = lambda shape, scale: scale * jax.random.normal(next(ks), shape, F32)
    x_prompt = nrm((BATCH, SEQ, D_MODEL), 1.0)
    x_sample = nrm((DEC_BATCH, DEC_SEQ, D_MODEL), 1.0)
    state_rwkv = nrm((DEPTH, DEC_BATCH, N_A_HEADS, HEAD_DIM, HEAD_DIM), 0.2)
    state_shift = nrm((DEPTH, DEC_BATCH, A_PROJ), 1.0)
    cache_k_win = nrm((DEPTH, DEC_BATCH, WIN_BUF, N_KV_HEADS, HEAD_DIM), 1.0)
    cache_v_win = nrm((DEPTH, DEC_BATCH, WIN_BUF, N_KV_HEADS, HEAD_DIM), 1.0)
    attn_norm = 1.0 + nrm((DEPTH, D_MODEL), 0.02)
    w_in = nrm((DEPTH, D_MODEL, IN_PROJ), D_MODEL ** -0.5)
    mu = jax.random.uniform(next(ks), (DEPTH, A_PROJ), F32)
    w0 = jax.random.uniform(next(ks), (DEPTH, A_WIDTH), F32, -6.0, -0.5)
    w_decay_up = nrm((DEPTH, DECAY_LORA, A_WIDTH), 0.1 * DECAY_LORA ** -0.5)
    a0 = nrm((DEPTH, A_WIDTH), 0.1)
    w_a_up = nrm((DEPTH, AAA_LORA, A_WIDTH), 0.5 * AAA_LORA ** -0.5)
    w_g_up = nrm((DEPTH, GATE_LORA, A_WIDTH), GATE_LORA ** -0.5)
    k_k = 0.85 + nrm((DEPTH, A_WIDTH), 0.05)
    k_a = 1.0 + nrm((DEPTH, A_WIDTH), 0.05)
    r_k = nrm((DEPTH, N_A_HEADS, HEAD_DIM), 0.1)
    lnx_g = 1.0 + nrm((DEPTH, A_WIDTH), 0.02)
    lnx_b = nrm((DEPTH, A_WIDTH), 0.02)
    sinks = nrm((DEPTH, N_Q_HEADS), 0.5)
    w_out = nrm((DEPTH, MIX_WIDTH, D_MODEL), MIX_WIDTH ** -0.5)
    ffn_norm = 1.0 + nrm((DEPTH, D_MODEL), 0.02)
    w_gate = nrm((DEPTH, D_MODEL, D_FF), D_MODEL ** -0.5)
    w_up = nrm((DEPTH, D_MODEL, D_FF), D_MODEL ** -0.5)
    w_down = nrm((DEPTH, D_FF, D_MODEL), D_FF ** -0.5)
    final_norm = 1.0 + nrm((D_MODEL,), 0.02)
    return {"x_prompt": x_prompt, "x_sample": x_sample, "state_rwkv": state_rwkv, "state_shift": state_shift,
            "cache_k_win": cache_k_win, "cache_v_win": cache_v_win, "attn_norm": attn_norm, "w_in": w_in,
            "mu": mu, "w0": w0, "w_decay_up": w_decay_up, "a0": a0, "w_a_up": w_a_up, "w_g_up": w_g_up,
            "k_k": k_k, "k_a": k_a, "r_k": r_k, "lnx_g": lnx_g, "lnx_b": lnx_b, "sinks": sinks,
            "w_out": w_out, "ffn_norm": ffn_norm, "w_gate": w_gate, "w_up": w_up, "w_down": w_down,
            "final_norm": final_norm}

def reference(x_prompt, x_sample, state_rwkv, state_shift, cache_k_win, cache_v_win, attn_norm, w_in, mu, w0,
              w_decay_up, a0, w_a_up, w_g_up, k_k, k_a, r_k, lnx_g, lnx_b, sinks, w_out, ffn_norm, w_gate, w_up,
              w_down, final_norm):
    W = dict(attn_norm=attn_norm, w_in=w_in, mu=mu, w0=w0, w_decay_up=w_decay_up, a0=a0, w_a_up=w_a_up,
             w_g_up=w_g_up, k_k=k_k, k_a=k_a, r_k=r_k, lnx_g=lnx_g, lnx_b=lnx_b, sinks=sinks, w_out=w_out,
             ffn_norm=ffn_norm, w_gate=w_gate, w_up=w_up, w_down=w_down)
    Bp, Tp = x_prompt.shape[0], x_prompt.shape[1]
    Ts = x_sample.shape[1]
    pos_p = jnp.arange(Tp, dtype=jnp.int32)
    pos_s = PAST_LEN + jnp.arange(Ts, dtype=jnp.int32)
    xp, xs = x_prompt, x_sample
    p_S, p_sh, p_k, p_v = [], [], [], []
    s_S, s_sh, s_k, s_v = [], [], [], []
    for l in range(DEPTH):
        shift0 = jnp.zeros((Bp, A_PROJ), xp.dtype)
        S0 = jnp.zeros((Bp, N_A_HEADS, HEAD_DIM, HEAD_DIM), F32)
        xp, sh, S, kw, vw = decoder_layer(xp, l, pos_p, shift0, S0, None, None, W)
        p_S.append(S); p_sh.append(sh); p_k.append(kw); p_v.append(vw)
        xs, sh, S, kw, vw = decoder_layer(xs, l, pos_s, state_shift[l], state_rwkv[l], cache_k_win[l],
                                          cache_v_win[l], W)
        s_S.append(S); s_sh.append(sh); s_k.append(kw); s_v.append(vw)
    y_prompt = rmsnorm(xp, final_norm)
    y_sample = rmsnorm(xs, final_norm)
    return (y_prompt, y_sample, jnp.stack(p_S), jnp.stack(p_sh), jnp.stack(p_k), jnp.stack(p_v),
            jnp.stack(s_S), jnp.stack(s_sh), jnp.stack(s_k), jnp.stack(s_v))


_drawn_inputs = setup_inputs


def setup_inputs(seed=0):
    import zlib

    import numpy as np

    out = dict(_drawn_inputs(seed))
    spreads = {}
    factors = {'w_decay_up': 8.0,
     'lnx_g': 5.024,
     'lnx_b': 4.817,
     'sinks': 8.0,
     'ffn_norm': 2.679,
     'final_norm': 2.802}
    for name, (base, spread) in spreads.items():
        noise = np.random.default_rng([zlib.crc32(name.encode()), seed]).standard_normal(out[name].shape)
        drawn = base * np.exp(spread * noise) if base else spread * noise
        out[name] = __import__('jax').numpy.asarray(drawn.astype(out[name].dtype))
    for name, factor in factors.items():
        out[name] = (out[name] * factor).astype(out[name].dtype)
    return out
```

```python
from contextlib import ExitStack, contextmanager

import numpy as np

import concourse.bass as bass
from concourse import mybir

F32 = mybir.dt.float32
F32R = mybir.dt.float32r
ALU = mybir.AluOpType
ACT = mybir.ActivationFunctionType
AX = mybir.AxisListType

L = 2
DM = 1024
KT = DM // 128
NP_, NS = 1024, 8
T = NP_ + NS
NC3, CW = 3, T // 3
HD = 64
NPAIR = 4
CH = 64
NCH = NP_ // CH
FF = 2816
NFF = FF // 128
NIN = 21
UL = NIN + KT + 3 * NFF
U = 1024
WIN = 128
CDEC = float(np.exp(-0.5))
SCALE = HD ** -0.5
EPS, LNX_EPS = 1e-5, 64e-5
ENGINES = ("tensor", "vector", "scalar", "pool")
CREDIT = 6000

PAR = {}
_at = 0
for _n, _w in (("an", 8), ("fn", 8), ("mu", 15), ("w0", 4), ("a0", 4), ("k_k", 4), ("k_a", 4), ("r_k", 4),
               ("lg", 4), ("lb", 4), ("sink", 8), ("sinkcol", 1)):
    PAR[_n] = _at
    _at += _w
NPAR = _at

CST = {}
_at = 0
for _n, _w in (("ident", 128), ("ones", 128), ("bdones", 128), ("II", 64), ("bd", 128), ("up", 128), ("low", 128),
               ("d16", 256), ("upi", 64), ("d16c", 128), ("o32", 128), ("o64", 64)):
    CST[_n] = (_at, _w)
    _at += _w
NCST = _at


class Steps:

    def __init__(self, known=None):
        self.known = known
        self.at, self.per_round = {}, {}


class Count:

    def __init__(self, steps, own):
        self.steps, self.own = steps, own
        self.scopes = [["", 1, {}, None]]
        self.last = None

    @contextmanager
    def rounds(self, name, n, i):
        self.scopes.append([name, n, {}, i])
        yield
        _, _, counts, _ = self.scopes.pop()
        for sem, k in counts.items():
            self.scopes[-1][2][sem] = self.scopes[-1][2].get(sem, 0) + n * k
            self.steps.per_round[sem, name] = k

    def load(self, sem, name=None):
        self.scopes[-1][2][sem] = self.scopes[-1][2].get(sem, 0) + 1
        place = (sem, tuple((s[0], s[1], s[2].get(sem, 0)) for s in self.scopes))
        if name is not None:
            assert name not in self.steps.at, name
            self.steps.at[name] = place
        if sem == self.own:
            self.last = place
        return 16

    def step(self, name=None):
        self.load(self.own, name)
        return 1

    def also(self, name):
        self.steps.at[name] = self.last

    def value(self, place, back):
        if self.steps.known is None:
            return 1
        sem, path = place
        known = self.steps.known[1]
        inc, start = (1, CREDIT) if sem in ENGINES else (16, 0)
        here = {s[0]: s[3] for s in self.scopes[1:]}
        v = inc * sum(off for _, _, off in path) + start
        inner = None
        for name, n, _ in path[1:]:
            k = known[sem, name]
            if name in here:
                v = v + here[name] * (inc * k)
                inner = k
            else:
                v = v + (n - 1) * inc * k
        if back:
            v = v - back * inc * inner
        return v

    def at(self, name, back=0):
        return self.value(self.steps.known[0][name] if self.steps.known else None, back)

    def mine(self):
        return self.value(self.last, 0)


def bcast(v, axis, n):
    v = v.unsqueeze(axis)
    shape = list(v.shape)
    shape[axis] = n
    return v.to_broadcast(shape)


class Space:

    def __init__(self, nc, tag, *free):
        self.nc, self.tag, self.free = nc, tag, [list(f) for f in free]

    def __call__(self, name, n, dt=F32):
        n8 = -(-n // 8) * 8
        for f in self.free:
            if f[1] - f[0] >= n8:
                at = f[0]
                f[0] += n8
                return self.nc.alloc_sbuf_tensor_at(self.tag + name, [128, n], dt, offset=BASE + 4 * at)
        raise ValueError(f"no room for {name}: {n} of {self.free}")


BASE = 16512
END = 229344
HH, HL, PJ = 0, KT * T, 2 * KT * T
EX = PJ + NIN * T
TOTAL = (END - BASE) // 4
RING = TOTAL - 9 * U
FIXED = RING - NCST - 160


def program(nc, d, steps):
    with ExitStack() as ctx:
        fence = ctx.enter_context(nc.sbuf_tensor("fence", [128, (nc.sbuf_bytes_remaining - 64) // 4], F32))
        del fence
        at = lambda name, n, off, dt=F32: nc.alloc_sbuf_tensor_at(name, [128, n], dt, offset=BASE + 4 * off)
        hh = at("act_high", KT * T, HH, F32R)[:, :].rearrange("p (k t) -> p k t", k=KT)
        hl = at("act_low", KT * T, HL, F32R)[:, :].rearrange("p (k t) -> p k t", k=KT)
        proj = at("proj", NIN * T, PJ)[:, :].rearrange("p (k t) -> p k t", k=NIN)
        x = at("resid", KT * T, PJ)[:, :].rearrange("p (k t) -> p k t", k=KT)
        cst = at("consts", NCST, FIXED)
        par = at("params", NPAR, FIXED + NCST)
        dpar = at("derived", 24, FIXED + NCST + 72)
        raw = [at(f"w_raw{s}", U, RING + s * U) for s in range(3)]
        wh = [at(f"w_high{s}", U, RING + (3 + s) * U, F32R) for s in range(3)]
        wl = [at(f"w_low{s}", U, RING + (6 + s) * U, F32R) for s in range(3)]
        bank = [ctx.enter_context(nc.psum_tensor(f"bank{i}", [128, 512], F32)) for i in range(8)]

        c_ = lambda n: cst[:, CST[n][0]:CST[n][0] + CST[n][1]]
        ident, ones, bdones, II = c_("ident"), c_("ones"), c_("bdones"), c_("II")
        pc = lambda n, i=0: par[:, PAR[n] + i:PAR[n] + i + 1]
        negkk, omka, fng = dpar[:, 0:4], dpar[:, 4:8], dpar[:, 8:16]
        eps_rms, eps_lnx = dpar[:, 16:17], dpar[:, 17:18]

        sp = Space(nc, "n_", (PJ + KT * T, EX))
        sq = sp("squares", KT * CW)[:, :].rearrange("p (k t) -> p k t", k=KT)
        hn = sp("normed", KT * CW)[:, :].rearrange("p (k t) -> p k t", k=KT)
        std, rstd = sp("std", CW), sp("rstd", CW)
        sp = Space(nc, "f_", (PJ + KT * T, EX))
        mh = sp("mid_high", 2 * T, F32R)[:, :].rearrange("p (j t) -> p j t", j=2)
        ml = sp("mid_low", 2 * T, F32R)[:, :].rearrange("p (j t) -> p j t", j=2)
        sil = sp("silu", 3 * CW)[:, :].rearrange("p (c t) -> p c t", c=3)
        midf = sp("mid", 3 * CW)[:, :].rearrange("p (c t) -> p c t", c=3)
        sp = Space(nc, "s_", (EX, FIXED))
        raw9 = sp("raw_last", 15 * 9)[:, :].rearrange("p (k t) -> p k t", k=15)
        shd = sp("shift_in", 15 * 8)[:, :].rearrange("p (k t) -> p k t", k=15)
        edge = sp("edge", 15 * 8)[:, :].rearrange("p (k t) -> p k t", k=15)
        dif = sp("diff", T)
        lo_h, lo_l = (HH, HH + 4 * T), (HL, HL + 4 * T)
        sp = Space(nc, "a_", lo_h, lo_l, (EX + 384, FIXED), (RING, TOTAL))
        cos, sin = sp("cos", T), sp("sin", T)
        amask = sp("amask", 5 * 256)
        vp = [sp(f"v_padded{e}", 2 * 192)[:, :].rearrange("p (g d) -> p g d", g=2) for e in range(2)]
        kd = sp("k_twice", 2 * (WIN + T))[:, :].rearrange("p (g t) -> p g t", g=2)
        bdq = sp("q_spread", 4 * 256)[:, :].rearrange("p (k t) -> p k t", k=4)
        sm = sp("scores", 8 * 256)[:, :].rearrange("p (h t) -> p h t", h=8)
        stat = sp("stats", 64)
        mats = sp("rope_mats", 5 * 128)
        sel = sp("select", 4 * 128)
        pT = sp("probs_t", 16 * 128)[:, :].rearrange("p (h t) -> p h t", h=16)
        vblk = sp("v_block", 128)
        rt = sp("rope_tmp", 3 * CW)[:, :].rearrange("p (c t) -> p c t", c=3)
        kro = sp("k_tail", 136)
        Kw = sp("k_window", 8 * 128)[:, :].rearrange("p (b t) -> p b t", b=8)
        Vw = sp("v_window", 8 * 128)[:, :].rearrange("p (b t) -> p b t", b=8)
        VwT = sp("v_window_t", 8 * 128)[:, :].rearrange("p (b t) -> p b t", b=8)
        qz, pTd, ov = sp("q_dec", 64), sp("probs_dec_t", 64), sp("o_dec", 64)
        smd = sp("scores_dec", 1024)[:, :].rearrange("p (b t) -> p b t", b=8)
        rotm, dup, rdup = mats[:, 0:128], mats[:, 128:384], mats[:, 384:640]
        q_tiles = (PJ + 15 * T, PJ + 21 * T)
        nkk = at("neg_kk", 4 * T, HH)[:, :].rearrange("p (k t) -> p k t", k=4)
        yar = at("y_heads", 4 * T, HH)[:, :].rearrange("p (k t) -> p k t", k=4)
        bb = at("b_heads", 4 * T, HL)[:, :].rearrange("p (k t) -> p k t", k=4)
        sp = Space(nc, "w_", q_tiles)
        lw_t = sp("log_decay", 4 * NCH * 65)
        lw = lw_t[:, :].rearrange("p (k n t) -> p k n t", k=4, n=NCH)
        lw_flat = lw_t[:, :].rearrange("p (k m) -> p k m", k=4)
        lwd = sp("log_decay_dec", 32)[:, :].rearrange("p (k t) -> p k t", k=4)
        rest = tuple(sp.free[0])
        sp = Space(nc, "e_", (RING, TOTAL))
        wda = sp("w_decay_a", 1024)[:, :].rearrange("p (w n) -> p w n", w=2)
        smask = sp("scan_mask", NCH * 65)
        ksq = sp("k_squared", T)
        nrm = sp("k_norm", T)
        at_ = sp("a_term", T)
        tile12 = (PJ + 12 * T, PJ + 13 * T)
        sp = Space(nc, "c_", (RING, TOTAL), rest, (EX + 384, FIXED), tile12)
        abd = sp("A_spread", 512)[:, :].rearrange("p (k t) -> p k t", k=4)
        bbd = sp("B_spread", 512)[:, :].rearrange("p (k t) -> p k t", k=4)
        kbd = sp("K_spread", 512)[:, :].rearrange("p (k t) -> p k t", k=4)
        vbd = sp("Vt_spread", 512)[:, :].rearrange("p (k t) -> p k t", k=4)
        arc = sp("AR", 512)[:, :].rearrange("p (k w t) -> p k w t", k=4, w=2)
        bc = sp("B", 256)[:, :].rearrange("p (k t) -> p k t", k=4)
        e1 = sp("P", 256)[:, :].rearrange("p (k t) -> p k t", k=4)
        e1s = sp("P_before", 256)[:, :].rearrange("p (k t) -> p k t", k=4)
        e2 = sp("P_inv", 256)[:, :].rearrange("p (k t) -> p k t", k=4)

        def grp(name, n, shape):
            return [sp(f"{name}{g}", n)[:, :].rearrange(*shape[:1], **shape[1]) for g in range(2)]

        sh4 = ("p (k t) -> p k t", {"k": 4})
        sh2 = ("p (k t) -> p k t", {"k": 2})
        nm = grp("N_Mak_spread", 512, sh4)
        xb = grp("X_spread", 256, sh2)
        nxc = grp("NX", 256, sh4)
        lc = grp("NX_other", 256, sh4)
        la = grp("NX_spread_a", 512, sh4)
        lb = grp("NX_spread_b", 512, sh4)
        rqa = grp("RQ_a", 256, sh4)
        rqb = grp("RQ_b", 256, sh4)
        rqs = grp("RQ_spread", 512, sh4)
        mr = grp("M_r", 256, sh4)
        vc = grp("V", 128, sh2)
        vts = grp("V_spread", 256, sh2)
        bks = grp("BK_spread", 512, sh4)
        sa0 = grp("SA0", 128, sh2)
        sac = grp("SA", 128, sh2)
        sas = grp("SA_spread", 256, sh2)
        Sc = grp("S", 128, sh2)
        Ss = grp("S_spread", 256, sh2)
        sp = Space(nc, "d_", (RING, TOTAL))
        SD = sp("states", 2048)[:, :].rearrange("p (k b i) -> p k b i", k=4, b=8)
        t1 = sp("t1", 512)[:, :].rearrange("p (b i) -> p b i", b=8)
        t2 = sp("t2", 512)[:, :].rearrange("p (b i) -> p b i", b=8)
        t3 = sp("t3", 512)[:, :].rearrange("p (b i) -> p b i", b=8)
        wdec = sp("decay", 32)[:, :].rearrange("p (k t) -> p k t", k=4)
        wg = sp("w_gate_up", 1024)[:, :].rearrange("p (w n) -> p w n", w=2)
        fb = [[sp(f"fin{e}_{n}", CW) for n in ("yc", "sq", "sd", "rs", "bo", "ot")] for e in range(2)]

        sem = lambda n: ctx.enter_context(nc.semaphore(n))
        tensor_steps, vector_steps, scalar_steps, pool_steps = (sem(n + "_steps") for n in ENGINES)
        x_in, const_in, par_in, shift_in, rope_in, window_in, lora_in, state_in, wg_in = (sem(n) for n in (
            "x_in", "const_in", "par_in", "shift_in", "rope_in", "window_in", "lora_in", "state_in", "wg_in"))
        x_back = [sem(f"x_back{k}") for k in range(KT)]
        spill, shift_out, k_out, window_out, state_out, sample_out, y_out = (sem(n) for n in (
            "spill", "shift_out", "k_out", "window_out", "state_out", "sample_out", "y_out"))
        sync_idle, tensor_idle, vector_idle, scalar_idle, pool_idle = (sem(n + "_idle") for n in ("sync", *ENGINES))
        raw_in = [sem(f"w_raw_in{s}") for s in range(3)]
        w_high = sem("w_high_ready")
        w_low = sem("w_low_ready")

        PER_SLOT = (32, 32, 31)

        def slot(k):
            return (k + 2) % 3 if k < NIN else (k - NIN) % 3

        def loads(l, k, i=0, per=0):
            base = k // 3 if k < NIN else NIN // 3 + (k - NIN) // 3
            return (l * PER_SLOT[slot(k)] + base + 1 + i * (per // 3)) * 16

        def after(k):
            return (1, k - UL) if k >= UL else (0, k)

        block = ctx.enter_context(nc.Block())
        cs = lambda c: slice(c * CW, (c + 1) * CW)

        @block.sync
        def _(eng):
            e = Count(steps, "x_in")

            def fill_dma(l, k, i=0, per=0, wait=True):
                dl, kk = after(k)
                g = (l + dl) * UL + kk + i * per
                if wait:
                    eng.wait_ge(w_low, g - 3 + 1)
                eng.dma_start(raw[slot(kk)][:, :], d["wts"][bass.ds(g, 1)].rearrange("a p n -> p (a n)")
                              ).then_inc(raw_in[slot(kk)], 16)

            eng.dma_start(x[:, :, :], d["x"].rearrange("p (k t) -> p k t", k=KT)).then_inc(x_in, e.load("x_in", "x_in"))
            eng.dma_start(cst[:, :], d["cst"]).then_inc(const_in, e.load("const_in", "const_in"))
            eng.dma_start(fng, d["fin"]).then_inc(const_in, e.load("const_in", "fin_in"))
            for k in range(3):
                fill_dma(0, k, wait=False)
            for k in range(3, 6):
                fill_dma(0, k)
            with eng.Fori(0, L) as l, e.rounds("layer", L, l):
                row = lambda n: d[n][bass.ds(l, 1)].rearrange("a p n -> p (a n)")
                eng.wait_ge(vector_steps, e.at("ff_add_last", back=1))
                eng.wait_ge(x_in, e.at("x_in"))
                eng.dma_start(par[:, :], row("par")).then_inc(par_in, e.load("par_in", "par_in"))
                eng.dma_start(d["x_keep"].rearrange("p (k t) -> p k t", k=KT), x[:, :, :]).then_inc(spill, e.load("spill", "spill"))
                eng.wait_ge(vector_steps, e.at("edge_put", back=1))
                eng.dma_start(shd, row("shift").rearrange("p (k t) -> p k t", k=15)).then_inc(shift_in, e.load("shift_in", "shift_in"))
                with eng.Fori(0, 5) as i, e.rounds("wa", 5, i):
                    for j in range(3):
                        fill_dma(l, 6 + j, i, 3)
                eng.wait_ge(tensor_steps, e.at("win_last"))
                eng.dma_start(cos[:, :], d["rope"][:, 0:T]).then_inc(rope_in, e.load("rope_in"))
                eng.dma_start(sin[:, :], d["rope"][:, T:2 * T]).then_inc(rope_in, e.load("rope_in"))
                eng.dma_start(mats[:, :], d["mats"][:, 0:640]).then_inc(rope_in, e.load("rope_in"))
                eng.dma_start(sel[:, :], d["mats"][:, 640:1152]).then_inc(rope_in, e.load("rope_in"))
                eng.dma_start(amask[:, :], d["amask"]).then_inc(rope_in, e.load("rope_in", "rope_in"))
                eng.dma_start(Kw[:, :, 0:127], row("kwin").rearrange("p (b t) -> p b t", b=8)).then_inc(window_in, e.load("window_in"))
                eng.dma_start(Vw[:, :, 0:127], row("vwin").rearrange("p (b t) -> p b t", b=8)).then_inc(window_in, e.load("window_in", "window_in"))
                eng.wait_ge(scalar_steps, e.at("raw9_last"))
                eng.dma_start(row("o_shift").rearrange("p (k t) -> p k t", k=15), raw9).then_inc(shift_out, e.load("shift_out", "shift_out"))
                eng.wait_ge(scalar_steps, e.at("k_tail1"))
                eng.dma_start(row("o_pk"), kro[:, 0:128]).then_inc(k_out, e.load("k_out"))
                eng.dma_start(row("o_pv"), proj[:, 20, NP_ - WIN:NP_]).then_inc(k_out, e.load("k_out", "k_out"))
                eng.wait_ge(scalar_steps, e.at("v_new"))
                eng.dma_start(row("o_sk").rearrange("p (b t) -> p b t", b=8), Kw).then_inc(window_out, e.load("window_out"))
                eng.dma_start(row("o_sv").rearrange("p (b t) -> p b t", b=8), Vw).then_inc(window_out, e.load("window_out", "window_out"))
                eng.wait_ge(vector_steps, e.at("att_low_dec"))
                eng.wait_ge(window_out, e.at("window_out"))
                eng.wait_ge(k_out, e.at("k_out"))
                eng.dma_start(wda, row("wda").rearrange("p (w n) -> p w n", w=2)).then_inc(lora_in, e.load("lora_in"))
                eng.dma_start(smask[:, :], d["smask"]).then_inc(lora_in, e.load("lora_in", "lora_in"))
                eng.wait_ge(vector_steps, e.at("S_new1"))
                for g in range(2):
                    eng.dma_start(row("o_ps").rearrange("p (k t) -> p k t", k=4)[:, 2 * g:2 * g + 2, :], Sc[g]).then_inc(state_out, e.load("state_out", f"state_out{g}"))
                eng.wait_ge(scalar_steps, e.at("y_chunk1"))
                eng.wait_ge(state_out, e.at("state_out1"))
                eng.dma_start(SD, row("states").rearrange("p (k b i) -> p k b i", k=4, b=8)).then_inc(state_in, e.load("state_in", "state_in"))
                eng.dma_start(wg, row("wg").rearrange("p (w n) -> p w n", w=2)).then_inc(wg_in, e.load("wg_in", "wg_in"))
                eng.wait_ge(vector_steps, e.at("dec_y"))
                eng.dma_start(row("o_ss").rearrange("p (k b i) -> p k b i", k=4, b=8), SD).then_inc(sample_out, e.load("sample_out", "sample_out"))
                eng.wait_ge(vector_steps, e.at("fin_low3_all"))
                eng.wait_ge(sample_out, e.at("sample_out"))
                eng.wait_ge(shift_out, e.at("shift_out"))
                eng.wait_ge(spill, e.at("spill"))
                for k in range(NIN, NIN + 3):
                    eng.sem_inc(sync_idle, 1)
                    fill_dma(l, k, wait=False)
                for k in range(KT):
                    eng.dma_start(x[:, k, :], d["x_keep"][:, k * T:(k + 1) * T]).then_inc(x_back[k], e.load(f"x_back{k}", f"x_back{k}"))
                for k in range(NIN + 3, NIN + KT + 6):
                    fill_dma(l, k)
                with eng.Fori(0, NFF // 2) as i, e.rounds("ff", NFF // 2, i):
                    for j in range(6):
                        fill_dma(l, NIN + KT + 6 + j, i, 6)
            with eng.Fori(0, NC3) as c, e.rounds("nf", NC3, c):
                seg = bass.ds(c * CW, CW)
                eng.wait_ge(vector_steps, e.at("y_done"))
                eng.dma_start(d["o_y"].rearrange("p (k t) -> p k t", k=KT)[:, :, seg], x[:, :, seg]).then_inc(y_out, e.load("y_out", "y_out"))
            eng.wait_ge(y_out, e.at("y_out"))
            eng.wait_ge(state_out, e.at("state_out1"))
            eng.wait_ge(sample_out, e.at("sample_out"))
            eng.wait_ge(shift_out, e.at("shift_out"))
            eng.wait_ge(k_out, e.at("k_out"))
            eng.wait_ge(window_out, e.at("window_out"))
            for s in range(3):
                eng.wait_ge(raw_in[s], (L * PER_SLOT[s] + 2) * 16)

        @block.gpsimd
        def _(eng):
            e = Count(steps, "pool")
            eng.sem_inc(pool_steps, CREDIT)

            def fill_low(l, k, i=0, per=0):
                dl, kk = after(k)
                g = (l + dl) * UL + kk + i * per
                eng.wait_ge(w_high, g + 1)
                eng.tensor_tensor(wl[slot(kk)][:, :], raw[slot(kk)][:, :], wh[slot(kk)][:, :].bitcast(F32),
                                  ALU.subtract).then_inc(w_low, 1)

            for k in range(3):
                fill_low(0, k)
            with eng.Fori(0, L) as l, e.rounds("layer", L, l):
                with eng.Fori(0, 5) as i, e.rounds("wa", 5, i):
                    for j in range(3):
                        fill_low(l, 3 + j, i, 3)
                for k in range(18, NIN):
                    fill_low(l, k)
                eng.wait_ge(tensor_steps, e.at("win_last"))
                eng.sem_inc(pool_idle, 1)
                for v in (kd[:, :, 0:WIN], vp[0], vp[1], bdq):
                    eng.memset(v, 0.0).then_inc(pool_steps, e.step())
                eng.memset(stat[:, :], 0.0).then_inc(pool_steps, e.step("att_zero"))
                eng.wait_ge(scalar_steps, e.at("att_high_dec"))
                eng.wait_ge(vector_steps, e.at("att_low_dec"))
                eng.wait_ge(k_out, e.at("k_out"))
                eng.sem_inc(pool_idle, 1)
                eng.memset(lw[:, :, :, 0], 0.0).then_inc(pool_steps, e.step("lw_zero"))
                eng.wait_ge(vector_steps, e.at("elem_last"))
                eng.sem_inc(pool_idle, 1)
                for v in (abd, bbd, vbd, Sc[0], Sc[1], Ss[0]):
                    eng.memset(v, 0.0).then_inc(pool_steps, e.step())
                eng.memset(Ss[1], 0.0).then_inc(pool_steps, e.step("chunk_zero"))
                for k in range(NIN, NIN + KT + 3):
                    fill_low(l, k)
                with eng.Fori(0, NFF // 2) as i, e.rounds("ff", NFF // 2, i):
                    for j in range(6):
                        fill_low(l, NIN + KT + 3 + j, i, 6)

        @block.scalar
        def _(eng):
            e = Count(steps, "scalar")
            eng.sem_inc(scalar_steps, CREDIT)
            a = eng.activation

            def fill_high(l, k, i=0, per=0, used=None):
                dl, kk = after(k)
                g = (l + dl) * UL + kk + i * per
                eng.wait_ge(raw_in[slot(kk)], loads(l + dl, kk, i, per))
                if used:
                    eng.wait_ge(tensor_steps, e.at(used))
                eng.copy(wh[slot(kk)][:, :], raw[slot(kk)][:, :]).then_inc(w_high, 1)

            def norm(p, last):
                with eng.Fori(0, NC3) as c, e.rounds(p, NC3, c):
                    seg = bass.ds(c * CW, CW)
                    eng.wait_ge(tensor_steps, e.at(p + "_ss", back=1))
                    for k in range(KT):
                        a(sq[:, k, :], x[:, k, seg], ACT.Square).then_inc(scalar_steps, e.step(f"{p}_sq{k}"))
                    eng.wait_ge(tensor_steps, e.at(p + "_ss"))
                    if last:
                        eng.wait_ge(vector_steps, e.at(p + "_recip", back=1))
                    a(std[:, :], bank[7][:, 0:CW], ACT.Sqrt, bias=eps_rms, scale=1.0 / DM).then_inc(scalar_steps, e.step(p + "_std"))
                    if not last:
                        for k in range(KT):
                            eng.wait_ge(vector_steps, e.at(f"{p}_n{k}"))
                            eng.copy(hh[:, k, seg], hn[:, k, :]).then_inc(scalar_steps, e.step(f"{p}_high{k}"))

            for k in range(3):
                fill_high(0, k)
            eng.wait_ge(x_in, e.at("x_in"))
            eng.wait_ge(vector_steps, e.at("eps"))
            with eng.Fori(0, L) as l, e.rounds("layer", L, l):
                eng.wait_ge(vector_steps, e.at("ff_add_last", back=1))
                eng.wait_ge(tensor_steps, e.at("ff_down_last", back=1))
                norm("n1", False)
                eng.wait_ge(spill, e.at("spill"))
                eng.wait_ge(vector_steps, e.at("n1_low7"))
                with eng.Fori(0, 5) as i, e.rounds("wa", 5, i):
                    for j in range(3):
                        for c in range(NC3):
                            eng.wait_ge(tensor_steps, e.at(f"wa_mm{j}{c}"))
                            eng.copy(proj[:, bass.ds(3 * i + j, 1), cs(c)].rearrange("p a t -> p (a t)"),
                                            bank[c][:, 0:CW]).then_inc(scalar_steps, e.step(f"wa_ev{j}{c}"))
                        eng.wait_ge(scalar_steps, e.mine())
                        eng.copy(raw9[:, bass.ds(3 * i + j, 1), :].rearrange("p a t -> p (a t)"),
                                        proj[:, bass.ds(3 * i + j, 1), NP_ - 1:T].rearrange("p a t -> p (a t)")).then_inc(scalar_steps, e.step("raw9_last" if j == 2 else f"raw9_{j}"))
                        fill_high(l, 3 + j, i, 3, f"wa_mm{j}2")
                for k in range(15, NIN):
                    for c in range(NC3):
                        eng.wait_ge(tensor_steps, e.at(f"wb_mm{k}{c}"))
                        eng.copy(proj[:, k, cs(c)], bank[c][:, 0:CW]).then_inc(scalar_steps, e.step(f"wb_ev{k}{c}"))
                    if k + 3 < NIN:
                        fill_high(l, k + 3, used=f"wb_mm{k}2")

                for g in range(2):
                    eng.wait_ge(vector_steps, e.at("kd_last"))
                    eng.copy(kro[64 * g:64 * g + 64, :], kd[64 * g:64 * g + 64, g, NP_:NP_ + 136]).then_inc(scalar_steps, e.step(f"k_tail{g}"))
                eng.wait_ge(scalar_steps, e.mine())
                eng.wait_ge(window_in, e.at("window_in"))
                eng.copy(Kw[:, :, 127], kro[:, 128:136]).then_inc(scalar_steps, e.step("k_new"))
                eng.copy(Vw[:, :, 127], proj[:, 20, NP_:T]).then_inc(scalar_steps, e.step("v_new"))
                eng.wait_ge(pool_steps, e.at("att_zero"))
                eng.wait_ge(vector_steps, e.at("rq_last"))
                with eng.Fori(0, 4) as i, e.rounds("ab", 4, i):
                    for n in range(2):
                        blk = bass.ds(i * 256 + n * 128, 128)
                        o = f"ab{n}_"
                        if n == 0:
                            eng.wait_ge(tensor_steps, e.at("ab1_score", back=1))
                            eng.wait_ge(tensor_steps, e.at("ab1_vt", back=1))
                        else:
                            eng.wait_ge(tensor_steps, e.at("ab0_score"))
                            eng.wait_ge(tensor_steps, e.at("ab0_vt"))
                        for h in range(2):
                            rows = slice(64 * h, 64 * h + 64)
                            eng.copy(bdq[rows, :, 128 * h:128 * h + 128], proj[rows, 15:19, blk]).then_inc(scalar_steps, e.step(f"{o}bdq{h}"))
                        eng.copy(vblk[:, :], proj[:, 20, blk]).then_inc(scalar_steps, e.step(o + "vblk"))
                        eng.wait_ge(tensor_steps, e.at(o + "vt"))
                        if n == 0:
                            eng.wait_ge(tensor_steps, e.at("ab1_pv", back=1))
                        else:
                            eng.wait_ge(tensor_steps, e.at("ab0_pv"))
                        eng.copy(vp[n][:, :, 64:128], bank[7][:, 0:128].rearrange("p (g t) -> p g t", g=2)).then_inc(scalar_steps, e.step(o + "vp"))
                        eng.wait_ge(vector_steps, e.at(o + "negmax"))
                        for h in range(8):
                            a(sm[:, h, :], sm[:, h, :], ACT.Exp, bias=stat[:, 16 + h:17 + h],
                                     accum_out=stat[:, 24 + h:25 + h]).then_inc(scalar_steps, e.step(f"{o}exp{h}"))
                        a(stat[:, 40:48], stat[:, 32:40], ACT.Exp).then_inc(scalar_steps, e.step(o + "sinkexp"))
                        for q in (1, 3):
                            eng.wait_ge(tensor_steps, e.at(f"{o}pt{q}"))
                            eng.copy(pT[:, 4 * q:4 * q + 4, :],
                                            bank[4 + q][:, :].rearrange("p (h t) -> p h t", h=4)).then_inc(scalar_steps, e.step(f"{o}ptc{q}"))
                        eng.wait_ge(tensor_steps, e.at(o + "pv"))
                        eng.copy(hh[:, 4:8, blk], bank[0][:, :].rearrange("p (k t) -> p k t", k=4)).then_inc(scalar_steps, e.step(o + "high"))
                eng.wait_ge(tensor_steps, e.at("d_qz"))
                eng.copy(qz[:, :], bank[1][:, 0:64]).then_inc(scalar_steps, e.step("d_qz_c"))
                eng.wait_ge(vector_steps, e.at("d_sub"))
                a(smd[0:8, :, :], smd[0:8, :, :], ACT.Exp).then_inc(scalar_steps, e.step("d_exp"))
                a(stat[0:8, 8:16], stat[0:8, 0:8], ACT.Exp, bias=par[0:8, PAR["sinkcol"]:PAR["sinkcol"] + 1],
                         scale=-1.0).then_inc(scalar_steps, e.step("d_sinkexp"))
                for q in range(2):
                    eng.wait_ge(tensor_steps, e.at(f"d_vt{q}"))
                    eng.copy(VwT[:, 4 * q:4 * q + 4, :], bank[5 + q][:, :].rearrange("p (b t) -> p b t", b=4)).then_inc(scalar_steps, e.step(f"d_vtc{q}"))
                eng.wait_ge(tensor_steps, e.at("d_pt"))
                eng.copy(pTd[:, :], bank[4][:, 0:64]).then_inc(scalar_steps, e.step("d_ptc"))
                eng.wait_ge(tensor_steps, e.at("d_pv"))
                eng.copy(ov[:, :], bank[7][:, 0:64]).then_inc(scalar_steps, e.step("d_ov"))
                eng.wait_ge(tensor_steps, e.at("d_place"))
                eng.copy(hh[:, 4:8, NP_:T], bank[0][:, 0:32].rearrange("p (k t) -> p k t", k=4)).then_inc(scalar_steps, e.step("att_high_dec"))

                eng.wait_ge(vector_steps, e.at("edge_put"))
                a(proj[0:64, 12, :], proj[0:64, 12, :], ACT.Tanh).then_inc(scalar_steps, e.step("tanh"))
                a(proj[:, 13:15, :], proj[:, 13:15, :], ACT.Sigmoid).then_inc(scalar_steps, e.step("sig_gate"))
                eng.wait_ge(pool_steps, e.at("lw_zero"))
                eng.wait_ge(vector_steps, e.at("att_low_dec"))
                eng.wait_ge(k_out, e.at("k_out"))
                for o in range(4):
                    for q in range(2):
                        eng.wait_ge(tensor_steps, e.at(f"lora{o}"))
                        a(lw[:, o, 8 * q:8 * q + 8, 1:65], bank[q][:, :].rearrange("p (n t) -> p n t", n=8),
                                 ACT.Sigmoid, bias=pc("w0", o)).then_inc(scalar_steps, e.step(f"lw{o}{q}"))
                        a(bb[:, o, 512 * q:512 * q + 512], bank[3 + q][:, :], ACT.Sigmoid, bias=pc("a0", o)).then_inc(scalar_steps, e.step(f"a{o}{q}"))
                    a(lwd[:, o, :], bank[2][:, 0:8], ACT.Sigmoid, bias=pc("w0", o)).then_inc(scalar_steps, e.step())
                    a(bb[:, o, NP_:T], bank[2][:, 8:16], ACT.Sigmoid, bias=pc("a0", o)).then_inc(scalar_steps, e.step(f"lora_ev{o}"))
                for o in range(4):
                    if o:
                        eng.wait_ge(tensor_steps, e.at(f"kk_mm{o - 1}"))
                    a(ksq[:, :], proj[:, 4 + o, :], ACT.Square, scale=pc("k_k", o)).then_inc(scalar_steps, e.step(f"ksq{o}"))
                    eng.wait_ge(tensor_steps, e.at(f"kk_mm{o}"))
                    if o:
                        eng.wait_ge(vector_steps, e.at(f"kk_recip{o - 1}"))
                    for c in range(NC3):
                        a(nrm[:, cs(c)], bank[5 + c][:, 0:CW], ACT.Sqrt).then_inc(scalar_steps, e.step(f"knorm{o}{c}"))

                eng.wait_ge(vector_steps, e.at("elem_last"))
                eng.wait_ge(pool_steps, e.at("chunk_zero"))
                with eng.Fori(0, NCH) as i, e.rounds("rc", NCH, i):
                    tok = bass.ds(i * CH, CH)
                    lwi = lambda rows, lo: lw[rows, :, bass.ds(i, 1), lo:lo + 64].rearrange("p k a t -> p k (a t)")
                    allp = slice(0, 128)
                    eng.wait_ge(vector_steps, e.at("prep_last", back=1))
                    eng.wait_ge(tensor_steps, e.at("g1_1", back=1))
                    eng.wait_ge(vector_steps, e.at("S_new1", back=1))
                    a(e1s, lwi(allp, 0), ACT.Exp, scale=-CDEC).then_inc(scalar_steps, e.step("e1s"))
                    a(e1, lwi(allp, 1), ACT.Exp, scale=-CDEC).then_inc(scalar_steps, e.step("e1"))
                    a(e2, lwi(allp, 1), ACT.Exp, scale=CDEC).then_inc(scalar_steps, e.step("e2"))
                    eng.wait_ge(tensor_steps, e.at("s1_1", back=1))
                    for h in range(2):
                        rows, cols = slice(64 * h, 64 * h + 64), slice(64 * h, 64 * h + 64)
                        eng.sem_inc(scalar_idle, 1)
                        a(abd[rows, :, cols], lwi(rows, 0), ACT.Exp, scale=-CDEC).then_inc(scalar_steps, e.step(f"e1bd{h}"))
                        a(bbd[rows, :, cols], lwi(rows, 1), ACT.Exp, scale=CDEC).then_inc(scalar_steps, e.step(f"e2bd{h}"))
                        eng.copy(vbd[rows, :, cols], proj[rows, 8:12, tok]).then_inc(scalar_steps, e.step(f"vbd{h}"))
                    for g in range(2):
                        eng.wait_ge(tensor_steps, e.at(f"g1_{g}"))
                        eng.copy(vc[g], bank[4 * g + 2][:, 0:128].rearrange("p (k t) -> p k t", k=2)).then_inc(scalar_steps, e.step(f"vc{g}"))
                        eng.copy(vts[g], bank[4 * g + 2][:, 128:384].rearrange("p (k t) -> p k t", k=2)).then_inc(scalar_steps, e.step(f"vts{g}"))
                        eng.copy(bks[g], bank[4 * g + 3][:, :].rearrange("p (k t) -> p k t", k=4)).then_inc(scalar_steps, e.step(f"bks{g}"))
                    for g in range(2):
                        eng.wait_ge(tensor_steps, e.at(f"s1_{g}"))
                        eng.copy(sa0[g], bank[4 * g + 3][:, 256:384].rearrange("p (k t) -> p k t", k=2)).then_inc(scalar_steps, e.step(f"sa0_{g}"))
                    for g in range(2):
                        eng.wait_ge(tensor_steps, e.at(f"s3_{g}"))
                        eng.copy(yar[:, 2 * g:2 * g + 2, tok], bank[4 * g + 2][:, 384:512].rearrange("p (k t) -> p k t", k=2)).then_inc(scalar_steps, e.step(f"y_chunk{g}"))

                eng.wait_ge(vector_steps, e.at("S_new1"))
                eng.wait_ge(tensor_steps, e.at("s3_1"))
                eng.wait_ge(state_out, e.at("state_out1"))
                a(wdec, lwd, ACT.Exp, scale=-CDEC).then_inc(scalar_steps, e.step("wdec"))
                with eng.Fori(0, NC3) as c, e.rounds("fin", NC3, c):
                    seg = bass.ds(c * CW, CW)
                    for o in range(4):
                        yc, q2, sd, rs, bo, ot = fb[o % 2]
                        b4 = 4 * (o % 2)
                        eng.wait_ge(vector_steps, e.at(f"fin_yc{o}"))
                        if o >= 2:
                            eng.wait_ge(tensor_steps, e.at(f"fin_var{o - 2}"))
                        else:
                            eng.wait_ge(tensor_steps, e.at(f"fin_var{o + 2}", back=1))
                        a(q2[:, :], yc[:, :], ACT.Square).then_inc(scalar_steps, e.step(f"fin_sq{o}"))
                        eng.wait_ge(tensor_steps, e.at(f"fin_var{o}"))
                        a(sd[:, :], bank[b4 + 1][:, 0:CW], ACT.Sqrt, bias=eps_lnx, scale=1.0 / HD).then_inc(scalar_steps, e.step(f"fin_sd{o}"))
                        eng.wait_ge(vector_steps, e.at(f"fin_out{o}"))
                        eng.copy(hh[:, o, seg], ot[:, :]).then_inc(scalar_steps, e.step(f"fin_high{o}"))

                eng.wait_ge(vector_steps, e.at("fin_low3_all"))
                for k in range(NIN, NIN + 3):
                    fill_high(l, k)
                for k in range(NIN, NIN + KT):
                    fill_high(l, k + 3, used=f"wo_mm{k - NIN}2")
                eng.wait_ge(vector_steps, e.at("wo_add_last"))
                norm("n2", False)
                with eng.Fori(0, NFF // 2) as i, e.rounds("ff", NFF // 2, i):
                    for j in range(2):
                        for c in range(NC3):
                            eng.wait_ge(tensor_steps, e.at(f"ff_g{j}{c}"))
                            if j:
                                eng.wait_ge(vector_steps, e.at(f"ff_mid{j - 1}{c}"))
                            else:
                                eng.wait_ge(vector_steps, e.at(f"ff_mid1{c}", back=1))
                            a(sil[:, c, :], bank[c][:, 0:CW], ACT.Silu).then_inc(scalar_steps, e.step(f"ff_sil{j}{c}"))
                        fill_high(l, NIN + KT + 3 + 2 * j, i, 6, f"ff_g{j}2")
                        for c in range(NC3):
                            eng.wait_ge(vector_steps, e.at(f"ff_mid{j}{c}"))
                            if j == 0 and c == 0:
                                eng.wait_ge(tensor_steps, e.at("ff_down_last", back=1))
                            eng.copy(mh[:, j, cs(c)], midf[:, c, :]).then_inc(scalar_steps, e.step(f"ff_high{j}{c}"))
                        fill_high(l, NIN + KT + 3 + 2 * j + 1, i, 6, f"ff_u{j}2")
                    for j in (4, 5):
                        fill_high(l, NIN + KT + 3 + j, i, 6, "ff_down_last")
            eng.wait_ge(vector_steps, e.at("ff_add_last"))
            norm("nf", True)

        @block.vector
        def _(eng):
            e = Count(steps, "vector")
            eng.sem_inc(vector_steps, CREDIT)
            tt, ts, stt = eng.tensor_tensor, eng.tensor_scalar, eng.scalar_tensor_tensor
            two = lambda v: v.rearrange("p k (a t) -> p k a t", a=2)
            wide = lambda v: bcast(v, 2, 2)
            mask2 = lambda m, k: bcast(m.rearrange("p (a t) -> p a t", a=2), 1, k)

            def norm(p, gain, last=False):
                def group(seg):
                    eng.wait_ge(scalar_steps, e.at(p + "_std"))
                    if last:
                        eng.wait_ge(vector_steps, e.at(f"{p}_n{KT - 1}", back=1))
                    eng.reciprocal(rstd[:, :], std[:, :]).then_inc(vector_steps, e.step(p + "_recip"))
                    eng.wait_ge(vector_steps, e.mine())
                    for k in range(KT):
                        out = x[:, k, seg] if last else hn[:, k, :]
                        stt(out, x[:, k, seg], gain(k), rstd[:, :], ALU.mult, ALU.mult).then_inc(vector_steps, e.step(f"{p}_n{k}"))
                    if last:
                        e.also("y_done")
                    else:
                        for k in range(KT):
                            eng.wait_ge(scalar_steps, e.at(f"{p}_high{k}"))
                            tt(hl[:, k, seg], hn[:, k, :], hh[:, k, seg].bitcast(F32), ALU.subtract).then_inc(vector_steps, e.step(f"{p}_low{k}"))
                        eng.wait_ge(vector_steps, e.mine())
                eng.sem_inc(vector_idle, 1)
                with eng.Fori(0, NC3) as c, e.rounds(p, NC3, c):
                    group(bass.ds(c * CW, CW))

            eng.memset(eps_rms, EPS).then_inc(vector_steps, e.step())
            eng.memset(eps_lnx, LNX_EPS).then_inc(vector_steps, e.step("eps"))
            eng.wait_ge(x_in, e.at("x_in"))
            eng.wait_ge(const_in, e.at("fin_in"))
            eng.sem_inc(vector_idle, 1)
            with eng.Fori(0, L) as l, e.rounds("layer", L, l):
                eng.wait_ge(par_in, e.at("par_in"))
                ts(negkk, par[:, PAR["k_k"]:PAR["k_k"] + 4], -1.0, None, ALU.mult).then_inc(vector_steps, e.step())
                ts(omka, par[:, PAR["k_a"]:PAR["k_a"] + 4], -1.0, 1.0, ALU.mult, ALU.add).then_inc(vector_steps, e.step())
                norm("n1", lambda k: pc("an", k))
                with eng.Fori(0, 5) as i, e.rounds("wa", 5, i):
                    for j in range(3):
                        tile = lambda lo, hi: proj[:, bass.ds(3 * i + j, 1), lo:hi].rearrange("p a t -> p (a t)")
                        eng.wait_ge(scalar_steps, e.at("raw9_last" if j == 2 else f"raw9_{j}"))
                        if j:
                            eng.wait_ge(vector_steps, e.at(f"shifted{j - 1}"))
                        else:
                            eng.wait_ge(vector_steps, e.at("shifted2", back=1))
                        tt(dif[:, 0:NP_ - 1], tile(0, NP_ - 1), tile(1, NP_), ALU.subtract).then_inc(vector_steps, e.step())
                        eng.wait_ge(vector_steps, e.mine())
                        stt(tile(1, NP_), dif[:, 0:NP_ - 1], par[:, bass.ds(3 * i + (PAR["mu"] + j), 1)], tile(1, NP_),
                                   ALU.mult, ALU.add).then_inc(vector_steps, e.step(f"shifted{j}"))
                mu = par[:, PAR["mu"]:PAR["mu"] + 15]
                eng.wait_ge(vector_steps, e.mine())
                tt(dif[:, 0:15], proj[:, 0:15, 0], mu, ALU.mult).then_inc(vector_steps, e.step())
                eng.wait_ge(shift_in, e.at("shift_in"))
                tt(edge, shd, raw9[:, :, 1:9], ALU.subtract).then_inc(vector_steps, e.step())
                eng.wait_ge(vector_steps, e.mine())
                tt(proj[:, 0:15, 0], proj[:, 0:15, 0], dif[:, 0:15], ALU.subtract).then_inc(vector_steps, e.step())
                tt(edge, edge, bcast(mu, 2, 8), ALU.mult).then_inc(vector_steps, e.step())
                eng.wait_ge(vector_steps, e.mine())
                tt(proj[:, 0:15, NP_:T], raw9[:, :, 1:9], edge, ALU.add).then_inc(vector_steps, e.step("edge_put"))

                eng.wait_ge(rope_in, e.at("rope_in"))
                eng.sem_inc(vector_idle, 1)
                with eng.Fori(0, 4) as p, e.rounds("rq", 4, p):
                    for c in range(NC3):
                        qt = proj[:, bass.ds(15 + p, 1), cs(c)].rearrange("p a t -> p (a t)")
                        eng.wait_ge(vector_steps, e.mine())
                        eng.wait_ge(tensor_steps, e.at(f"rq_rot{c}"))
                        tt(rt[:, c, :], bank[c][:, 0:CW], sin[:, cs(c)], ALU.mult).then_inc(vector_steps, e.step())
                        tt(qt, qt, cos[:, cs(c)], ALU.mult).then_inc(vector_steps, e.step())
                        eng.wait_ge(vector_steps, e.mine())
                        tt(qt, qt, rt[:, c, :], ALU.add).then_inc(vector_steps, e.step("rq_last" if c == 2 else f"rq_add{c}"))
                for g in range(2):
                    for c in range(NC3):
                        kt = kd[:, g, WIN + c * CW:WIN + (c + 1) * CW]
                        eng.wait_ge(tensor_steps, e.at(f"rk{g}{c}"))
                        eng.wait_ge(vector_steps, e.mine())
                        tt(rt[:, c, :], bank[3 + c][:, 0:CW], sin[:, cs(c)], ALU.mult).then_inc(vector_steps, e.step())
                        tt(kt, bank[c][:, 0:CW], cos[:, cs(c)], ALU.mult).then_inc(vector_steps, e.step())
                        eng.wait_ge(vector_steps, e.mine())
                        tt(kt, kt, rt[:, c, :], ALU.add).then_inc(vector_steps, e.step("kd_last" if (g, c) == (1, 2) else f"kd{g}{c}"))
                mx, nmx, den, sk, se, rd = (stat[:, 8 * n:8 * n + 8] for n in (0, 2, 3, 4, 5, 6))
                sink = par[:, PAR["sink"]:PAR["sink"] + 8]
                eng.wait_ge(pool_steps, e.at("att_zero"))
                eng.sem_inc(vector_idle, 1)
                with eng.Fori(0, 4) as i, e.rounds("ab", 4, i):
                    for n in range(2):
                        o = f"ab{n}_"
                        blk = bass.ds(i * 256 + n * 128, 128)
                        mk = (amask[:, bass.ds(i * 256, 256)] if n == 0 else amask[:, 1024:1280])
                        for p in range(4):
                            eng.wait_ge(tensor_steps, e.at(f"{o}s{p}"))
                            eng.wait_ge(vector_steps, e.mine())
                            stt(sm[:, 2 * p:2 * p + 2, :], bank[p][:, :].rearrange("p (h t) -> p h t", h=2), SCALE,
                                       bcast(mk, 1, 2), ALU.mult, ALU.add).then_inc(vector_steps, e.step(f"{o}sc{p}"))
                        eng.wait_ge(vector_steps, e.mine())
                        eng.tensor_reduce(mx, sm, AX.X, ALU.max).then_inc(vector_steps, e.step())
                        eng.wait_ge(vector_steps, e.mine())
                        tt(mx, mx, sink, ALU.max).then_inc(vector_steps, e.step())
                        eng.wait_ge(vector_steps, e.mine())
                        tt(sk, sink, mx, ALU.subtract).then_inc(vector_steps, e.step())
                        ts(nmx, mx, -1.0, None, ALU.mult).then_inc(vector_steps, e.step(o + "negmax"))
                        eng.wait_ge(scalar_steps, e.at(o + "sinkexp"))
                        tt(den, den, se, ALU.add).then_inc(vector_steps, e.step())
                        eng.wait_ge(vector_steps, e.mine())
                        eng.reciprocal(rd, den).then_inc(vector_steps, e.step())
                        eng.wait_ge(vector_steps, e.mine())
                        for h in range(8):
                            ts(sm[:, h, :], sm[:, h, :], rd[:, h:h + 1], None, ALU.mult).then_inc(vector_steps, e.step(f"{o}p{h}"))
                        for q in (0, 2):
                            eng.wait_ge(tensor_steps, e.at(f"{o}pt{q}"))
                            eng.tensor_copy(pT[:, 4 * q:4 * q + 4, :], bank[4 + q][:, :].rearrange("p (h t) -> p h t", h=4)).then_inc(vector_steps, e.step(f"{o}ptc{q}"))
                        eng.wait_ge(scalar_steps, e.at(o + "high"))
                        tt(hl[:, 4:8, blk], bank[0][:, :].rearrange("p (k t) -> p k t", k=4), hh[:, 4:8, blk].bitcast(F32),
                                  ALU.subtract).then_inc(vector_steps, e.step(o + "low"))
                eng.wait_ge(vector_steps, e.mine())
                for q in range(2):
                    eng.wait_ge(tensor_steps, e.at(f"d_s{q}"))
                    ts(smd[0:8, 4 * q:4 * q + 4, :], bank[2 + q][0:8, :].rearrange("p (b t) -> p b t", b=4), SCALE, None, ALU.mult).then_inc(vector_steps, e.step())
                eng.wait_ge(vector_steps, e.mine())
                dm, dd, dr = stat[0:8, 0:8], stat[0:8, 48:56], stat[0:8, 56:64]
                bcol = lambda v: bcast(v, 2, 128)
                eng.tensor_reduce(dm, smd[0:8], AX.X, ALU.max).then_inc(vector_steps, e.step())
                eng.wait_ge(vector_steps, e.mine())
                ts(dm, dm, par[0:8, PAR["sinkcol"]:PAR["sinkcol"] + 1], None, ALU.max).then_inc(vector_steps, e.step())
                eng.wait_ge(vector_steps, e.mine())
                tt(smd[0:8], smd[0:8], bcol(dm), ALU.subtract).then_inc(vector_steps, e.step("d_sub"))
                eng.wait_ge(scalar_steps, e.at("d_exp"))
                eng.tensor_reduce(dd, smd[0:8], AX.X, ALU.add).then_inc(vector_steps, e.step())
                eng.wait_ge(scalar_steps, e.at("d_sinkexp"))
                eng.wait_ge(vector_steps, e.mine())
                tt(dd, dd, stat[0:8, 8:16], ALU.add).then_inc(vector_steps, e.step())
                eng.wait_ge(vector_steps, e.mine())
                eng.reciprocal(dr, dd).then_inc(vector_steps, e.step())
                eng.wait_ge(vector_steps, e.mine())
                tt(smd[0:8], smd[0:8], bcol(dr), ALU.mult).then_inc(vector_steps, e.step("d_p"))
                eng.wait_ge(scalar_steps, e.at("att_high_dec"))
                tt(hl[:, 4:8, NP_:T], bank[0][:, 0:32].rearrange("p (k t) -> p k t", k=4), hh[:, 4:8, NP_:T].bitcast(F32),
                          ALU.subtract).then_inc(vector_steps, e.step("att_low_dec"))

                for o in range(4):
                    eng.wait_ge(scalar_steps, e.at(f"lw{o}1"))
                    eng.wait_ge(lora_in, e.at("lora_in"))
                    eng.tensor_tensor_scan(lw_flat[:, o, :], smask[:, :], lw_flat[:, o, :], 0.0, ALU.mult, ALU.add).then_inc(vector_steps, e.step())
                for o in range(4):
                    kt = proj[:, 4 + o, :]
                    eng.wait_ge(scalar_steps, e.at(f"knorm{o}2"))
                    eng.wait_ge(vector_steps, e.mine())
                    ts(nrm[:, :], nrm[:, :], 1e-12, None, ALU.max).then_inc(vector_steps, e.step())
                    eng.wait_ge(vector_steps, e.mine())
                    eng.reciprocal(at_[:, :], nrm[:, :]).then_inc(vector_steps, e.step(f"kk_recip{o}"))
                    eng.wait_ge(vector_steps, e.mine())
                    stt(nkk[:, o, :], kt, negkk[:, o:o + 1], at_[:, :], ALU.mult, ALU.mult).then_inc(vector_steps, e.step())
                    eng.wait_ge(scalar_steps, e.at(f"lora_ev{o}"))
                    eng.wait_ge(vector_steps, e.mine())
                    ts(at_[:, :], bb[:, o, :], pc("k_a", o), omka[:, o:o + 1], ALU.mult, ALU.add).then_inc(vector_steps, e.step())
                    eng.wait_ge(vector_steps, e.mine())
                    tt(kt, kt, at_[:, :], ALU.mult).then_inc(vector_steps, e.step())
                    stt(bb[:, o, :], nkk[:, o, :], -1.0, bb[:, o, :], ALU.mult, ALU.mult).then_inc(vector_steps, e.step("elem_last" if o == 3 else None))

                eng.wait_ge(pool_steps, e.at("chunk_zero"))
                eng.sem_inc(vector_idle, 1)
                with eng.Fori(0, NCH) as i, e.rounds("rc", NCH, i):
                    tok = bass.ds(i * CH, CH)
                    q4 = lambda v: v.rearrange("p (k a) t -> p k a t", a=2)
                    pb = lambda b, lo, hi, k: bank[b][:, lo:hi].rearrange("p (k t) -> p k t", k=k)
                    eng.wait_ge(vector_steps, e.mine())
                    eng.wait_ge(scalar_steps, e.at("e1s"))
                    tt(arc[:, :, 0, :], nkk[:, :, tok], e1s, ALU.mult).then_inc(vector_steps, e.step())
                    eng.wait_ge(scalar_steps, e.at("e2"))
                    tt(arc[:, :, 1, :], proj[:, 0:4, tok], e1, ALU.mult).then_inc(vector_steps, e.step())
                    tt(bc, bb[:, :, tok], e2, ALU.mult).then_inc(vector_steps, e.step())
                    eng.wait_ge(scalar_steps, e.at("e2bd1"))
                    tt(two(kbd), wide(proj[:, 4:8, tok]), two(bbd), ALU.mult).then_inc(vector_steps, e.step())
                    tt(two(abd), wide(nkk[:, :, tok]), two(abd), ALU.mult).then_inc(vector_steps, e.step())
                    eng.wait_ge(vector_steps, e.mine())
                    tt(two(bbd), wide(bb[:, :, tok]), two(bbd), ALU.mult).then_inc(vector_steps, e.step("prep_last"))
                    for g in range(2):
                        B = 4 * g
                        eng.wait_ge(tensor_steps, e.at(f"g1_{g}"))
                        X = pb(B + 1, 0, 128, 2)
                        G = bank[B][:, :].rearrange("p (k t) -> p k t", k=4)
                        Gn = bank[B][:, :].rearrange("p (k w t) -> p k w t", k=2, w=2)[:, :, 0, 0:64]
                        m16 = CST["d16"][0]
                        tt(two(lb[g][:, 2:4, :]), wide(X), mask2(cst[:, m16 + 128:m16 + 256], 2), ALU.mult).then_inc(vector_steps, e.step())
                        tt(nxc[g][:, 2:4, :], X, bcast(c_("d16c")[:, 64:128], 1, 2), ALU.mult).then_inc(vector_steps, e.step())
                        tt(two(xb[g]), wide(X), mask2(c_("low"), 2), ALU.mult).then_inc(vector_steps, e.step())
                        tt(two(lb[g][:, 0:2, :]), wide(Gn), mask2(cst[:, m16:m16 + 128], 2), ALU.mult).then_inc(vector_steps, e.step())
                        tt(nxc[g][:, 0:2, :], Gn, bcast(c_("d16c")[:, 0:64], 1, 2), ALU.mult).then_inc(vector_steps, e.step(f"n16_{g}"))
                    eng.wait_ge(vector_steps, e.mine())
                    for g in range(2):
                        B = 4 * g
                        G = bank[B][:, :].rearrange("p (k t) -> p k t", k=4)
                        tt(two(nm[g]), wide(G[:, :, 0:64]), mask2(c_("up"), 4), ALU.mult).then_inc(vector_steps, e.step())
                        tt(mr[g], G[:, :, 64:128], bcast(c_("upi"), 1, 4), ALU.mult).then_inc(vector_steps, e.step(f"m_{g}"))
                        tt(rqa[g], nxc[g], bcast(II, 1, 4), ALU.add).then_inc(vector_steps, e.step(f"rq1_{g}"))

                    def spread(dst, src, k):
                        return tt(two(dst), wide(src), mask2(c_("bd"), k), ALU.mult)

                    for g in range(2):
                        B = 4 * g
                        eng.wait_ge(tensor_steps, e.at(f"l2_{g}"))
                        eng.tensor_copy(lc[g], pb(B + 1, 256, 512, 4)).then_inc(vector_steps, e.step())
                        spread(la[g], pb(B + 1, 256, 512, 4), 4).then_inc(vector_steps, e.step(f"l2e_{g}"))
                    for g in range(2):
                        B = 4 * g
                        eng.wait_ge(tensor_steps, e.at(f"l4_{g}"))
                        eng.tensor_copy(nxc[g], pb(B, 0, 256, 4)).then_inc(vector_steps, e.step())
                        spread(lb[g], pb(B, 0, 256, 4), 4).then_inc(vector_steps, e.step())
                        tt(rqb[g], pb(B, 256, 512, 4), rqa[g], ALU.add).then_inc(vector_steps, e.step(f"l4e_{g}"))
                    for g in range(2):
                        B = 4 * g
                        eng.wait_ge(tensor_steps, e.at(f"l8_{g}"))
                        spread(la[g], pb(B + 1, 0, 256, 4), 4).then_inc(vector_steps, e.step())
                        tt(rqa[g], pb(B + 1, 256, 512, 4), rqb[g], ALU.add).then_inc(vector_steps, e.step(f"l8e_{g}"))
                    for g in range(2):
                        B = 4 * g
                        eng.wait_ge(tensor_steps, e.at(f"r8_{g}"))
                        tt(rqb[g], pb(B + 2, 0, 256, 4), rqa[g], ALU.add).then_inc(vector_steps, e.step(f"r8c_{g}"))
                        eng.wait_ge(vector_steps, e.mine())
                        spread(rqs[g], rqb[g], 4).then_inc(vector_steps, e.step(f"r8e_{g}"))
                    for g in range(2):
                        B = 4 * g
                        eng.wait_ge(tensor_steps, e.at(f"m1_{g}"))
                        o32 = bcast(c_("o32").rearrange("p (w t) -> p w t", w=2), 2, 2)
                        tt(q4(lc[g]), q4(pb(B + 3, 0, 256, 4)), o32, ALU.mult).then_inc(vector_steps, e.step(f"m1e_{g}"))
                    for g in range(2):
                        B = 4 * g
                        eng.wait_ge(tensor_steps, e.at(f"m2_{g}"))
                        tt(rqa[g], pb(B, 0, 256, 4), rqb[g], ALU.add).then_inc(vector_steps, e.step(f"m2c_{g}"))
                        eng.wait_ge(vector_steps, e.mine())
                        spread(lb[g][:, 0:2, :], rqa[g][:, 2:4, :], 2).then_inc(vector_steps, e.step(f"m2e_{g}"))
                    for g in range(2):
                        B = 4 * g
                        eng.wait_ge(tensor_steps, e.at(f"m3_{g}"))
                        tt(lc[g][:, 0:2, :], pb(B + 1, 0, 128, 2), bcast(c_("o64"), 1, 2),
                                  ALU.mult).then_inc(vector_steps, e.step(f"m3e_{g}"))
                    for g in range(2):
                        B = 4 * g
                        eng.wait_ge(tensor_steps, e.at(f"m4_{g}"))
                        tt(rqb[g][:, 0:2, :], pb(B + 2, 0, 128, 2), rqa[g][:, 0:2, :], ALU.add).then_inc(vector_steps, e.step())
                        eng.wait_ge(vector_steps, e.mine())
                        spread(la[g][:, 0:2, :], rqb[g][:, 0:2, :], 2).then_inc(vector_steps, e.step(f"m4e_{g}"))
                    for g in range(2):
                        B = 4 * g
                        eng.wait_ge(tensor_steps, e.at(f"s2_{g}"))
                        eng.tensor_copy(sac[g], pb(B + 3, 384, 512, 2)).then_inc(vector_steps, e.step())
                        spread(sas[g], pb(B + 3, 384, 512, 2), 2).then_inc(vector_steps, e.step(f"sa_{g}"))
                    for g in range(2):
                        B = 4 * g
                        eng.wait_ge(tensor_steps, e.at(f"s3_{g}"))
                        tt(Sc[g], pb(B + 1, 256, 384, 2), Sc[g], ALU.add).then_inc(vector_steps, e.step())
                        eng.wait_ge(vector_steps, e.mine())
                        tt(Sc[g], Sc[g], bcast(e1[:, 2 * g:2 * g + 2, 63], 2, 64), ALU.mult).then_inc(vector_steps, e.step())
                        eng.wait_ge(vector_steps, e.mine())
                        spread(Ss[g], Sc[g], 2).then_inc(vector_steps, e.step(f"S_new{g}"))

                eng.wait_ge(state_in, e.at("state_in"))
                eng.wait_ge(scalar_steps, e.at("wdec"))
                eng.wait_ge(scalar_steps, e.at("y_chunk1"))
                eng.sem_inc(vector_idle, 1)
                with eng.Fori(0, 4) as p, e.rounds("dp", 4, p):
                    col = lambda v: bcast(v.rearrange("p a t -> p (a t)"), 2, 64)
                    tile = lambda t, q: col(t[:, bass.ds(q, 1), NP_:T])
                    S = SD[:, bass.ds(p, 1)].rearrange("p a b i -> p (a b) i")
                    iib = bcast(II, 1, 8)
                    eng.wait_ge(vector_steps, e.mine())
                    tt(t1, S, tile(nkk, p), ALU.mult).then_inc(vector_steps, e.step("dp_sa_in"))
                    tt(t2, iib, tile(proj, p + 8), ALU.mult).then_inc(vector_steps, e.step("dp_v_in"))
                    tt(S, S, col(wdec[:, bass.ds(p, 1), :]), ALU.mult).then_inc(vector_steps, e.step())
                    eng.wait_ge(tensor_steps, e.at("dp_sa"))
                    tt(t3, bank[0][:, :].rearrange("p (b i) -> p b i", b=8), tile(bb, p), ALU.mult).then_inc(vector_steps, e.step())
                    eng.wait_ge(tensor_steps, e.at("dp_v"))
                    tt(t1, bank[1][:, :].rearrange("p (b i) -> p b i", b=8), tile(proj, p + 4), ALU.mult).then_inc(vector_steps, e.step())
                    eng.wait_ge(vector_steps, e.mine())
                    tt(S, S, t3, ALU.add).then_inc(vector_steps, e.step())
                    eng.wait_ge(vector_steps, e.mine())
                    tt(S, S, t1, ALU.add).then_inc(vector_steps, e.step())
                    eng.wait_ge(vector_steps, e.mine())
                    tt(t2, S, tile(proj, p), ALU.mult).then_inc(vector_steps, e.step("dp_r_in"))
                    eng.wait_ge(tensor_steps, e.at("dp_y"))
                    tt(t3, bank[2][:, :].rearrange("p (b i) -> p b i", b=8), iib, ALU.mult).then_inc(vector_steps, e.step())
                    eng.wait_ge(vector_steps, e.mine())
                    eng.sem_inc(vector_idle, 1)
                    eng.tensor_reduce(yar[:, bass.ds(p, 1), NP_:T].rearrange("p a t -> p (a t)"), t3, AX.X, ALU.add).then_inc(vector_steps, e.step("dec_y"))

                eng.wait_ge(vector_steps, e.mine())
                eng.sem_inc(vector_idle, 1)
                with eng.Fori(0, NC3) as c, e.rounds("fin", NC3, c):
                    seg = bass.ds(c * CW, CW)
                    for o in range(4):
                        yc, q2, sd, rs, bo, ot = fb[o % 2]
                        b4 = 4 * (o % 2)
                        eng.wait_ge(vector_steps, e.mine())
                        eng.wait_ge(wg_in, e.at("wg_in"))
                        stt(bo[:, :], proj[:, o, seg], pc("r_k", o), proj[:, 4 + o, seg], ALU.mult, ALU.mult).then_inc(vector_steps, e.step(f"fin_rk{o}"))
                        eng.wait_ge(tensor_steps, e.at(f"fin_mean{o}"))
                        stt(yc[:, :], bank[b4][:, 0:CW], -1.0 / HD, yar[:, o, seg], ALU.mult, ALU.add).then_inc(vector_steps, e.step(f"fin_yc{o}"))
                        eng.wait_ge(scalar_steps, e.at(f"fin_sd{o}"))
                        eng.reciprocal(rs[:, :], sd[:, :]).then_inc(vector_steps, e.step())
                        eng.wait_ge(tensor_steps, e.at(f"fin_bonus{o}"))
                        tt(bo[:, :], bank[b4 + 2][:, 0:CW], proj[:, 8 + o, seg], ALU.mult).then_inc(vector_steps, e.step())
                        eng.wait_ge(vector_steps, e.mine())
                        stt(yc[:, :], yc[:, :], pc("lg", o), rs[:, :], ALU.mult, ALU.mult).then_inc(vector_steps, e.step())
                        eng.wait_ge(vector_steps, e.mine())
                        stt(yc[:, :], yc[:, :], pc("lb", o), bo[:, :], ALU.add, ALU.add).then_inc(vector_steps, e.step())
                        eng.wait_ge(tensor_steps, e.at(f"fin_gate{o}"))
                        eng.wait_ge(vector_steps, e.mine())
                        tt(ot[:, :], yc[:, :], bank[b4 + 3][:, 0:CW], ALU.mult).then_inc(vector_steps, e.step(f"fin_out{o}"))
                        eng.wait_ge(scalar_steps, e.at(f"fin_high{o}"))
                        tt(hl[:, o, seg], ot[:, :], hh[:, o, seg].bitcast(F32), ALU.subtract).then_inc(vector_steps, e.step("fin_low3_all" if o == 3 else f"fin_low{o}"))

                for k in range(KT):
                    eng.wait_ge(x_back[k], e.at(f"x_back{k}"))
                    for c in range(NC3):
                        eng.wait_ge(tensor_steps, e.at(f"wo_mm{k}{c}"))
                        tt(x[:, k, cs(c)], bank[c][:, 0:CW], x[:, k, cs(c)], ALU.add).then_inc(vector_steps, e.step(f"wo_add{k}{c}"))
                e.also("wo_add_last")
                eng.wait_ge(vector_steps, e.mine())
                eng.sem_inc(vector_idle, 1)
                norm("n2", lambda k: pc("fn", k))
                with eng.Fori(0, NFF // 2) as i, e.rounds("ff", NFF // 2, i):
                    for j in range(2):
                        for c in range(NC3):
                            eng.wait_ge(tensor_steps, e.at(f"ff_u{j}{c}"))
                            eng.wait_ge(scalar_steps, e.at(f"ff_sil{j}{c}"))
                            eng.wait_ge(vector_steps, e.mine())
                            tt(midf[:, c, :], sil[:, c, :], bank[3 + c][:, 0:CW], ALU.mult).then_inc(vector_steps, e.step(f"ff_mid{j}{c}"))
                        for c in range(NC3):
                            eng.wait_ge(scalar_steps, e.at(f"ff_high{j}{c}"))
                            tt(ml[:, j, cs(c)], midf[:, c, :], mh[:, j, cs(c)].bitcast(F32), ALU.subtract).then_inc(vector_steps, e.step(f"ff_low{j}{c}"))
                    for c in range(NC3):
                        for k in range(KT):
                            eng.wait_ge(tensor_steps, e.at(f"ff_d{c * KT + k}"))
                            tt(x[:, k, cs(c)], bank[6 + k % 2][:, 0:CW], x[:, k, cs(c)], ALU.add).then_inc(vector_steps, e.step(f"ff_add{c * KT + k}"))
                    e.also("ff_add_last")
                    eng.wait_ge(vector_steps, e.mine())

            eng.sem_inc(vector_idle, 1)
            norm("nf", lambda k: fng[:, k:k + 1], last=True)

        @block.tensor
        def _(eng):
            e = Count(steps, "tensor")
            eng.sem_inc(tensor_steps, CREDIT)
            mm = eng.matmul

            def norm(p):
                with eng.Fori(0, NC3) as c, e.rounds(p, NC3, c):
                    eng.wait_ge(scalar_steps, e.at(p + "_std", back=1))
                    for k in range(KT):
                        eng.wait_ge(scalar_steps, e.at(f"{p}_sq{k}"))
                        last = mm(bank[7][:, 0:CW], ones, sq[:, k, :], start=(k == 0), stop=(k == KT - 1))
                    last.then_inc(tensor_steps, e.step(p + "_ss"))

            def unit(k, i=0, per=0):
                eng.wait_ge(w_low, layer[0] * UL + k + i * per + 1)
                return slot(k)

            def column(out, s, wcols, act_h, act_l, start, stop):
                mm(out, wh[s][:, wcols], act_h, start=start, stop=False)
                mm(out, wh[s][:, wcols], act_l, start=False, stop=False)
                return mm(out, wl[s][:, wcols], act_h, start=False, stop=stop)

            def tile(s, out, c):
                for k in range(KT):
                    last = column(out, s, slice(k * 128, k * 128 + 128), hh[:, k, cs(c)], hl[:, k, cs(c)], k == 0, k == KT - 1)
                return last

            layer = [0]
            eng.wait_ge(const_in, e.at("fin_in"))
            eng.sem_inc(tensor_idle, 1)
            with eng.Fori(0, L) as l, e.rounds("layer", L, l):
                layer[0] = l
                norm("n1")
                eng.wait_ge(vector_steps, e.at("n1_low7"))
                eng.sem_inc(tensor_idle, 1)
                with eng.Fori(0, 5) as i, e.rounds("wa", 5, i):
                    for j in range(3):
                        s = unit(j, i, 3)
                        for c in range(NC3):
                            if j:
                                eng.wait_ge(scalar_steps, e.at(f"wa_ev{j - 1}{c}"))
                            else:
                                eng.wait_ge(scalar_steps, e.at(f"wa_ev2{c}", back=1))
                            tile(s, bank[c][:, 0:CW], c).then_inc(tensor_steps, e.step(f"wa_mm{j}{c}"))
                for k in range(15, NIN):
                    s = unit(k)
                    for c in range(NC3):
                        eng.wait_ge(scalar_steps, e.at(f"wb_ev{k - 1}{c}" if k > 15 else f"wa_ev2{c}"))
                        tile(s, bank[c][:, 0:CW], c).then_inc(tensor_steps, e.step(f"wb_mm{k}{c}"))
                e.also("win_last")

                eng.wait_ge(rope_in, e.at("rope_in"))
                eng.wait_ge(scalar_steps, e.at(f"wb_ev{NIN - 1}2"))
                eng.sem_inc(tensor_idle, 1)
                with eng.Fori(0, 4) as p, e.rounds("rq", 4, p):
                    for c in range(NC3):
                        eng.wait_ge(vector_steps, e.at("rq_last" if c == 2 else f"rq_add{c}", back=1))
                        mm(bank[c][:, 0:CW], rotm, proj[:, bass.ds(15 + p, 1), cs(c)].rearrange("p a t -> p (a t)"),
                                  start=True, stop=True).then_inc(tensor_steps, e.step(f"rq_rot{c}"))
                eng.wait_ge(vector_steps, e.at("rq_last"))
                for g in range(2):
                    for c in range(NC3):
                        if g:
                            eng.wait_ge(vector_steps, e.at(f"kd0{c}"))
                        mm(bank[c][:, 0:CW], dup[:, 128 * g:128 * g + 128], proj[:, 19, cs(c)], start=True, stop=True)
                        mm(bank[3 + c][:, 0:CW], rdup[:, 128 * g:128 * g + 128], proj[:, 19, cs(c)], start=True, stop=True).then_inc(tensor_steps, e.step(f"rk{g}{c}"))
                eng.wait_ge(vector_steps, e.at("kd_last"))
                eng.wait_ge(pool_steps, e.at("att_zero"))
                eng.sem_inc(tensor_idle, 1)
                with eng.Fori(0, 4) as i, e.rounds("ab", 4, i):
                    for n in range(2):
                        o = f"ab{n}_"
                        eng.wait_ge(scalar_steps, e.at(o + "bdq1"))
                        if n == 0:
                            eng.wait_ge(vector_steps, e.at("ab1_low", back=1))
                        else:
                            eng.wait_ge(vector_steps, e.at("ab0_low"))
                        for p in range(4):
                            for h in range(2):
                                last = mm(bank[p][:, 256 * h:256 * h + 256], bdq[:, p, 128 * h:128 * h + 128],
                                          kd[:, p // 2, bass.ds(i * 256 + n * 128, 256)], start=True, stop=True)
                            last.then_inc(tensor_steps, e.step(f"{o}s{p}"))
                        e.also(o + "score")
                        eng.wait_ge(scalar_steps, e.at(o + "vblk"))
                        if n == 0:
                            eng.wait_ge(scalar_steps, e.at("ab1_ptc3", back=1))
                        else:
                            eng.wait_ge(scalar_steps, e.at("ab0_ptc3"))
                        mm(bank[7][:, 0:128], vblk[:, :], ident, is_transpose=True, start=True, stop=True).then_inc(tensor_steps, e.step(o + "vt"))
                        eng.wait_ge(scalar_steps, e.at(o + "vp"))
                        for q in range(4):
                            for w in range(4):
                                h, kt = (4 * q + w) // 2, w % 2
                                eng.wait_ge(vector_steps, e.at(f"{o}p{h}"))
                                last = mm(bank[4 + q][:, 128 * w:128 * w + 128], sm[:, h, 128 * kt:128 * kt + 128], ident,
                                          is_transpose=True, start=True, stop=True)
                            last.then_inc(tensor_steps, e.step(f"{o}pt{q}"))
                        for p in range(4):
                            eng.wait_ge(scalar_steps if p % 2 else vector_steps, e.at(f"{o}ptc{p}"))
                            for h in range(2):
                                for kt in range(2):
                                    v = vp[(n + 1 + kt) % 2][:, p // 2, (64 - 64 * h):(192 - 64 * h)]
                                    last = mm(bank[0][:, 128 * p:128 * p + 128], v, pT[:, 2 * (2 * p + h) + kt, :],
                                              start=(h, kt) == (0, 0), stop=(h, kt) == (1, 1))
                        last.then_inc(tensor_steps, e.step(o + "pv"))
                eng.wait_ge(vector_steps, e.at("ab1_low"))
                for h in range(8):
                    s2 = 2 * (h % 2) + h // 4
                    last = mm(bank[1][:, 8 * h:8 * h + 8], sel[:, 128 * s2:128 * s2 + 128], proj[:, 15 + h // 2, NP_:T],
                              start=True, stop=True)
                last.then_inc(tensor_steps, e.step("d_qz"))
                eng.wait_ge(scalar_steps, e.at("d_qz_c"))
                eng.wait_ge(scalar_steps, e.at("v_new"))
                eng.wait_ge(scalar_steps, e.at("k_new"))
                for q in range(2):
                    for b in range(4):
                        last = mm(bank[2 + q][0:8, 128 * b:128 * b + 128],
                                  qz[:, :].rearrange("p (h b) -> p h b", h=8)[:, :, 4 * q + b], Kw[:, 4 * q + b, :], start=True, stop=True)
                    last.then_inc(tensor_steps, e.step(f"d_s{q}"))
                for q in range(2):
                    for b in range(4):
                        last = mm(bank[5 + q][:, 128 * b:128 * b + 128], Vw[:, 4 * q + b, :], ident, is_transpose=True, start=True, stop=True)
                    last.then_inc(tensor_steps, e.step(f"d_vt{q}"))
                eng.wait_ge(vector_steps, e.at("d_p"))
                eng.sem_inc(tensor_idle, 1)
                for b in range(8):
                    last = mm(bank[4][:, 8 * b:8 * b + 8], smd[0:8, b, :], ident[0:8, 0:8], is_transpose=True, start=True, stop=True)
                last.then_inc(tensor_steps, e.step("d_pt"))
                eng.wait_ge(scalar_steps, e.at("d_ptc"))
                for b in range(8):
                    last = mm(bank[7][:, 8 * b:8 * b + 8], VwT[:, b, :], pTd[:, 8 * b:8 * b + 8], start=True, stop=True)
                last.then_inc(tensor_steps, e.step("d_pv"))
                eng.wait_ge(scalar_steps, e.at("d_ov"))
                ovh = ov[:, :].rearrange("p (b h) -> p b h", b=8)
                for p in range(4):
                    for h in range(2):
                        s2 = 2 * (p // 2) + h
                        last = mm(bank[0][:, 8 * p:8 * p + 8], sel[:, 128 * s2:128 * s2 + 128], ovh[:, :, 2 * p + h],
                                  start=(h == 0), stop=(h == 1))
                last.then_inc(tensor_steps, e.step("d_place"))

                eng.wait_ge(scalar_steps, e.at("tanh"))
                eng.wait_ge(lora_in, e.at("lora_in"))
                eng.wait_ge(vector_steps, e.at("att_low_dec"))
                for o in range(4):
                    if o:
                        eng.wait_ge(scalar_steps, e.at(f"lora_ev{o - 1}"))
                    oc = slice(128 * o, 128 * o + 128)
                    for w in range(2):
                        for q in range(2):
                            mm(bank[3 * w + q][:, :], wda[:, w, oc], proj[:, 12, 512 * q:512 * q + 512], start=True, stop=True)
                        last = mm(bank[2][:, 8 * w:8 * w + 8], wda[:, w, oc], proj[:, 12, NP_:T], start=True, stop=True)
                    last.then_inc(tensor_steps, e.step(f"lora{o}"))
                for o in range(4):
                    eng.wait_ge(scalar_steps, e.at(f"ksq{o}"))
                    if o:
                        eng.wait_ge(scalar_steps, e.at(f"knorm{o - 1}2"))
                    for c in range(NC3):
                        last = mm(bank[5 + c][:, 0:CW], bdones, ksq[:, cs(c)], start=True, stop=True)
                    last.then_inc(tensor_steps, e.step(f"kk_mm{o}"))

                eng.wait_ge(vector_steps, e.at("elem_last"))
                eng.wait_ge(pool_steps, e.at("chunk_zero"))
                eng.sem_inc(tensor_idle, 1)
                with eng.Fori(0, NCH) as i, e.rounds("rc", NCH, i):
                    eng.wait_ge(vector_steps, e.at("prep_last"))
                    eng.wait_ge(scalar_steps, e.at("vbd1"))
                    for g in range(2):
                        B = 4 * g
                        eng.wait_ge(vector_steps, e.at(f"S_new{g}", back=1))
                        eng.wait_ge(scalar_steps, e.at(f"y_chunk{g}", back=1))
                        for q in range(2):
                            p = 2 * g + q
                            ar = arc[:, p].rearrange("p w t -> p (w t)")
                            mm(bank[B][:, 256 * q:256 * q + 128], bbd[:, p, :], ar, start=True, stop=True)
                            mm(bank[B][:, 256 * q + 128:256 * q + 256], kbd[:, p, :], ar, start=True, stop=True)
                            mm(bank[B + 1][:, 64 * q:64 * q + 64], abd[:, p, :], bc[:, p, :], start=True, stop=True)
                            mm(bank[B + 2][:, 64 * q:64 * q + 64], vbd[:, p, :], II, start=True, stop=True)
                            mm(bank[B + 2][:, 128 + 128 * q:256 + 128 * q], vbd[:, p, :], ident, is_transpose=True, start=True, stop=True)
                            mm(bank[B + 3][:, 256 * q:256 * q + 128], bbd[:, p, :], ident, is_transpose=True, start=True, stop=True)
                            last = mm(bank[B + 3][:, 256 * q + 128:256 * q + 256], kbd[:, p, :], ident, is_transpose=True,
                                      start=True, stop=True)
                        last.then_inc(tensor_steps, e.step(f"g1_{g}"))

                    def square(b, at0, spread, cur, g):
                        for q in range(2):
                            mm(bank[b][:, at0 + 64 * q:at0 + 64 * q + 64], spread[:, 2 + q, :], cur[:, q, :], start=True, stop=True)
                        for q in range(2):
                            last = mm(bank[b][:, at0 + 128 + 64 * q:at0 + 192 + 64 * q], spread[:, q, :], cur[:, 2 + q, :],
                                      start=True, stop=True)
                        return last

                    for g in range(2):
                        eng.wait_ge(vector_steps, e.at(f"n16_{g}"))
                        square(4 * g + 1, 256, lb[g], nxc[g], g).then_inc(tensor_steps, e.step(f"l2_{g}"))
                    for g in range(2):
                        eng.wait_ge(vector_steps, e.at(f"l2e_{g}"))
                        eng.wait_ge(vector_steps, e.at(f"m_{g}"))
                        eng.wait_ge(vector_steps, e.at(f"rq1_{g}"))
                        square(4 * g, 0, la[g], lc[g], g)
                        square(4 * g, 256, la[g], rqa[g], g).then_inc(tensor_steps, e.step(f"l4_{g}"))
                    for g in range(2):
                        eng.wait_ge(vector_steps, e.at(f"l4e_{g}"))
                        square(4 * g + 1, 0, lb[g], nxc[g], g)
                        square(4 * g + 1, 256, lb[g], rqb[g], g).then_inc(tensor_steps, e.step(f"l8_{g}"))
                    for g in range(2):
                        eng.wait_ge(vector_steps, e.at(f"l8e_{g}"))
                        eng.wait_ge(scalar_steps, e.at(f"vts{g}"))
                        square(4 * g + 2, 0, la[g], rqa[g], g).then_inc(tensor_steps, e.step(f"r8_{g}"))
                    for g in range(2):
                        eng.wait_ge(vector_steps, e.at(f"r8c_{g}"))
                        eng.wait_ge(scalar_steps, e.at(f"bks{g}"))
                        for q in range(2):
                            mm(bank[4 * g + 3][:, 64 * q:64 * q + 64], xb[g][:, q, :], rqb[g][:, q, :], start=True, stop=True)
                        for q in range(2):
                            last = mm(bank[4 * g + 3][:, 128 + 64 * q:192 + 64 * q], nm[g][:, 2 * q, :], rqb[g][:, 2 + q, :],
                                      start=True, stop=True)
                        last.then_inc(tensor_steps, e.step(f"m1_{g}"))
                    for g in range(2):
                        eng.wait_ge(vector_steps, e.at(f"m1e_{g}"))
                        eng.wait_ge(vector_steps, e.at(f"r8e_{g}"))
                        square(4 * g, 0, rqs[g], lc[g], g).then_inc(tensor_steps, e.step(f"m2_{g}"))
                    for g in range(2):
                        eng.wait_ge(vector_steps, e.at(f"m2c_{g}"))
                        for q in range(2):
                            last = mm(bank[4 * g + 1][:, 64 * q:64 * q + 64], xb[g][:, q, :], rqa[g][:, q, :], start=True, stop=True)
                        last.then_inc(tensor_steps, e.step(f"m3_{g}"))
                    for g in range(2):
                        eng.wait_ge(scalar_steps, e.at(f"vc{g}"))
                        for q in range(2):
                            out = bank[4 * g + 3][:, 256 + 64 * q:320 + 64 * q]
                            mm(out, abd[:, 2 * g + q, :], Sc[g][:, q, :], start=True, stop=False)
                            last = mm(out, nm[g][:, 2 * q + 1, :], vc[g][:, q, :], start=False, stop=True)
                        last.then_inc(tensor_steps, e.step(f"s1_{g}"))
                    for g in range(2):
                        eng.wait_ge(vector_steps, e.at(f"m3e_{g}"))
                        eng.wait_ge(vector_steps, e.at(f"m2e_{g}"))
                        for q in range(2):
                            last = mm(bank[4 * g + 2][:, 64 * q:64 * q + 64], lb[g][:, q, :], lc[g][:, q, :], start=True, stop=True)
                        last.then_inc(tensor_steps, e.step(f"m4_{g}"))
                    for g in range(2):
                        eng.wait_ge(vector_steps, e.at(f"m4e_{g}"))
                        eng.wait_ge(scalar_steps, e.at(f"sa0_{g}"))
                        for q in range(2):
                            last = mm(bank[4 * g + 3][:, 384 + 64 * q:448 + 64 * q], la[g][:, q, :], sa0[g][:, q, :], start=True, stop=True)
                        last.then_inc(tensor_steps, e.step(f"s2_{g}"))
                    for g in range(2):
                        eng.wait_ge(vector_steps, e.at(f"sa_{g}"))
                        for q in range(2):
                            out = bank[4 * g + 1][:, 256 + 64 * q:320 + 64 * q]
                            mm(out, bks[g][:, 2 * q, :], sac[g][:, q, :], start=True, stop=False)
                            mm(out, bks[g][:, 2 * q + 1, :], vc[g][:, q, :], start=False, stop=True)
                        for q in range(2):
                            out = bank[4 * g + 2][:, 384 + 64 * q:448 + 64 * q]
                            mm(out, Ss[g][:, q, :], arc[:, 2 * g + q, 1, :], start=True, stop=False)
                            mm(out, sas[g][:, q, :], mr[g][:, 2 * q, :], start=False, stop=False)
                            last = mm(out, vts[g][:, q, :], mr[g][:, 2 * q + 1, :], start=False, stop=True)
                        last.then_inc(tensor_steps, e.step(f"s3_{g}"))

                eng.wait_ge(vector_steps, e.at("S_new1"))
                eng.wait_ge(scalar_steps, e.at("y_chunk1"))
                flat = lambda v: v.rearrange("p b i -> p (b i)")
                eng.sem_inc(tensor_idle, 1)
                with eng.Fori(0, 4) as p, e.rounds("dp", 4, p):
                    eng.wait_ge(vector_steps, e.at("dp_sa_in"))
                    mm(bank[0][:, :], bdones, flat(t1), start=True, stop=True).then_inc(tensor_steps, e.step("dp_sa"))
                    eng.wait_ge(vector_steps, e.at("dp_v_in"))
                    mm(bank[1][:, :], bdones, flat(t2), start=True, stop=True).then_inc(tensor_steps, e.step("dp_v"))
                    eng.wait_ge(vector_steps, e.at("dp_r_in"))
                    mm(bank[2][:, :], bdones, flat(t2), start=True, stop=True).then_inc(tensor_steps, e.step("dp_y"))
                eng.wait_ge(vector_steps, e.at("dec_y"))
                eng.wait_ge(wg_in, e.at("wg_in"))
                eng.wait_ge(scalar_steps, e.at("sig_gate"))
                eng.sem_inc(tensor_idle, 1)
                with eng.Fori(0, NC3) as c, e.rounds("fin", NC3, c):
                    seg = bass.ds(c * CW, CW)
                    for o in range(4):
                        b4 = 4 * (o % 2)
                        yc, q2, sd, rs, bo, ot = fb[o % 2]
                        if o >= 2:
                            eng.wait_ge(vector_steps, e.at(f"fin_out{o - 2}"))
                        else:
                            eng.wait_ge(vector_steps, e.at(f"fin_out{o + 2}", back=1))
                        mm(bank[b4][:, 0:CW], bdones, yar[:, o, seg], start=True, stop=True).then_inc(tensor_steps, e.step(f"fin_mean{o}"))
                        oc = slice(128 * o, 128 * o + 128)
                        mm(bank[b4 + 3][:, 0:CW], wg[:, 0, oc], proj[:, 13, seg], start=True, stop=False)
                        mm(bank[b4 + 3][:, 0:CW], wg[:, 1, oc], proj[:, 14, seg], start=False, stop=True).then_inc(tensor_steps, e.step(f"fin_gate{o}"))
                        eng.wait_ge(vector_steps, e.at(f"fin_rk{o}"))
                        mm(bank[b4 + 2][:, 0:CW], bdones, bo[:, :], start=True, stop=True).then_inc(tensor_steps, e.step(f"fin_bonus{o}"))
                        eng.wait_ge(scalar_steps, e.at(f"fin_sq{o}"))
                        mm(bank[b4 + 1][:, 0:CW], bdones, q2[:, :], start=True, stop=True).then_inc(tensor_steps, e.step(f"fin_var{o}"))

                eng.wait_ge(vector_steps, e.at("fin_low3_all"))
                eng.wait_ge(scalar_steps, e.at("fin_high3"))
                for k in range(KT):
                    s = unit(NIN + k)
                    for c in range(NC3):
                        if k:
                            eng.wait_ge(vector_steps, e.at(f"wo_add{k - 1}{c}"))
                        tile(s, bank[c][:, 0:CW], c).then_inc(tensor_steps, e.step(f"wo_mm{k}{c}"))
                norm("n2")
                eng.wait_ge(vector_steps, e.at("n2_low7"))
                eng.sem_inc(tensor_idle, 1)
                with eng.Fori(0, NFF // 2) as i, e.rounds("ff", NFF // 2, i):
                    for j in range(2):
                        for w, n in ((0, "g"), (1, "u")):
                            s = unit(NIN + KT + 2 * j + w, i, 6)
                            for c in range(NC3):
                                prev = "sil" if n == "g" else "mid"
                                if j:
                                    eng.wait_ge(scalar_steps if n == "g" else vector_steps, e.at(f"ff_{prev}0{c}"))
                                else:
                                    eng.wait_ge(scalar_steps if n == "g" else vector_steps, e.at(f"ff_{prev}1{c}", back=1))
                                tile(s, bank[3 * w + c][:, 0:CW], c).then_inc(tensor_steps, e.step(f"ff_{n}{j}{c}"))
                    s = [unit(NIN + KT + 4 + j, i, 6) for j in range(2)]
                    for c in range(NC3):
                        eng.wait_ge(vector_steps, e.at(f"ff_low1{c}"))
                        for k in range(KT):
                            n = c * KT + k
                            eng.wait_ge(vector_steps, e.at(f"ff_add{(n - 2) % (3 * KT)}", back=int(n < 2)))
                            for j in range(2):
                                last = column(bank[6 + k % 2][:, 0:CW], s[j], slice(128 * k, 128 * k + 128),
                                              mh[:, j, cs(c)], ml[:, j, cs(c)], j == 0, j == 1)
                            last.then_inc(tensor_steps, e.step(f"ff_d{n}"))
                    e.also("ff_down_last")
            norm("nf")


def _consts():
    C = np.zeros((128, NCST), np.float32)
    put = lambda n, v: C.__setitem__((slice(None), slice(CST[n][0], CST[n][0] + CST[n][1])), v)
    r = np.arange(128)
    s, h = r % 64, r // 64
    col = np.arange(64)
    put("ident", np.eye(128))
    put("ones", 1.0)
    put("bdones", (h[:, None] == h[None, :]))
    put("II", (s[:, None] == col[None, :]))
    half = np.repeat(np.arange(2), 64)
    sameh = h[:, None] == half[None, :]
    c2 = np.tile(col, 2)
    put("bd", sameh)
    up, low = s[:, None] < c2[None, :], s[:, None] > c2[None, :]
    b16 = (s[:, None] // 16) == (c2[None, :] // 16)
    put("up", sameh & up)
    put("low", sameh & low)
    put("d16", np.concatenate([sameh & up & b16, sameh & low & b16], 1))
    u, w = s[:, None] < col[None, :], s[:, None] > col[None, :]
    k16 = (s[:, None] // 16) == (col[None, :] // 16)
    k32 = (s[:, None] // 32) == (col[None, :] // 32)
    put("upi", s[:, None] <= col[None, :])
    put("d16c", np.concatenate([u & k16, w & k16], 1))
    put("o32", np.concatenate([u & k32 & ~k16, w & k32 & ~k16], 1))
    put("o64", u & ~k32)
    inv = (10000.0 ** (-np.arange(32) / 32)).astype(np.float32)
    pos = np.concatenate([np.arange(NP_), np.full(NS, 1024)]).astype(np.float32)
    ang = (pos[None, :] * inv[r % 32][:, None]).astype(np.float32)
    rope = np.concatenate([np.cos(ang), np.sin(ang)], 1).astype(np.float32)
    rot = np.zeros((128, 128), np.float32)
    for m in range(128):
        dd = m % 64
        if dd < 32:
            rot[m + 32, m] = -1.0
        else:
            rot[m - 32, m] = 1.0
    S = np.zeros((2, 2, 128, 128), np.float32)
    for a in range(2):
        for b in range(2):
            S[a, b, a * 64 + col, b * 64 + col] = 1.0
    dup = [S[g, 0] + S[g, 1] for g in range(2)]
    mats = np.concatenate([rot, dup[0], dup[1], rot @ dup[0], rot @ dup[1], S[0, 0], S[0, 1], S[1, 0], S[1, 1]], 1)
    j = np.arange(256)
    diff = r[:, None] - j[None, :] + 128
    ok = (diff >= 0) & (diff < WIN)
    m = np.where(ok, 0.0, -1e30).astype(np.float32)
    m0 = np.where(ok & (j[None, :] >= 128), 0.0, -1e30).astype(np.float32)
    amask = np.concatenate([m0, m, m, m, m], 1)
    smask = np.ones((128, NCH, 65), np.float32)
    smask[:, :, 0] = 0.0
    return {"cst": C, "rope": rope, "mats": mats.astype(np.float32), "amask": amask, "smask": smask.reshape(128, -1)}


def _chan(v, tiles):
    v = np.asarray(v)
    return np.moveaxis(v.reshape(v.shape[0], tiles, 128, *v.shape[2:]), 1, 2)


def _pad(v, n, axis):
    out = list(v.shape)
    out[axis] = n - v.shape[axis]
    return np.concatenate([v, np.zeros(out, v.dtype)], axis)


def _lay_out(i):
    A = {k: np.asarray(v) for k, v in i.items()}
    z = dict(_consts())
    xall = np.concatenate([A["x_prompt"][0], A["x_sample"][:, 0]], 0)
    z["x"] = np.ascontiguousarray(xall.T.reshape(KT, 128, T).transpose(1, 0, 2)).reshape(128, KT * T)
    w = A["w_in"]
    w = np.concatenate([_pad(w[:, :, :1824], 1920, 2), w[:, :, 1824:]], 2)

    def tiles(w):
        ll, ki, no = w.shape
        return w.reshape(ll, ki // 128, 128, no // 128, 128).transpose(0, 3, 2, 1, 4).reshape(ll, no // 128, 128, ki)

    g, u = tiles(A["w_gate"]), tiles(A["w_up"])
    dn = A["w_down"].reshape(L, NFF, 128, DM)
    ff = np.stack([g[:, 0::2], u[:, 0::2], g[:, 1::2], u[:, 1::2], dn[:, 0::2], dn[:, 1::2]], 2).reshape(L, 3 * NFF, 128, U)
    wts = np.concatenate([tiles(w), tiles(A["w_out"]), ff], 1).reshape(L * UL, 128, U)
    z["wts"] = _pad(wts, L * UL + 6, 0)
    par = np.zeros((L, 128, NPAR), np.float32)

    def put(n, v, tiles):
        par[:, :, PAR[n]:PAR[n] + tiles] = _chan(v, tiles)

    put("an", A["attn_norm"], 8)
    put("fn", A["ffn_norm"], 8)
    put("mu", _pad(A["mu"], 1920, 1), 15)
    for n, k in (("w0", "w0"), ("a0", "a0"), ("k_k", "k_k"), ("k_a", "k_a"), ("lg", "lnx_g"), ("lb", "lnx_b")):
        put(n, A[k], 4)
    put("r_k", A["r_k"].reshape(L, 512), 4)
    par[:, :, PAR["sink"]:PAR["sink"] + 8] = A["sinks"][:, None, :]
    par[:, 0:8, PAR["sinkcol"]] = A["sinks"]
    z["par"] = par
    z["fin"] = _chan(A["final_norm"][None], 8)[0]
    z["shift"] = _chan(_pad(A["state_shift"].transpose(0, 2, 1), 1920, 1), 15).reshape(L, 128, 15 * 8)
    win = lambda c: c[:, :, 1:].transpose(0, 3, 4, 1, 2).reshape(L, 128, 8 * 127)
    z["kwin"], z["vwin"] = win(A["cache_k_win"]), win(A["cache_v_win"])
    zero = np.zeros((L, 64, 512), np.float32)
    z["wda"] = np.stack([np.concatenate([A["w_decay_up"], zero], 1), np.concatenate([zero, A["w_a_up"]], 1)], 2).reshape(L, 128, 1024)
    z["wg"] = _pad(A["w_g_up"], 256, 1).reshape(L, 2, 128, 512).transpose(0, 2, 1, 3).reshape(L, 128, 1024)
    st = A["state_rwkv"].reshape(L, 8, 4, 2, 64, 64).transpose(0, 3, 5, 2, 1, 4)
    z["states"] = st.reshape(L, 128, 2048)
    return {k: np.ascontiguousarray(v) for k, v in z.items()}


_OUT = {"o_y": (128, KT * T), "o_ps": (L, 128, 256), "o_shift": (L, 128, 135), "o_pk": (L, 128, 128), "o_pv": (L, 128, 128),
        "o_ss": (L, 128, 2048), "o_sk": (L, 128, 1024), "o_sv": (L, 128, 1024)}


def _declare(nc, arrays):
    d = {n: nc.dram_tensor(n, a.shape, F32, kind="ExternalInput").ap() for n, a in arrays.items()}
    for n, s in _OUT.items():
        d[n] = nc.dram_tensor(n, s, F32, kind="ExternalOutput").ap()
    d["x_keep"] = nc.dram_tensor("x_keep", (128, KT * T), F32).ap()
    return d


def kernel(**inputs):
    import concourse.bacc as bacc
    from concourse.bass_utils import run_bass_kernel_spmd

    arrays = _lay_out(inputs)
    known = None
    for _ in range(2):
        nc = bacc.Bacc("TRN2", target_bir_lowering=False, num_devices=1)
        steps = Steps(known)
        program(nc, _declare(nc, arrays), steps)
        known = (steps.at, steps.per_round)
    return _results(run_bass_kernel_spmd(nc, [arrays], core_ids=[0]).results[0])


def _results(r):
    y = np.asarray(r["o_y"]).reshape(128, KT, T).transpose(2, 1, 0).reshape(T, DM)
    ps = np.asarray(r["o_ps"]).reshape(L, 2, 64, 4, 64).transpose(0, 3, 1, 4, 2).reshape(L, 1, 8, 64, 64)
    ss = np.asarray(r["o_ss"]).reshape(L, 2, 64, 4, 8, 64).transpose(0, 4, 3, 1, 5, 2).reshape(L, 8, 8, 64, 64)
    sh = np.asarray(r["o_shift"]).reshape(L, 128, 15, 9).transpose(0, 3, 2, 1).reshape(L, 9, 1920)[:, :, :1824]
    pk = np.asarray(r["o_pk"]).transpose(0, 2, 1).reshape(L, 1, 128, 2, 64)
    pv = np.asarray(r["o_pv"]).transpose(0, 2, 1).reshape(L, 1, 128, 2, 64)
    sk = np.asarray(r["o_sk"]).reshape(L, 128, 8, 128).transpose(0, 2, 3, 1).reshape(L, 8, 128, 2, 64)
    sv = np.asarray(r["o_sv"]).reshape(L, 128, 8, 128).transpose(0, 2, 3, 1).reshape(L, 8, 128, 2, 64)
    c = np.ascontiguousarray
    return (c(y[None, :NP_]), c(y[NP_:, None]), c(ps), c(sh[:, 0:1]), c(pk), c(pv), c(ss), c(sh[:, 1:9]), c(sk), c(sv))
```

```python
from contextlib import ExitStack, contextmanager

import numpy as np

import concourse.bass as bass
from concourse import mybir

F32 = mybir.dt.float32
F32R = mybir.dt.float32r
ALU = mybir.AluOpType
ACT = mybir.ActivationFunctionType
AX = mybir.AxisListType

L = 2
DM = 1024
KT = DM // 128
NP_, NS = 1024, 8
T = NP_ + NS
NC3, CW = 3, T // 3
HD = 64
NPAIR = 4
CH = 64
NCH = NP_ // CH
FF = 2816
NFF = FF // 128
NIN = 21
UL = NIN + KT + 3 * NFF
U = 1024
WIN = 128
CDEC = float(np.exp(-0.5))
SCALE = HD ** -0.5
EPS, LNX_EPS = 1e-5, 64e-5
ENGINES = ("tensor", "vector", "scalar", "pool")
CREDIT = 6000

PAR = {}
_at = 0
for _n, _w in (("an", 8), ("fn", 8), ("mu", 15), ("w0", 4), ("a0", 4), ("k_k", 4), ("k_a", 4), ("r_k", 4),
               ("lg", 4), ("lb", 4), ("sink", 8), ("sinkcol", 1)):
    PAR[_n] = _at
    _at += _w
NPAR = _at

CST = {}
_at = 0
for _n, _w in (("ident", 128), ("ones", 128), ("bdones", 128), ("II", 64), ("bd", 128), ("up", 128), ("low", 128),
               ("d16", 256), ("upi", 64), ("d16c", 128), ("o32", 128), ("o64", 64)):
    CST[_n] = (_at, _w)
    _at += _w
NCST = _at


CHUNK_CREDIT = 200


class Steps:

    def __init__(self, known=None):
        self.known = known
        self.at, self.per_round = {}, {}


class Count:

    def __init__(self, steps, own):
        self.steps, self.own = steps, own
        self.scopes = [["", 1, {}, None]]
        self.last = None

    @contextmanager
    def rounds(self, name, n, i):
        self.scopes.append([name, n, {}, i])
        yield
        _, _, counts, _ = self.scopes.pop()
        for sem, k in counts.items():
            self.scopes[-1][2][sem] = self.scopes[-1][2].get(sem, 0) + n * k
            self.steps.per_round[sem, name] = k

    def load(self, sem, name=None):
        self.scopes[-1][2][sem] = self.scopes[-1][2].get(sem, 0) + 1
        place = (sem, tuple((s[0], s[1], s[2].get(sem, 0)) for s in self.scopes))
        if name is not None:
            assert name not in self.steps.at, name
            self.steps.at[name] = place
        if sem == self.own:
            self.last = place
        return 16

    def step(self, name=None):
        self.load(self.own, name)
        return 1

    def also(self, name):
        self.steps.at[name] = self.last

    def value(self, place, back):
        if self.steps.known is None:
            return 1
        sem, path = place
        known = self.steps.known[1]
        inc, start = (1, CREDIT) if sem in ENGINES else (16, 0)
        here = {s[0]: s[3] for s in self.scopes[1:]}
        v = inc * sum(off for _, _, off in path) + start
        inner = None
        for name, n, _ in path[1:]:
            k = known[sem, name]
            if name in here:
                v = v + here[name] * (inc * k)
                inner = k
            else:
                v = v + (n - 1) * inc * k
        if back:
            v = v - back * inc * inner
        return v

    def at(self, name, back=0):
        return self.value(self.steps.known[0][name] if self.steps.known else None, back)

    def mine(self):
        return self.value(self.last, 0)


class Chunk:

    def __init__(self, steps, own):
        self.steps, self.own, self.n = steps, own, 0

    def begin(self):
        self.n = 0

    def step(self, name=None):
        self.n += 1
        self.steps.at[self.own, self.n] = None
        self.steps.per_round[self.own] = max(self.n, self.steps.per_round.get(self.own, 0))
        if name is not None:
            self.steps.at[self.own, name] = self.n
        return 1


def chunk_at(steps, own, name, l, c):
    if steps.known is None:
        return 1
    at, per_round = steps.known
    off = name if isinstance(name, int) else at[own, name]
    return l * (NCH * per_round[own]) + (c * per_round[own] + (CHUNK_CREDIT + off))


def bcast(v, axis, n):
    v = v.unsqueeze(axis)
    shape = list(v.shape)
    shape[axis] = n
    return v.to_broadcast(shape)


class Space:

    def __init__(self, nc, tag, *free):
        self.nc, self.tag, self.free = nc, tag, [list(f) for f in free]

    def __call__(self, name, n, dt=F32):
        n8 = -(-n // 8) * 8
        for f in self.free:
            if f[1] - f[0] >= n8:
                at = f[0]
                f[0] += n8
                return self.nc.alloc_sbuf_tensor_at(self.tag + name, [128, n], dt, offset=BASE + 4 * at)
        raise ValueError(f"no room for {name}: {n} of {self.free}")


BASE = 16512
END = 229344
HH, HL, PJ = 0, KT * T, 2 * KT * T
EX = PJ + NIN * T
TOTAL = (END - BASE) // 4
RING = TOTAL - 9 * U
FIXED = RING - NCST - 160


def program(nc, d, steps):
    with ExitStack() as ctx:
        fence = ctx.enter_context(nc.sbuf_tensor("fence", [128, (nc.sbuf_bytes_remaining - 64) // 4], F32))
        del fence
        at = lambda name, n, off, dt=F32: nc.alloc_sbuf_tensor_at(name, [128, n], dt, offset=BASE + 4 * off)
        hh = at("act_high", KT * T, HH, F32R)[:, :].rearrange("p (k t) -> p k t", k=KT)
        hl = at("act_low", KT * T, HL, F32R)[:, :].rearrange("p (k t) -> p k t", k=KT)
        proj = at("proj", NIN * T, PJ)[:, :].rearrange("p (k t) -> p k t", k=NIN)
        x = at("resid", KT * T, PJ)[:, :].rearrange("p (k t) -> p k t", k=KT)
        cst = at("consts", NCST, FIXED)
        par = at("params", NPAR, FIXED + NCST)
        dpar = at("derived", 24, FIXED + NCST + 72)
        raw = [at(f"w_raw{s}", U, RING + s * U) for s in range(3)]
        wh = [at(f"w_high{s}", U, RING + (3 + s) * U, F32R) for s in range(3)]
        wl = [at(f"w_low{s}", U, RING + (6 + s) * U, F32R) for s in range(3)]
        bank = [ctx.enter_context(nc.psum_tensor(f"bank{i}", [128, 512], F32)) for i in range(8)]

        c_ = lambda n: cst[:, CST[n][0]:CST[n][0] + CST[n][1]]
        ident, ones, bdones, II = c_("ident"), c_("ones"), c_("bdones"), c_("II")
        pc = lambda n, i=0: par[:, PAR[n] + i:PAR[n] + i + 1]
        negkk, omka, fng = dpar[:, 0:4], dpar[:, 4:8], dpar[:, 8:16]
        eps_rms, eps_lnx = dpar[:, 16:17], dpar[:, 17:18]

        sp = Space(nc, "n_", (PJ + KT * T, EX))
        sq = sp("squares", KT * CW)[:, :].rearrange("p (k t) -> p k t", k=KT)
        hn = sp("normed", KT * CW)[:, :].rearrange("p (k t) -> p k t", k=KT)
        std, rstd = sp("std", CW), sp("rstd", CW)
        sp = Space(nc, "f_", (PJ + KT * T, EX))
        mh = sp("mid_high", 2 * T, F32R)[:, :].rearrange("p (j t) -> p j t", j=2)
        ml = sp("mid_low", 2 * T, F32R)[:, :].rearrange("p (j t) -> p j t", j=2)
        sil = sp("silu", 3 * CW)[:, :].rearrange("p (c t) -> p c t", c=3)
        midf = sp("mid", 3 * CW)[:, :].rearrange("p (c t) -> p c t", c=3)
        sp = Space(nc, "s_", (EX, FIXED))
        raw9 = sp("raw_last", 15 * 9)[:, :].rearrange("p (k t) -> p k t", k=15)
        shd = sp("shift_in", 15 * 8)[:, :].rearrange("p (k t) -> p k t", k=15)
        edge = sp("edge", 15 * 8)[:, :].rearrange("p (k t) -> p k t", k=15)
        dif = sp("diff", T)
        lo_h, lo_l = (HH, HH + 4 * T), (HL, HL + 4 * T)
        sp = Space(nc, "a_", lo_h, lo_l, (EX + 384, FIXED), (RING, TOTAL))
        cos, sin = sp("cos", T), sp("sin", T)
        amask = sp("amask", 5 * 256)
        vp = [sp(f"v_padded{e}", 2 * 192)[:, :].rearrange("p (g d) -> p g d", g=2) for e in range(2)]
        kd = sp("k_twice", 2 * (WIN + T))[:, :].rearrange("p (g t) -> p g t", g=2)
        bdq = sp("q_spread", 4 * 256)[:, :].rearrange("p (k t) -> p k t", k=4)
        sm = sp("scores", 8 * 256)[:, :].rearrange("p (h t) -> p h t", h=8)
        stat = sp("stats", 64)
        mats = sp("rope_mats", 5 * 128)
        sel = sp("select", 4 * 128)
        pT = sp("probs_t", 16 * 128)[:, :].rearrange("p (h t) -> p h t", h=16)
        vblk = sp("v_block", 128)
        rt = sp("rope_tmp", 3 * CW)[:, :].rearrange("p (c t) -> p c t", c=3)
        kro = sp("k_tail", 136)
        Kw = sp("k_window", 8 * 128)[:, :].rearrange("p (b t) -> p b t", b=8)
        Vw = sp("v_window", 8 * 128)[:, :].rearrange("p (b t) -> p b t", b=8)
        VwT = sp("v_window_t", 8 * 128)[:, :].rearrange("p (b t) -> p b t", b=8)
        qz, pTd, ov = sp("q_dec", 64), sp("probs_dec_t", 64), sp("o_dec", 64)
        smd = sp("scores_dec", 1024)[:, :].rearrange("p (b t) -> p b t", b=8)
        rotm, dup, rdup = mats[:, 0:128], mats[:, 128:384], mats[:, 384:640]
        q_tiles = (PJ + 15 * T, PJ + 21 * T)
        nkk = at("neg_kk", 4 * T, HH)[:, :].rearrange("p (k t) -> p k t", k=4)
        yar = at("y_heads", 4 * T, HH)[:, :].rearrange("p (k t) -> p k t", k=4)
        bb = at("b_heads", 4 * T, HL)[:, :].rearrange("p (k t) -> p k t", k=4)
        sp = Space(nc, "w_", q_tiles)
        lw_t = sp("log_decay", 4 * NCH * 65)
        lw = lw_t[:, :].rearrange("p (k n t) -> p k n t", k=4, n=NCH)
        lw_flat = lw_t[:, :].rearrange("p (k m) -> p k m", k=4)
        lwd = sp("log_decay_dec", 32)[:, :].rearrange("p (k t) -> p k t", k=4)
        rest = tuple(sp.free[0])
        sp = Space(nc, "e_", (RING, TOTAL))
        wda = sp("w_decay_a", 1024)[:, :].rearrange("p (w n) -> p w n", w=2)
        smask = sp("scan_mask", NCH * 65)
        ksq = sp("k_squared", T)
        nrm = sp("k_norm", T)
        at_ = sp("a_term", T)
        tile12 = (PJ + 12 * T, PJ + 13 * T)
        sp = Space(nc, "c_", (RING, TOTAL), rest, (EX + 384, FIXED), tile12, (HL + 4 * T, HL + 8 * T))
        k4 = lambda name: sp(name, 512)[:, :].rearrange("p (k t) -> p k t", k=4)
        k2 = lambda name: sp(name, 256)[:, :].rearrange("p (k t) -> p k t", k=2)
        k2c = lambda name: sp(name, 128)[:, :].rearrange("p (k t) -> p k t", k=2)
        par_grp = lambda f, name: [[f(f"{name}{q}{g}") for g in range(2)] for q in range(2)]
        grp = lambda f, name: [f(f"{name}{g}") for g in range(2)]
        abd = [k4(f"A_spread{q}") for q in range(2)]
        arc = [sp(f"AR{q}", 512)[:, :].rearrange("p (k w t) -> p k w t", k=4, w=2) for q in range(2)]
        pend = [sp(f"P_end{q}", 4) for q in range(2)]
        bbd, kbd, vbd = k4("B_spread"), k4("K_spread"), k4("Vt_spread")
        bc = sp("B", 256)[:, :].rearrange("p (k t) -> p k t", k=4)
        nm = par_grp(k4, "N_Mak_spread")
        mr = par_grp(lambda n: sp(n, 256)[:, :].rearrange("p (k t) -> p k t", k=4), "M_r")
        vc, vts = par_grp(k2c, "V"), par_grp(k2, "V_spread")
        bks = par_grp(k4, "BK_spread")
        Tt = par_grp(k2, "Tt_spread")
        xb = grp(k2, "X_spread")
        nr = [grp(lambda n: sp(n, 512)[:, :].rearrange("p (m r t) -> p m r t", m=4, r=2), f"NR_{w}") for w in range(2)]
        la, lb = grp(k4, "NX_spread_a"), grp(k4, "NX_spread_b")
        sa0, sac, sas = grp(k2c, "SA0"), grp(k2c, "SA"), grp(k2, "SA_spread")
        Sc, Ss = grp(k2c, "S"), grp(k2, "S_spread")
        att_low = at("att_low_back", 4 * T, HL + 4 * T)[:, :].rearrange("p (k t) -> p k t", k=4)
        sp = Space(nc, "d_", (RING, TOTAL))
        SD = sp("states", 2048)[:, :].rearrange("p (k b i) -> p k b i", k=4, b=8)
        t1 = sp("t1", 512)[:, :].rearrange("p (b i) -> p b i", b=8)
        t2 = sp("t2", 512)[:, :].rearrange("p (b i) -> p b i", b=8)
        t3 = sp("t3", 512)[:, :].rearrange("p (b i) -> p b i", b=8)
        wdec = sp("decay", 32)[:, :].rearrange("p (k t) -> p k t", k=4)
        wg = sp("w_gate_up", 1024)[:, :].rearrange("p (w n) -> p w n", w=2)
        fb = [[sp(f"fin{e}_{n}", CW) for n in ("yc", "sq", "sd", "rs", "bo", "ot")] for e in range(2)]

        sem = lambda n: ctx.enter_context(nc.semaphore(n))
        tensor_steps, vector_steps, scalar_steps, pool_steps = (sem(n + "_steps") for n in ENGINES)
        x_in, const_in, par_in, shift_in, rope_in, window_in, lora_in, state_in, wg_in = (sem(n) for n in (
            "x_in", "const_in", "par_in", "shift_in", "rope_in", "window_in", "lora_in", "state_in", "wg_in"))
        x_back = [sem(f"x_back{k}") for k in range(KT)]
        spill, shift_out, k_out, window_out, state_out, sample_out, y_out = (sem(n) for n in (
            "spill", "shift_out", "k_out", "window_out", "state_out", "sample_out", "y_out"))
        pool_prep, scalar_prep, vector_prep = (sem(n) for n in ("pool_prep", "scalar_prep", "vector_prep"))
        tensor_inv, scalar_inv, vector_inv = (sem(n) for n in ("tensor_inv", "scalar_inv", "vector_inv"))
        tensor_state, scalar_state, vector_state = (sem(n) for n in ("tensor_state", "scalar_state", "vector_state"))
        att_out, att_back = sem("att_out"), sem("att_back")
        sync_idle, tensor_idle, vector_idle, scalar_idle, pool_idle = (sem(n + "_idle") for n in ("sync", *ENGINES))
        raw_in = [sem(f"w_raw_in{s}") for s in range(3)]
        w_high = sem("w_high_ready")
        w_low = sem("w_low_ready")

        PER_SLOT = (32, 32, 31)

        def slot(k):
            return (k + 2) % 3 if k < NIN else (k - NIN) % 3

        def loads(l, k, i=0, per=0):
            base = k // 3 if k < NIN else NIN // 3 + (k - NIN) // 3
            return (l * PER_SLOT[slot(k)] + base + 1 + i * (per // 3)) * 16

        def after(k):
            return (1, k - UL) if k >= UL else (0, k)

        def at_chunk(own, name, l, c):
            return chunk_at(steps, own, name, l, c)

        block = ctx.enter_context(nc.Block())
        cs = lambda c: slice(c * CW, (c + 1) * CW)

        @block.sync
        def _(eng):
            e = Count(steps, "x_in")

            def fill_dma(l, k, i=0, per=0, wait=True):
                dl, kk = after(k)
                g = (l + dl) * UL + kk + i * per
                if wait:
                    eng.wait_ge(w_low, g - 3 + 1)
                eng.dma_start(raw[slot(kk)][:, :], d["wts"][bass.ds(g, 1)].rearrange("a p n -> p (a n)")
                              ).then_inc(raw_in[slot(kk)], 16)

            eng.dma_start(x[:, :, :], d["x"].rearrange("p (k t) -> p k t", k=KT)).then_inc(x_in, e.load("x_in", "x_in"))
            eng.dma_start(cst[:, :], d["cst"]).then_inc(const_in, e.load("const_in", "const_in"))
            eng.dma_start(fng, d["fin"]).then_inc(const_in, e.load("const_in", "fin_in"))
            for k in range(3):
                fill_dma(0, k, wait=False)
            for k in range(3, 6):
                fill_dma(0, k)
            with eng.Fori(0, L) as l, e.rounds("layer", L, l):
                row = lambda n: d[n][bass.ds(l, 1)].rearrange("a p n -> p (a n)")
                eng.wait_ge(vector_steps, e.at("ff_add_last", back=1))
                eng.wait_ge(x_in, e.at("x_in"))
                eng.dma_start(par[:, :], row("par")).then_inc(par_in, e.load("par_in", "par_in"))
                eng.dma_start(d["x_keep"].rearrange("p (k t) -> p k t", k=KT), x[:, :, :]).then_inc(spill, e.load("spill", "spill"))
                eng.wait_ge(vector_steps, e.at("edge_put", back=1))
                eng.dma_start(shd, row("shift").rearrange("p (k t) -> p k t", k=15)).then_inc(shift_in, e.load("shift_in", "shift_in"))
                with eng.Fori(0, 5) as i, e.rounds("wa", 5, i):
                    for j in range(3):
                        fill_dma(l, 6 + j, i, 3)
                eng.wait_ge(tensor_steps, e.at("win_last"))
                eng.dma_start(cos[:, :], d["rope"][:, 0:T]).then_inc(rope_in, e.load("rope_in"))
                eng.dma_start(sin[:, :], d["rope"][:, T:2 * T]).then_inc(rope_in, e.load("rope_in"))
                eng.dma_start(mats[:, :], d["mats"][:, 0:640]).then_inc(rope_in, e.load("rope_in"))
                eng.dma_start(sel[:, :], d["mats"][:, 640:1152]).then_inc(rope_in, e.load("rope_in"))
                eng.dma_start(amask[:, :], d["amask"]).then_inc(rope_in, e.load("rope_in", "rope_in"))
                eng.dma_start(Kw[:, :, 0:127], row("kwin").rearrange("p (b t) -> p b t", b=8)).then_inc(window_in, e.load("window_in"))
                eng.dma_start(Vw[:, :, 0:127], row("vwin").rearrange("p (b t) -> p b t", b=8)).then_inc(window_in, e.load("window_in", "window_in"))
                eng.wait_ge(scalar_steps, e.at("raw9_last"))
                eng.dma_start(row("o_shift").rearrange("p (k t) -> p k t", k=15), raw9).then_inc(shift_out, e.load("shift_out", "shift_out"))
                eng.wait_ge(scalar_steps, e.at("k_tail1"))
                eng.dma_start(row("o_pk"), kro[:, 0:128]).then_inc(k_out, e.load("k_out"))
                eng.dma_start(row("o_pv"), proj[:, 20, NP_ - WIN:NP_]).then_inc(k_out, e.load("k_out", "k_out"))
                eng.wait_ge(scalar_steps, e.at("v_new"))
                eng.dma_start(row("o_sk").rearrange("p (b t) -> p b t", b=8), Kw).then_inc(window_out, e.load("window_out"))
                eng.dma_start(row("o_sv").rearrange("p (b t) -> p b t", b=8), Vw).then_inc(window_out, e.load("window_out", "window_out"))
                eng.wait_ge(vector_steps, e.at("att_low_dec"))
                eng.dma_start(d["att_keep"].rearrange("p (k t) -> p k t", k=4), hl[:, 4:8, :].bitcast(F32)).then_inc(att_out, e.load("att_out", "att_out"))
                eng.wait_ge(window_out, e.at("window_out"))
                eng.wait_ge(k_out, e.at("k_out"))
                eng.dma_start(wda, row("wda").rearrange("p (w n) -> p w n", w=2)).then_inc(lora_in, e.load("lora_in"))
                eng.dma_start(smask[:, :], d["smask"]).then_inc(lora_in, e.load("lora_in", "lora_in"))
                eng.wait_ge(vector_state, at_chunk("vector_state", "S_new1", l, NCH - 1))
                eng.sem_inc(sync_idle, 1)
                for g in range(2):
                    eng.dma_start(row("o_ps").rearrange("p (k t) -> p k t", k=4)[:, 2 * g:2 * g + 2, :], Sc[g]).then_inc(state_out, e.load("state_out", f"state_out{g}"))
                eng.wait_ge(scalar_state, at_chunk("scalar_state", "y1", l, NCH - 1))
                eng.wait_ge(att_out, e.at("att_out"))
                eng.dma_start(att_low, d["att_keep"].rearrange("p (k t) -> p k t", k=4)).then_inc(att_back, e.load("att_back", "att_back"))
                eng.wait_ge(state_out, e.at("state_out1"))
                eng.dma_start(SD, row("states").rearrange("p (k b i) -> p k b i", k=4, b=8)).then_inc(state_in, e.load("state_in", "state_in"))
                eng.dma_start(wg, row("wg").rearrange("p (w n) -> p w n", w=2)).then_inc(wg_in, e.load("wg_in", "wg_in"))
                eng.wait_ge(vector_steps, e.at("dec_y"))
                eng.dma_start(row("o_ss").rearrange("p (k b i) -> p k b i", k=4, b=8), SD).then_inc(sample_out, e.load("sample_out", "sample_out"))
                eng.wait_ge(vector_steps, e.at("fin_low3_all"))
                eng.wait_ge(sample_out, e.at("sample_out"))
                eng.wait_ge(shift_out, e.at("shift_out"))
                eng.wait_ge(spill, e.at("spill"))
                for k in range(NIN, NIN + 3):
                    eng.sem_inc(sync_idle, 1)
                    fill_dma(l, k, wait=False)
                for k in range(KT):
                    eng.dma_start(x[:, k, :], d["x_keep"][:, k * T:(k + 1) * T]).then_inc(x_back[k], e.load(f"x_back{k}", f"x_back{k}"))
                for k in range(NIN + 3, NIN + KT + 6):
                    fill_dma(l, k)
                with eng.Fori(0, NFF // 2) as i, e.rounds("ff", NFF // 2, i):
                    for j in range(6):
                        fill_dma(l, NIN + KT + 6 + j, i, 6)
            with eng.Fori(0, NC3) as c, e.rounds("nf", NC3, c):
                seg = bass.ds(c * CW, CW)
                eng.wait_ge(vector_steps, e.at("y_done"))
                eng.dma_start(d["o_y"].rearrange("p (k t) -> p k t", k=KT)[:, :, seg], x[:, :, seg]).then_inc(y_out, e.load("y_out", "y_out"))
            eng.wait_ge(y_out, e.at("y_out"))
            eng.wait_ge(state_out, e.at("state_out1"))
            eng.wait_ge(sample_out, e.at("sample_out"))
            eng.wait_ge(shift_out, e.at("shift_out"))
            eng.wait_ge(k_out, e.at("k_out"))
            eng.wait_ge(window_out, e.at("window_out"))
            for s in range(3):
                eng.wait_ge(raw_in[s], (L * PER_SLOT[s] + 2) * 16)

        @block.gpsimd
        def _(eng):
            e = Count(steps, "pool")
            prep = Chunk(steps, "pool_prep")
            eng.sem_inc(pool_steps, CREDIT)
            eng.sem_inc(pool_prep, CHUNK_CREDIT)

            def fill_low(l, k, i=0, per=0):
                dl, kk = after(k)
                g = (l + dl) * UL + kk + i * per
                eng.wait_ge(w_high, g + 1)
                eng.tensor_tensor(wl[slot(kk)][:, :], raw[slot(kk)][:, :], wh[slot(kk)][:, :].bitcast(F32),
                                  ALU.subtract).then_inc(w_low, 1)

            for k in range(3):
                fill_low(0, k)
            with eng.Fori(0, L) as l, e.rounds("layer", L, l):
                with eng.Fori(0, 5) as i, e.rounds("wa", 5, i):
                    for j in range(3):
                        fill_low(l, 3 + j, i, 3)
                for k in range(18, NIN):
                    fill_low(l, k)
                eng.wait_ge(tensor_steps, e.at("win_last"))
                eng.sem_inc(pool_idle, 1)
                for v in (kd[:, :, 0:WIN], vp[0], vp[1], bdq):
                    eng.memset(v, 0.0).then_inc(pool_steps, e.step())
                eng.memset(stat[:, :], 0.0).then_inc(pool_steps, e.step("att_zero"))
                eng.wait_ge(scalar_steps, e.at("att_high_dec"))
                eng.wait_ge(vector_steps, e.at("att_low_dec"))
                eng.wait_ge(k_out, e.at("k_out"))
                eng.sem_inc(pool_idle, 1)
                eng.memset(lw[:, :, :, 0], 0.0).then_inc(pool_steps, e.step("lw_zero"))
                eng.wait_ge(att_out, e.at("att_out"))
                eng.wait_ge(vector_steps, e.at("elem_last"))
                eng.sem_inc(pool_idle, 1)
                for v in (*abd, bbd, vbd, *Sc, *la, *Tt[0], *Tt[1], *sas, Ss[0]):
                    eng.memset(v, 0.0).then_inc(pool_steps, e.step())
                eng.memset(Ss[1], 0.0).then_inc(pool_steps, e.step("chunk_zero"))

                def chunk(c, q, P):
                    if P:
                        prep.begin()
                        tok = bass.ds((c + 2) * CH, CH)
                        eng.wait_ge(scalar_prep, at_chunk("scalar_prep", "exp_ar", l, c + 2))
                        eng.sem_inc(pool_idle, 1)
                        eng.tensor_tensor(arc[q][:, :, 0, :], nkk[:, :, tok], arc[q][:, :, 0, :], ALU.mult).then_inc(pool_prep, prep.step())
                        eng.tensor_tensor(arc[q][:, :, 1, :], proj[:, 0:4, tok], arc[q][:, :, 1, :], ALU.mult).then_inc(pool_prep, prep.step("ar"))
                        eng.wait_ge(scalar_prep, at_chunk("scalar_prep", "exp_b", l, c + 2))
                        eng.sem_inc(pool_idle, 1)
                        eng.tensor_tensor(bc, bb[:, :, tok], bc, ALU.mult).then_inc(pool_prep, prep.step("bc"))

                chunk(-2, 0, True)
                chunk(-1, 1, True)
                with eng.Fori(0, NCH // 2 - 1) as i, e.rounds("rc", NCH // 2 - 1, i):
                    for q in range(2):
                        chunk(i * 2 + q, q, True)
                eng.wait_ge(att_back, e.at("att_back"))
                eng.sem_inc(pool_idle, 1)
                eng.tensor_copy(hl[:, 4:8, :], att_low).then_inc(pool_steps, e.step("att_low_back"))
                for k in range(NIN, NIN + KT + 3):
                    fill_low(l, k)
                with eng.Fori(0, NFF // 2) as i, e.rounds("ff", NFF // 2, i):
                    for j in range(6):
                        fill_low(l, NIN + KT + 3 + j, i, 6)

        @block.scalar
        def _(eng):
            e = Count(steps, "scalar")
            prep, inv, state = Chunk(steps, "scalar_prep"), Chunk(steps, "scalar_inv"), Chunk(steps, "scalar_state")
            eng.sem_inc(scalar_steps, CREDIT)
            eng.sem_inc(scalar_prep, CHUNK_CREDIT)
            eng.sem_inc(scalar_inv, CHUNK_CREDIT)
            eng.sem_inc(scalar_state, CHUNK_CREDIT)
            a = eng.activation

            def fill_high(l, k, i=0, per=0, used=None):
                dl, kk = after(k)
                g = (l + dl) * UL + kk + i * per
                eng.wait_ge(raw_in[slot(kk)], loads(l + dl, kk, i, per))
                if used:
                    eng.wait_ge(tensor_steps, e.at(used))
                eng.copy(wh[slot(kk)][:, :], raw[slot(kk)][:, :]).then_inc(w_high, 1)

            def norm(p, last):
                with eng.Fori(0, NC3) as c, e.rounds(p, NC3, c):
                    seg = bass.ds(c * CW, CW)
                    eng.wait_ge(tensor_steps, e.at(p + "_ss", back=1))
                    for k in range(KT):
                        a(sq[:, k, :], x[:, k, seg], ACT.Square).then_inc(scalar_steps, e.step(f"{p}_sq{k}"))
                    eng.wait_ge(tensor_steps, e.at(p + "_ss"))
                    if last:
                        eng.wait_ge(vector_steps, e.at(p + "_recip", back=1))
                    a(std[:, :], bank[7][:, 0:CW], ACT.Sqrt, bias=eps_rms, scale=1.0 / DM).then_inc(scalar_steps, e.step(p + "_std"))
                    if not last:
                        for k in range(KT):
                            eng.wait_ge(vector_steps, e.at(f"{p}_n{k}"))
                            eng.copy(hh[:, k, seg], hn[:, k, :]).then_inc(scalar_steps, e.step(f"{p}_high{k}"))

            for k in range(3):
                fill_high(0, k)
            eng.wait_ge(x_in, e.at("x_in"))
            eng.wait_ge(vector_steps, e.at("eps"))
            with eng.Fori(0, L) as l, e.rounds("layer", L, l):
                eng.wait_ge(vector_steps, e.at("ff_add_last", back=1))
                eng.wait_ge(tensor_steps, e.at("ff_down_last", back=1))
                norm("n1", False)
                eng.wait_ge(spill, e.at("spill"))
                eng.wait_ge(vector_steps, e.at("n1_low7"))
                with eng.Fori(0, 5) as i, e.rounds("wa", 5, i):
                    for j in range(3):
                        for c in range(NC3):
                            eng.wait_ge(tensor_steps, e.at(f"wa_mm{j}{c}"))
                            eng.copy(proj[:, bass.ds(3 * i + j, 1), cs(c)].rearrange("p a t -> p (a t)"),
                                            bank[c][:, 0:CW]).then_inc(scalar_steps, e.step(f"wa_ev{j}{c}"))
                        eng.wait_ge(scalar_steps, e.mine())
                        eng.copy(raw9[:, bass.ds(3 * i + j, 1), :].rearrange("p a t -> p (a t)"),
                                        proj[:, bass.ds(3 * i + j, 1), NP_ - 1:T].rearrange("p a t -> p (a t)")).then_inc(scalar_steps, e.step("raw9_last" if j == 2 else f"raw9_{j}"))
                        fill_high(l, 3 + j, i, 3, f"wa_mm{j}2")
                for k in range(15, NIN):
                    for c in range(NC3):
                        eng.wait_ge(tensor_steps, e.at(f"wb_mm{k}{c}"))
                        eng.copy(proj[:, k, cs(c)], bank[c][:, 0:CW]).then_inc(scalar_steps, e.step(f"wb_ev{k}{c}"))
                    if k + 3 < NIN:
                        fill_high(l, k + 3, used=f"wb_mm{k}2")

                for g in range(2):
                    eng.wait_ge(vector_steps, e.at("kd_last"))
                    eng.copy(kro[64 * g:64 * g + 64, :], kd[64 * g:64 * g + 64, g, NP_:NP_ + 136]).then_inc(scalar_steps, e.step(f"k_tail{g}"))
                eng.wait_ge(scalar_steps, e.mine())
                eng.wait_ge(window_in, e.at("window_in"))
                eng.copy(Kw[:, :, 127], kro[:, 128:136]).then_inc(scalar_steps, e.step("k_new"))
                eng.copy(Vw[:, :, 127], proj[:, 20, NP_:T]).then_inc(scalar_steps, e.step("v_new"))
                eng.wait_ge(pool_steps, e.at("att_zero"))
                eng.wait_ge(vector_steps, e.at("rq_last"))
                with eng.Fori(0, 4) as i, e.rounds("ab", 4, i):
                    for n in range(2):
                        blk = bass.ds(i * 256 + n * 128, 128)
                        o = f"ab{n}_"
                        if n == 0:
                            eng.wait_ge(tensor_steps, e.at("ab1_score", back=1))
                            eng.wait_ge(tensor_steps, e.at("ab1_vt", back=1))
                        else:
                            eng.wait_ge(tensor_steps, e.at("ab0_score"))
                            eng.wait_ge(tensor_steps, e.at("ab0_vt"))
                        for h in range(2):
                            rows = slice(64 * h, 64 * h + 64)
                            eng.copy(bdq[rows, :, 128 * h:128 * h + 128], proj[rows, 15:19, blk]).then_inc(scalar_steps, e.step(f"{o}bdq{h}"))
                        eng.copy(vblk[:, :], proj[:, 20, blk]).then_inc(scalar_steps, e.step(o + "vblk"))
                        eng.wait_ge(tensor_steps, e.at(o + "vt"))
                        if n == 0:
                            eng.wait_ge(tensor_steps, e.at("ab1_pv", back=1))
                        else:
                            eng.wait_ge(tensor_steps, e.at("ab0_pv"))
                        eng.copy(vp[n][:, :, 64:128], bank[7][:, 0:128].rearrange("p (g t) -> p g t", g=2)).then_inc(scalar_steps, e.step(o + "vp"))
                        eng.wait_ge(vector_steps, e.at(o + "negmax"))
                        for h in range(8):
                            a(sm[:, h, :], sm[:, h, :], ACT.Exp, bias=stat[:, 16 + h:17 + h],
                                     accum_out=stat[:, 24 + h:25 + h]).then_inc(scalar_steps, e.step(f"{o}exp{h}"))
                        a(stat[:, 40:48], stat[:, 32:40], ACT.Exp).then_inc(scalar_steps, e.step(o + "sinkexp"))
                        for q in (1, 3):
                            eng.wait_ge(tensor_steps, e.at(f"{o}pt{q}"))
                            eng.copy(pT[:, 4 * q:4 * q + 4, :],
                                            bank[4 + q][:, :].rearrange("p (h t) -> p h t", h=4)).then_inc(scalar_steps, e.step(f"{o}ptc{q}"))
                        eng.wait_ge(tensor_steps, e.at(o + "pv"))
                        eng.copy(hh[:, 4:8, blk], bank[0][:, :].rearrange("p (k t) -> p k t", k=4)).then_inc(scalar_steps, e.step(o + "high"))
                eng.wait_ge(tensor_steps, e.at("d_qz"))
                eng.copy(qz[:, :], bank[1][:, 0:64]).then_inc(scalar_steps, e.step("d_qz_c"))
                eng.wait_ge(vector_steps, e.at("d_sub"))
                a(smd[0:8, :, :], smd[0:8, :, :], ACT.Exp).then_inc(scalar_steps, e.step("d_exp"))
                a(stat[0:8, 8:16], stat[0:8, 0:8], ACT.Exp, bias=par[0:8, PAR["sinkcol"]:PAR["sinkcol"] + 1],
                         scale=-1.0).then_inc(scalar_steps, e.step("d_sinkexp"))
                for q in range(2):
                    eng.wait_ge(tensor_steps, e.at(f"d_vt{q}"))
                    eng.copy(VwT[:, 4 * q:4 * q + 4, :], bank[5 + q][:, :].rearrange("p (b t) -> p b t", b=4)).then_inc(scalar_steps, e.step(f"d_vtc{q}"))
                eng.wait_ge(tensor_steps, e.at("d_pt"))
                eng.copy(pTd[:, :], bank[4][:, 0:64]).then_inc(scalar_steps, e.step("d_ptc"))
                eng.wait_ge(tensor_steps, e.at("d_pv"))
                eng.copy(ov[:, :], bank[7][:, 0:64]).then_inc(scalar_steps, e.step("d_ov"))
                eng.wait_ge(tensor_steps, e.at("d_place"))
                eng.copy(hh[:, 4:8, NP_:T], bank[0][:, 0:32].rearrange("p (k t) -> p k t", k=4)).then_inc(scalar_steps, e.step("att_high_dec"))

                eng.wait_ge(vector_steps, e.at("edge_put"))
                a(proj[0:64, 12, :], proj[0:64, 12, :], ACT.Tanh).then_inc(scalar_steps, e.step("tanh"))
                a(proj[:, 13:15, :], proj[:, 13:15, :], ACT.Sigmoid).then_inc(scalar_steps, e.step("sig_gate"))
                eng.wait_ge(pool_steps, e.at("lw_zero"))
                eng.wait_ge(vector_steps, e.at("att_low_dec"))
                eng.wait_ge(k_out, e.at("k_out"))
                for o in range(4):
                    for q in range(2):
                        eng.wait_ge(tensor_steps, e.at(f"lora{o}"))
                        a(lw[:, o, 8 * q:8 * q + 8, 1:65], bank[q][:, :].rearrange("p (n t) -> p n t", n=8),
                                 ACT.Sigmoid, bias=pc("w0", o)).then_inc(scalar_steps, e.step(f"lw{o}{q}"))
                        a(bb[:, o, 512 * q:512 * q + 512], bank[3 + q][:, :], ACT.Sigmoid, bias=pc("a0", o)).then_inc(scalar_steps, e.step(f"a{o}{q}"))
                    a(lwd[:, o, :], bank[2][:, 0:8], ACT.Sigmoid, bias=pc("w0", o)).then_inc(scalar_steps, e.step())
                    a(bb[:, o, NP_:T], bank[2][:, 8:16], ACT.Sigmoid, bias=pc("a0", o)).then_inc(scalar_steps, e.step(f"lora_ev{o}"))
                for o in range(4):
                    if o:
                        eng.wait_ge(tensor_steps, e.at(f"kk_mm{o - 1}"))
                    a(ksq[:, :], proj[:, 4 + o, :], ACT.Square, scale=pc("k_k", o)).then_inc(scalar_steps, e.step(f"ksq{o}"))
                    eng.wait_ge(tensor_steps, e.at(f"kk_mm{o}"))
                    if o:
                        eng.wait_ge(vector_steps, e.at(f"kk_recip{o - 1}"))
                    for c in range(NC3):
                        a(nrm[:, cs(c)], bank[5 + c][:, 0:CW], ACT.Sqrt).then_inc(scalar_steps, e.step(f"knorm{o}{c}"))

                eng.wait_ge(vector_steps, e.at("elem_last"))
                eng.wait_ge(pool_steps, e.at("chunk_zero"))

                def chunk(c, q, B, A, P):
                    o = 1 - q
                    ps = lambda b, lo, hi, k: bank[b][:, lo:hi].rearrange("p (k t) -> p k t", k=k)
                    low, lc = slice(64, 128), slice(64, 128)
                    lwi = lambda rows, lo: lw[rows, :, bass.ds(c + 2, 1), lo:lo + 64].rearrange("p k a t -> p k (a t)")
                    allp = slice(0, 128)
                    if B:
                        state.begin()
                        for g in range(2):
                            eng.wait_ge(tensor_state, at_chunk("tensor_state", f"s1_{g}", l, c))
                            eng.copy(sa0[g], ps(4 * g + 3, 0, 128, 2)).then_inc(scalar_state, state.step(f"sa0_{g}"))
                    if A:
                        inv.begin()
                        for g in range(2):
                            eng.wait_ge(tensor_inv, at_chunk("tensor_inv", f"g1_{g}", l, c + 1))
                            vt = ps(4 * g + 2, 0, 256, 2)
                            for h in range(2):
                                rows = slice(64 * h, 64 * h + 64)
                                eng.copy(vc[o][g][rows], vt[rows, :, rows]).then_inc(scalar_inv, inv.step())
                            eng.copy(vts[o][g], vt).then_inc(scalar_inv, inv.step(f"vts_{g}"))
                    if B:
                        for g in range(2):
                            eng.wait_ge(tensor_state, at_chunk("tensor_state", f"s2_{g}", l, c))
                            eng.copy(sac[g][low], ps(4 * g + 3, 128, 256, 2)[low]).then_inc(scalar_state, state.step())
                            eng.copy(sas[g][low, :, lc], ps(4 * g + 3, 128, 256, 2)[low]).then_inc(scalar_state, state.step(f"sa_{g}"))
                    if A:
                        for g in range(2):
                            eng.wait_ge(tensor_inv, at_chunk("tensor_inv", f"l2_{g}", l, c + 1))
                            eng.copy(nr[1][g][low, :, 0], ps(4 * g + 1, 128, 384, 4)[low]).then_inc(scalar_inv, inv.step())
                            eng.copy(la[g][low, :, lc], ps(4 * g + 1, 128, 384, 4)[low]).then_inc(scalar_inv, inv.step(f"l2e_{g}"))
                        for g in range(2):
                            eng.wait_ge(tensor_inv, at_chunk("tensor_inv", f"bkt_{g}", l, c + 1))
                            eng.copy(bks[o][g], ps(4 * g + 2, 0, 512, 4)).then_inc(scalar_inv, inv.step(f"bks_{g}"))
                    if B:
                        for g in range(2):
                            eng.wait_ge(vector_state, at_chunk("vector_state", f"S_add{g}", l, c))
                            eng.copy(yar[:, 2 * g:2 * g + 2, bass.ds(c * CH, CH)], ps(4 * g + 3, 384, 512, 2)
                                     ).then_inc(scalar_state, state.step(f"y{g}"))
                    if P:
                        prep.begin()
                        eng.wait_ge(tensor_state, at_chunk("tensor_state", "s3_1", l, c))
                        eng.wait_ge(vector_state, at_chunk("vector_state", "S_new1", l, c))
                        eng.sem_inc(scalar_idle, 1)
                        a(arc[q][:, :, 0, :], lwi(allp, 0), ACT.Exp, scale=-CDEC).then_inc(scalar_prep, prep.step())
                        a(arc[q][:, :, 1, :], lwi(allp, 1), ACT.Exp, scale=-CDEC).then_inc(scalar_prep, prep.step("exp_ar"))
                    if A:
                        for g in range(2):
                            v = bank[4 * g][:, :].rearrange("p (m r t) -> p m r t", m=4, r=2)
                            eng.wait_ge(tensor_inv, at_chunk("tensor_inv", f"l4_{g}", l, c + 1))
                            eng.copy(nr[0][g][low, :, 0], v[low, :, 0]).then_inc(scalar_inv, inv.step())
                            eng.copy(lb[g][low, :, lc], v[low, :, 0]).then_inc(scalar_inv, inv.step(f"l4e_{g}"))
                    if P:
                        a(pend[q][:, :].unsqueeze(2), lw[:, :, bass.ds(c + 2, 1), 64:65].rearrange("p k a t -> p k (a t)"), ACT.Exp, scale=-CDEC
                          ).then_inc(scalar_prep, prep.step("exp_end"))
                        eng.wait_ge(tensor_inv, at_chunk("tensor_inv", "bkt_1", l, c + 1))
                        eng.sem_inc(scalar_idle, 1)
                        a(bc, lwi(allp, 1), ACT.Exp, scale=CDEC).then_inc(scalar_prep, prep.step("exp_b"))
                    if A:
                        for g in range(2):
                            v = bank[4 * g + 1][:, :].rearrange("p (m r t) -> p m r t", m=4, r=2)
                            eng.wait_ge(tensor_inv, at_chunk("tensor_inv", f"l8_{g}", l, c + 1))
                            eng.copy(la[g][low, :, lc], v[low, :, 0]).then_inc(scalar_inv, inv.step(f"l8e_{g}"))
                    if P:
                        for h in range(2):
                            rows = slice(64 * h, 64 * h + 64)
                            a(bbd[rows, :, rows], lwi(rows, 1), ACT.Exp, scale=CDEC).then_inc(scalar_prep, prep.step(f"exp_bbd{h}"))
                    if A:
                        for g in range(2):
                            eng.wait_ge(vector_inv, at_chunk("vector_inv", f"r8c_{g}", l, c + 1))
                            eng.copy(lb[g][low, :, lc], nr[0][g][low, :, 1]).then_inc(scalar_inv, inv.step(f"r8e_{g}"))
                    if P:
                        for h in range(2):
                            rows = slice(64 * h, 64 * h + 64)
                            a(abd[q][rows, :, rows], lwi(rows, 0), ACT.Exp, scale=-CDEC).then_inc(scalar_prep, prep.step(f"exp_abd{h}"))
                    if A:
                        for g in range(2):
                            eng.wait_ge(vector_inv, at_chunk("vector_inv", f"m2c_{g}", l, c + 1))
                            eng.copy(la[g][low, 0:2, lc], nr[1][g][low, 2:4, 1]).then_inc(scalar_inv, inv.step(f"m2e_{g}"))
                    if P:
                        for h in range(2):
                            rows = slice(64 * h, 64 * h + 64)
                            eng.copy(vbd[rows, :, rows], proj[rows, 8:12, bass.ds((c + 2) * CH, CH)]).then_inc(scalar_prep, prep.step(f"vbd{h}"))
                    if A:
                        for g in range(2):
                            eng.wait_ge(vector_inv, at_chunk("vector_inv", f"m4c_{g}", l, c + 1))
                            eng.copy(Tt[o][g][low, :, lc], nr[0][g][low, 0:2, 1]).then_inc(scalar_inv, inv.step(f"m4e_{g}"))

                chunk(-2, 0, B=False, A=False, P=True)
                chunk(-1, 1, B=False, A=True, P=True)
                with eng.Fori(0, NCH // 2 - 1) as i, e.rounds("rc", NCH // 2 - 1, i):
                    for q in range(2):
                        chunk(i * 2 + q, q, B=True, A=True, P=True)
                chunk(NCH - 2, 0, B=True, A=True, P=False)
                chunk(NCH - 1, 1, B=True, A=False, P=False)

                eng.wait_ge(vector_state, at_chunk("vector_state", "S_new1", l, NCH - 1))
                eng.wait_ge(tensor_state, at_chunk("tensor_state", "s3_1", l, NCH - 1))
                eng.wait_ge(state_out, e.at("state_out1"))
                a(wdec, lwd, ACT.Exp, scale=-CDEC).then_inc(scalar_steps, e.step("wdec"))
                with eng.Fori(0, NC3) as c, e.rounds("fin", NC3, c):
                    seg = bass.ds(c * CW, CW)
                    for o in range(4):
                        yc, q2, sd, rs, bo, ot = fb[o % 2]
                        b4 = 4 * (o % 2)
                        eng.wait_ge(vector_steps, e.at(f"fin_yc{o}"))
                        if o >= 2:
                            eng.wait_ge(tensor_steps, e.at(f"fin_var{o - 2}"))
                        else:
                            eng.wait_ge(tensor_steps, e.at(f"fin_var{o + 2}", back=1))
                        a(q2[:, :], yc[:, :], ACT.Square).then_inc(scalar_steps, e.step(f"fin_sq{o}"))
                        eng.wait_ge(tensor_steps, e.at(f"fin_var{o}"))
                        a(sd[:, :], bank[b4 + 1][:, 0:CW], ACT.Sqrt, bias=eps_lnx, scale=1.0 / HD).then_inc(scalar_steps, e.step(f"fin_sd{o}"))
                        eng.wait_ge(vector_steps, e.at(f"fin_out{o}"))
                        eng.copy(hh[:, o, seg], ot[:, :]).then_inc(scalar_steps, e.step(f"fin_high{o}"))

                eng.wait_ge(vector_steps, e.at("fin_low3_all"))
                for k in range(NIN, NIN + 3):
                    fill_high(l, k)
                for k in range(NIN, NIN + KT):
                    fill_high(l, k + 3, used=f"wo_mm{k - NIN}2")
                eng.wait_ge(vector_steps, e.at("wo_add_last"))
                norm("n2", False)
                with eng.Fori(0, NFF // 2) as i, e.rounds("ff", NFF // 2, i):
                    for j in range(2):
                        for c in range(NC3):
                            eng.wait_ge(tensor_steps, e.at(f"ff_g{j}{c}"))
                            if j:
                                eng.wait_ge(vector_steps, e.at(f"ff_mid{j - 1}{c}"))
                            else:
                                eng.wait_ge(vector_steps, e.at(f"ff_mid1{c}", back=1))
                            a(sil[:, c, :], bank[c][:, 0:CW], ACT.Silu).then_inc(scalar_steps, e.step(f"ff_sil{j}{c}"))
                        fill_high(l, NIN + KT + 3 + 2 * j, i, 6, f"ff_g{j}2")
                        for c in range(NC3):
                            eng.wait_ge(vector_steps, e.at(f"ff_mid{j}{c}"))
                            if j == 0 and c == 0:
                                eng.wait_ge(tensor_steps, e.at("ff_down_last", back=1))
                            eng.copy(mh[:, j, cs(c)], midf[:, c, :]).then_inc(scalar_steps, e.step(f"ff_high{j}{c}"))
                        fill_high(l, NIN + KT + 3 + 2 * j + 1, i, 6, f"ff_u{j}2")
                    for j in (4, 5):
                        fill_high(l, NIN + KT + 3 + j, i, 6, "ff_down_last")
            eng.wait_ge(vector_steps, e.at("ff_add_last"))
            norm("nf", True)

        @block.vector
        def _(eng):
            e = Count(steps, "vector")
            prep, inv, state = Chunk(steps, "vector_prep"), Chunk(steps, "vector_inv"), Chunk(steps, "vector_state")
            eng.sem_inc(vector_steps, CREDIT)
            eng.sem_inc(vector_prep, CHUNK_CREDIT)
            eng.sem_inc(vector_inv, CHUNK_CREDIT)
            eng.sem_inc(vector_state, CHUNK_CREDIT)
            tt, ts, stt = eng.tensor_tensor, eng.tensor_scalar, eng.scalar_tensor_tensor
            two = lambda v: v.rearrange("p k (a t) -> p k a t", a=2)
            wide = lambda v: bcast(v, 2, 2)
            mask2 = lambda m, k: bcast(m.rearrange("p (a t) -> p a t", a=2), 1, k)

            def norm(p, gain, last=False):
                def group(seg):
                    eng.wait_ge(scalar_steps, e.at(p + "_std"))
                    if last:
                        eng.wait_ge(vector_steps, e.at(f"{p}_n{KT - 1}", back=1))
                    eng.reciprocal(rstd[:, :], std[:, :]).then_inc(vector_steps, e.step(p + "_recip"))
                    eng.wait_ge(vector_steps, e.mine())
                    for k in range(KT):
                        out = x[:, k, seg] if last else hn[:, k, :]
                        stt(out, x[:, k, seg], gain(k), rstd[:, :], ALU.mult, ALU.mult).then_inc(vector_steps, e.step(f"{p}_n{k}"))
                    if last:
                        e.also("y_done")
                    else:
                        for k in range(KT):
                            eng.wait_ge(scalar_steps, e.at(f"{p}_high{k}"))
                            tt(hl[:, k, seg], hn[:, k, :], hh[:, k, seg].bitcast(F32), ALU.subtract).then_inc(vector_steps, e.step(f"{p}_low{k}"))
                        eng.wait_ge(vector_steps, e.mine())
                eng.sem_inc(vector_idle, 1)
                with eng.Fori(0, NC3) as c, e.rounds(p, NC3, c):
                    group(bass.ds(c * CW, CW))

            eng.memset(eps_rms, EPS).then_inc(vector_steps, e.step())
            eng.memset(eps_lnx, LNX_EPS).then_inc(vector_steps, e.step("eps"))
            eng.wait_ge(x_in, e.at("x_in"))
            eng.wait_ge(const_in, e.at("fin_in"))
            eng.sem_inc(vector_idle, 1)
            with eng.Fori(0, L) as l, e.rounds("layer", L, l):
                eng.wait_ge(par_in, e.at("par_in"))
                ts(negkk, par[:, PAR["k_k"]:PAR["k_k"] + 4], -1.0, None, ALU.mult).then_inc(vector_steps, e.step())
                ts(omka, par[:, PAR["k_a"]:PAR["k_a"] + 4], -1.0, 1.0, ALU.mult, ALU.add).then_inc(vector_steps, e.step())
                norm("n1", lambda k: pc("an", k))
                with eng.Fori(0, 5) as i, e.rounds("wa", 5, i):
                    for j in range(3):
                        tile = lambda lo, hi: proj[:, bass.ds(3 * i + j, 1), lo:hi].rearrange("p a t -> p (a t)")
                        eng.wait_ge(scalar_steps, e.at("raw9_last" if j == 2 else f"raw9_{j}"))
                        if j:
                            eng.wait_ge(vector_steps, e.at(f"shifted{j - 1}"))
                        else:
                            eng.wait_ge(vector_steps, e.at("shifted2", back=1))
                        tt(dif[:, 0:NP_ - 1], tile(0, NP_ - 1), tile(1, NP_), ALU.subtract).then_inc(vector_steps, e.step())
                        eng.wait_ge(vector_steps, e.mine())
                        stt(tile(1, NP_), dif[:, 0:NP_ - 1], par[:, bass.ds(3 * i + (PAR["mu"] + j), 1)], tile(1, NP_),
                                   ALU.mult, ALU.add).then_inc(vector_steps, e.step(f"shifted{j}"))
                mu = par[:, PAR["mu"]:PAR["mu"] + 15]
                eng.wait_ge(vector_steps, e.mine())
                tt(dif[:, 0:15], proj[:, 0:15, 0], mu, ALU.mult).then_inc(vector_steps, e.step())
                eng.wait_ge(shift_in, e.at("shift_in"))
                tt(edge, shd, raw9[:, :, 1:9], ALU.subtract).then_inc(vector_steps, e.step())
                eng.wait_ge(vector_steps, e.mine())
                tt(proj[:, 0:15, 0], proj[:, 0:15, 0], dif[:, 0:15], ALU.subtract).then_inc(vector_steps, e.step())
                tt(edge, edge, bcast(mu, 2, 8), ALU.mult).then_inc(vector_steps, e.step())
                eng.wait_ge(vector_steps, e.mine())
                tt(proj[:, 0:15, NP_:T], raw9[:, :, 1:9], edge, ALU.add).then_inc(vector_steps, e.step("edge_put"))

                eng.wait_ge(rope_in, e.at("rope_in"))
                eng.sem_inc(vector_idle, 1)
                with eng.Fori(0, 4) as p, e.rounds("rq", 4, p):
                    for c in range(NC3):
                        qt = proj[:, bass.ds(15 + p, 1), cs(c)].rearrange("p a t -> p (a t)")
                        eng.wait_ge(vector_steps, e.mine())
                        eng.wait_ge(tensor_steps, e.at(f"rq_rot{c}"))
                        tt(rt[:, c, :], bank[c][:, 0:CW], sin[:, cs(c)], ALU.mult).then_inc(vector_steps, e.step())
                        tt(qt, qt, cos[:, cs(c)], ALU.mult).then_inc(vector_steps, e.step())
                        eng.wait_ge(vector_steps, e.mine())
                        tt(qt, qt, rt[:, c, :], ALU.add).then_inc(vector_steps, e.step("rq_last" if c == 2 else f"rq_add{c}"))
                for g in range(2):
                    for c in range(NC3):
                        kt = kd[:, g, WIN + c * CW:WIN + (c + 1) * CW]
                        eng.wait_ge(tensor_steps, e.at(f"rk{g}{c}"))
                        eng.wait_ge(vector_steps, e.mine())
                        tt(rt[:, c, :], bank[3 + c][:, 0:CW], sin[:, cs(c)], ALU.mult).then_inc(vector_steps, e.step())
                        tt(kt, bank[c][:, 0:CW], cos[:, cs(c)], ALU.mult).then_inc(vector_steps, e.step())
                        eng.wait_ge(vector_steps, e.mine())
                        tt(kt, kt, rt[:, c, :], ALU.add).then_inc(vector_steps, e.step("kd_last" if (g, c) == (1, 2) else f"kd{g}{c}"))
                mx, nmx, den, sk, se, rd = (stat[:, 8 * n:8 * n + 8] for n in (0, 2, 3, 4, 5, 6))
                sink = par[:, PAR["sink"]:PAR["sink"] + 8]
                eng.wait_ge(pool_steps, e.at("att_zero"))
                eng.sem_inc(vector_idle, 1)
                with eng.Fori(0, 4) as i, e.rounds("ab", 4, i):
                    for n in range(2):
                        o = f"ab{n}_"
                        blk = bass.ds(i * 256 + n * 128, 128)
                        mk = (amask[:, bass.ds(i * 256, 256)] if n == 0 else amask[:, 1024:1280])
                        for p in range(4):
                            eng.wait_ge(tensor_steps, e.at(f"{o}s{p}"))
                            eng.wait_ge(vector_steps, e.mine())
                            stt(sm[:, 2 * p:2 * p + 2, :], bank[p][:, :].rearrange("p (h t) -> p h t", h=2), SCALE,
                                       bcast(mk, 1, 2), ALU.mult, ALU.add).then_inc(vector_steps, e.step(f"{o}sc{p}"))
                        eng.wait_ge(vector_steps, e.mine())
                        eng.tensor_reduce(mx, sm, AX.X, ALU.max).then_inc(vector_steps, e.step())
                        eng.wait_ge(vector_steps, e.mine())
                        tt(mx, mx, sink, ALU.max).then_inc(vector_steps, e.step())
                        eng.wait_ge(vector_steps, e.mine())
                        tt(sk, sink, mx, ALU.subtract).then_inc(vector_steps, e.step())
                        ts(nmx, mx, -1.0, None, ALU.mult).then_inc(vector_steps, e.step(o + "negmax"))
                        eng.wait_ge(scalar_steps, e.at(o + "sinkexp"))
                        tt(den, den, se, ALU.add).then_inc(vector_steps, e.step())
                        eng.wait_ge(vector_steps, e.mine())
                        eng.reciprocal(rd, den).then_inc(vector_steps, e.step())
                        eng.wait_ge(vector_steps, e.mine())
                        for h in range(8):
                            ts(sm[:, h, :], sm[:, h, :], rd[:, h:h + 1], None, ALU.mult).then_inc(vector_steps, e.step(f"{o}p{h}"))
                        for q in (0, 2):
                            eng.wait_ge(tensor_steps, e.at(f"{o}pt{q}"))
                            eng.tensor_copy(pT[:, 4 * q:4 * q + 4, :], bank[4 + q][:, :].rearrange("p (h t) -> p h t", h=4)).then_inc(vector_steps, e.step(f"{o}ptc{q}"))
                        eng.wait_ge(scalar_steps, e.at(o + "high"))
                        tt(hl[:, 4:8, blk], bank[0][:, :].rearrange("p (k t) -> p k t", k=4), hh[:, 4:8, blk].bitcast(F32),
                                  ALU.subtract).then_inc(vector_steps, e.step(o + "low"))
                eng.wait_ge(vector_steps, e.mine())
                for q in range(2):
                    eng.wait_ge(tensor_steps, e.at(f"d_s{q}"))
                    ts(smd[0:8, 4 * q:4 * q + 4, :], bank[2 + q][0:8, :].rearrange("p (b t) -> p b t", b=4), SCALE, None, ALU.mult).then_inc(vector_steps, e.step())
                eng.wait_ge(vector_steps, e.mine())
                dm, dd, dr = stat[0:8, 0:8], stat[0:8, 48:56], stat[0:8, 56:64]
                bcol = lambda v: bcast(v, 2, 128)
                eng.tensor_reduce(dm, smd[0:8], AX.X, ALU.max).then_inc(vector_steps, e.step())
                eng.wait_ge(vector_steps, e.mine())
                ts(dm, dm, par[0:8, PAR["sinkcol"]:PAR["sinkcol"] + 1], None, ALU.max).then_inc(vector_steps, e.step())
                eng.wait_ge(vector_steps, e.mine())
                tt(smd[0:8], smd[0:8], bcol(dm), ALU.subtract).then_inc(vector_steps, e.step("d_sub"))
                eng.wait_ge(scalar_steps, e.at("d_exp"))
                eng.tensor_reduce(dd, smd[0:8], AX.X, ALU.add).then_inc(vector_steps, e.step())
                eng.wait_ge(scalar_steps, e.at("d_sinkexp"))
                eng.wait_ge(vector_steps, e.mine())
                tt(dd, dd, stat[0:8, 8:16], ALU.add).then_inc(vector_steps, e.step())
                eng.wait_ge(vector_steps, e.mine())
                eng.reciprocal(dr, dd).then_inc(vector_steps, e.step())
                eng.wait_ge(vector_steps, e.mine())
                tt(smd[0:8], smd[0:8], bcol(dr), ALU.mult).then_inc(vector_steps, e.step("d_p"))
                eng.wait_ge(scalar_steps, e.at("att_high_dec"))
                tt(hl[:, 4:8, NP_:T], bank[0][:, 0:32].rearrange("p (k t) -> p k t", k=4), hh[:, 4:8, NP_:T].bitcast(F32),
                          ALU.subtract).then_inc(vector_steps, e.step("att_low_dec"))

                for o in range(4):
                    eng.wait_ge(scalar_steps, e.at(f"lw{o}1"))
                    eng.wait_ge(lora_in, e.at("lora_in"))
                    eng.tensor_tensor_scan(lw_flat[:, o, :], smask[:, :], lw_flat[:, o, :], 0.0, ALU.mult, ALU.add).then_inc(vector_steps, e.step())
                for o in range(4):
                    kt = proj[:, 4 + o, :]
                    eng.wait_ge(scalar_steps, e.at(f"knorm{o}2"))
                    eng.wait_ge(vector_steps, e.mine())
                    ts(nrm[:, :], nrm[:, :], 1e-12, None, ALU.max).then_inc(vector_steps, e.step())
                    eng.wait_ge(vector_steps, e.mine())
                    eng.reciprocal(at_[:, :], nrm[:, :]).then_inc(vector_steps, e.step(f"kk_recip{o}"))
                    eng.wait_ge(vector_steps, e.mine())
                    stt(nkk[:, o, :], kt, negkk[:, o:o + 1], at_[:, :], ALU.mult, ALU.mult).then_inc(vector_steps, e.step())
                    eng.wait_ge(scalar_steps, e.at(f"lora_ev{o}"))
                    eng.wait_ge(vector_steps, e.mine())
                    ts(at_[:, :], bb[:, o, :], pc("k_a", o), omka[:, o:o + 1], ALU.mult, ALU.add).then_inc(vector_steps, e.step())
                    eng.wait_ge(vector_steps, e.mine())
                    tt(kt, kt, at_[:, :], ALU.mult).then_inc(vector_steps, e.step())
                    stt(bb[:, o, :], nkk[:, o, :], -1.0, bb[:, o, :], ALU.mult, ALU.mult).then_inc(vector_steps, e.step("elem_last" if o == 3 else None))

                eng.wait_ge(pool_steps, e.at("chunk_zero"))
                m16 = CST["d16"][0]
                o32 = bcast(c_("o32").rearrange("p (w t) -> p w t", w=2), 2, 2)
                k22 = lambda v: v.rearrange("p (w k) t -> p w k t", w=2)

                def chunk(c, q, B, A, P):
                    o = 1 - q
                    ps = lambda b, lo, hi, k: bank[b][:, lo:hi].rearrange("p (k t) -> p k t", k=k)
                    pr = lambda b: bank[b][:, :].rearrange("p (m r t) -> p m r t", m=4, r=2)
                    top = slice(0, 64)
                    tok = bass.ds((c + 2) * CH, CH)
                    mine = lambda: eng.wait_ge(vector_inv, at_chunk("vector_inv", inv.n, l, c + 1))
                    if A:
                        inv.begin()
                        for g in range(2):
                            eng.wait_ge(tensor_inv, at_chunk("tensor_inv", f"g1_{g}", l, c + 1))
                            X = ps(4 * g + 1, 0, 128, 2)
                            Gn = bank[4 * g][:, :].rearrange("p (k w t) -> p k w t", k=2, w=2)[:, :, 0, 0:64]
                            tt(two(lb[g][:, 2:4, :]), wide(X), mask2(cst[:, m16 + 128:m16 + 256], 2), ALU.mult).then_inc(vector_inv, inv.step())
                            tt(nr[0][g][:, 2:4, 0], X, bcast(c_("d16c")[:, 64:128], 1, 2), ALU.mult).then_inc(vector_inv, inv.step())
                            tt(two(xb[g]), wide(X), mask2(c_("low"), 2), ALU.mult).then_inc(vector_inv, inv.step())
                            tt(two(lb[g][:, 0:2, :]), wide(Gn), mask2(cst[:, m16:m16 + 128], 2), ALU.mult).then_inc(vector_inv, inv.step())
                            tt(nr[0][g][:, 0:2, 0], Gn, bcast(c_("d16c")[:, 0:64], 1, 2), ALU.mult).then_inc(vector_inv, inv.step(f"n16_{g}"))
                    if B:
                        state.begin()
                        for g in range(2):
                            eng.wait_ge(tensor_state, at_chunk("tensor_state", f"s2_{g}", l, c))
                            eng.tensor_copy(sac[g][top], ps(4 * g + 3, 128, 256, 2)[top]).then_inc(vector_state, state.step())
                            eng.tensor_copy(sas[g][top, :, 0:64], ps(4 * g + 3, 128, 256, 2)[top]).then_inc(vector_state, state.step(f"sa_{g}"))
                    if A:
                        for g in range(2):
                            G = ps(4 * g, 0, 512, 4)
                            mine()
                            tt(two(nm[o][g]), wide(G[:, :, 0:64]), mask2(c_("up"), 4), ALU.mult).then_inc(vector_inv, inv.step())
                            tt(mr[o][g], G[:, :, 64:128], bcast(c_("upi"), 1, 4), ALU.mult).then_inc(vector_inv, inv.step())
                            tt(nr[1][g][:, :, 1], nr[0][g][:, :, 0], bcast(II, 1, 4), ALU.add).then_inc(vector_inv, inv.step(f"m_{g}"))
                            eng.wait_ge(tensor_inv, at_chunk("tensor_inv", f"l2_{g}", l, c + 1))
                            eng.tensor_copy(nr[1][g][top, :, 0], ps(4 * g + 1, 128, 384, 4)[top]).then_inc(vector_inv, inv.step())
                            eng.tensor_copy(la[g][top, :, 0:64], ps(4 * g + 1, 128, 384, 4)[top]).then_inc(vector_inv, inv.step(f"l2e_{g}"))
                    if B:
                        for g in range(2):
                            eng.wait_ge(tensor_state, at_chunk("tensor_state", f"s3_{g}", l, c))
                            tt(Sc[g], ps(4 * g + 3, 256, 384, 2), Sc[g], ALU.add).then_inc(vector_state, state.step(f"S_add{g}"))
                        for g in range(2):
                            eng.wait_ge(scalar_prep, at_chunk("scalar_prep", "exp_end", l, c))
                            eng.wait_ge(vector_state, at_chunk("vector_state", f"S_add{g}", l, c))
                            tt(Sc[g], Sc[g], bcast(pend[q][:, 2 * g:2 * g + 2], 2, 64), ALU.mult).then_inc(vector_state, state.step(f"S_dec{g}"))
                        for g in range(2):
                            eng.wait_ge(vector_state, at_chunk("vector_state", f"S_dec{g}", l, c))
                            tt(two(Ss[g]), wide(Sc[g]), mask2(c_("bd"), 2), ALU.mult).then_inc(vector_state, state.step(f"S_new{g}"))
                    if A:
                        for g in range(2):
                            eng.wait_ge(tensor_inv, at_chunk("tensor_inv", f"l4_{g}", l, c + 1))
                            eng.tensor_copy(nr[0][g][top, :, 0], pr(4 * g)[top, :, 0]).then_inc(vector_inv, inv.step())
                            eng.tensor_copy(lb[g][top, :, 0:64], pr(4 * g)[top, :, 0]).then_inc(vector_inv, inv.step())
                            eng.wait_ge(scalar_inv, at_chunk("scalar_inv", f"l4e_{g}", l, c + 1))
                            tt(nr[0][g][:, :, 1], pr(4 * g)[:, :, 1], nr[1][g][:, :, 1], ALU.add).then_inc(vector_inv, inv.step(f"l4e_{g}"))
                        for g in range(2):
                            eng.wait_ge(tensor_inv, at_chunk("tensor_inv", f"l8_{g}", l, c + 1))
                            eng.tensor_copy(la[g][top, :, 0:64], pr(4 * g + 1)[top, :, 0]).then_inc(vector_inv, inv.step())
                            eng.wait_ge(scalar_inv, at_chunk("scalar_inv", f"l8e_{g}", l, c + 1))
                            tt(nr[1][g][:, :, 1], pr(4 * g + 1)[:, :, 1], nr[0][g][:, :, 1], ALU.add).then_inc(vector_inv, inv.step(f"l8e_{g}"))
                    if P:
                        prep.begin()
                        eng.wait_ge(scalar_prep, at_chunk("scalar_prep", "exp_bbd1", l, c + 2))
                        tt(two(kbd), wide(proj[:, 4:8, tok]), two(bbd), ALU.mult).then_inc(vector_prep, prep.step("kbd"))
                    if A:
                        for g in range(2):
                            eng.wait_ge(tensor_inv, at_chunk("tensor_inv", f"r8_{g}", l, c + 1))
                            tt(nr[0][g][:, :, 1], ps(4 * g, 0, 256, 4), nr[1][g][:, :, 1], ALU.add).then_inc(vector_inv, inv.step(f"r8c_{g}"))
                            mine()
                            eng.tensor_copy(lb[g][top, :, 0:64], nr[0][g][top, :, 1]).then_inc(vector_inv, inv.step(f"r8e_{g}"))
                    if P:
                        eng.wait_ge(vector_prep, at_chunk("vector_prep", "kbd", l, c + 2))
                        tt(two(bbd), wide(bb[:, :, tok]), two(bbd), ALU.mult).then_inc(vector_prep, prep.step("bbd"))
                    if A:
                        for g in range(2):
                            eng.wait_ge(tensor_inv, at_chunk("tensor_inv", f"m1_{g}", l, c + 1))
                            tt(k22(nr[1][g][:, :, 0]), k22(ps(4 * g + 1, 0, 256, 4)), o32, ALU.mult).then_inc(vector_inv, inv.step(f"m1e_{g}"))
                        for g in range(2):
                            eng.wait_ge(tensor_inv, at_chunk("tensor_inv", f"m2_{g}", l, c + 1))
                            tt(nr[1][g][:, :, 1], ps(4 * g, 256, 512, 4), nr[0][g][:, :, 1], ALU.add).then_inc(vector_inv, inv.step(f"m2c_{g}"))
                            mine()
                            eng.tensor_copy(la[g][top, 0:2, 0:64], nr[1][g][top, 2:4, 1]).then_inc(vector_inv, inv.step(f"m2e_{g}"))
                    if P:
                        eng.wait_ge(scalar_prep, at_chunk("scalar_prep", "exp_abd1", l, c + 2))
                        tt(two(abd[q]), wide(nkk[:, :, tok]), two(abd[q]), ALU.mult).then_inc(vector_prep, prep.step("abd"))
                    if A:
                        for g in range(2):
                            eng.wait_ge(tensor_inv, at_chunk("tensor_inv", f"m3_{g}", l, c + 1))
                            tt(nr[0][g][:, 0:2, 0], ps(4 * g + 1, 256, 384, 2), bcast(c_("o64"), 1, 2), ALU.mult).then_inc(vector_inv, inv.step(f"m3e_{g}"))
                        for g in range(2):
                            eng.wait_ge(tensor_inv, at_chunk("tensor_inv", f"m4_{g}", l, c + 1))
                            tt(nr[0][g][:, 0:2, 1], ps(4 * g, 0, 128, 2), nr[1][g][:, 0:2, 1], ALU.add).then_inc(vector_inv, inv.step(f"m4c_{g}"))
                            mine()
                            eng.tensor_copy(Tt[o][g][top, :, 0:64], nr[0][g][top, 0:2, 1]).then_inc(vector_inv, inv.step(f"m4e_{g}"))

                chunk(-2, 0, B=False, A=False, P=True)
                chunk(-1, 1, B=False, A=True, P=True)
                with eng.Fori(0, NCH // 2 - 1) as i, e.rounds("rc", NCH // 2 - 1, i):
                    for q in range(2):
                        chunk(i * 2 + q, q, B=True, A=True, P=True)
                chunk(NCH - 2, 0, B=True, A=True, P=False)
                chunk(NCH - 1, 1, B=True, A=False, P=False)

                eng.wait_ge(state_in, e.at("state_in"))
                eng.wait_ge(scalar_steps, e.at("wdec"))
                eng.wait_ge(scalar_state, at_chunk("scalar_state", "y1", l, NCH - 1))
                eng.sem_inc(vector_idle, 1)
                with eng.Fori(0, 4) as p, e.rounds("dp", 4, p):
                    col = lambda v: bcast(v.rearrange("p a t -> p (a t)"), 2, 64)
                    tile = lambda t, q: col(t[:, bass.ds(q, 1), NP_:T])
                    S = SD[:, bass.ds(p, 1)].rearrange("p a b i -> p (a b) i")
                    iib = bcast(II, 1, 8)
                    eng.wait_ge(vector_steps, e.mine())
                    tt(t1, S, tile(nkk, p), ALU.mult).then_inc(vector_steps, e.step("dp_sa_in"))
                    tt(t2, iib, tile(proj, p + 8), ALU.mult).then_inc(vector_steps, e.step("dp_v_in"))
                    tt(S, S, col(wdec[:, bass.ds(p, 1), :]), ALU.mult).then_inc(vector_steps, e.step())
                    eng.wait_ge(tensor_steps, e.at("dp_sa"))
                    tt(t3, bank[0][:, :].rearrange("p (b i) -> p b i", b=8), tile(bb, p), ALU.mult).then_inc(vector_steps, e.step())
                    eng.wait_ge(tensor_steps, e.at("dp_v"))
                    tt(t1, bank[1][:, :].rearrange("p (b i) -> p b i", b=8), tile(proj, p + 4), ALU.mult).then_inc(vector_steps, e.step())
                    eng.wait_ge(vector_steps, e.mine())
                    tt(S, S, t3, ALU.add).then_inc(vector_steps, e.step())
                    eng.wait_ge(vector_steps, e.mine())
                    tt(S, S, t1, ALU.add).then_inc(vector_steps, e.step())
                    eng.wait_ge(vector_steps, e.mine())
                    tt(t2, S, tile(proj, p), ALU.mult).then_inc(vector_steps, e.step("dp_r_in"))
                    eng.wait_ge(tensor_steps, e.at("dp_y"))
                    tt(t3, bank[2][:, :].rearrange("p (b i) -> p b i", b=8), iib, ALU.mult).then_inc(vector_steps, e.step())
                    eng.wait_ge(vector_steps, e.mine())
                    eng.sem_inc(vector_idle, 1)
                    eng.tensor_reduce(yar[:, bass.ds(p, 1), NP_:T].rearrange("p a t -> p (a t)"), t3, AX.X, ALU.add).then_inc(vector_steps, e.step("dec_y"))

                eng.wait_ge(vector_steps, e.mine())
                eng.sem_inc(vector_idle, 1)
                with eng.Fori(0, NC3) as c, e.rounds("fin", NC3, c):
                    seg = bass.ds(c * CW, CW)
                    for o in range(4):
                        yc, q2, sd, rs, bo, ot = fb[o % 2]
                        b4 = 4 * (o % 2)
                        eng.wait_ge(vector_steps, e.mine())
                        eng.wait_ge(wg_in, e.at("wg_in"))
                        stt(bo[:, :], proj[:, o, seg], pc("r_k", o), proj[:, 4 + o, seg], ALU.mult, ALU.mult).then_inc(vector_steps, e.step(f"fin_rk{o}"))
                        eng.wait_ge(tensor_steps, e.at(f"fin_mean{o}"))
                        stt(yc[:, :], bank[b4][:, 0:CW], -1.0 / HD, yar[:, o, seg], ALU.mult, ALU.add).then_inc(vector_steps, e.step(f"fin_yc{o}"))
                        eng.wait_ge(scalar_steps, e.at(f"fin_sd{o}"))
                        eng.reciprocal(rs[:, :], sd[:, :]).then_inc(vector_steps, e.step())
                        eng.wait_ge(tensor_steps, e.at(f"fin_bonus{o}"))
                        tt(bo[:, :], bank[b4 + 2][:, 0:CW], proj[:, 8 + o, seg], ALU.mult).then_inc(vector_steps, e.step())
                        eng.wait_ge(vector_steps, e.mine())
                        stt(yc[:, :], yc[:, :], pc("lg", o), rs[:, :], ALU.mult, ALU.mult).then_inc(vector_steps, e.step())
                        eng.wait_ge(vector_steps, e.mine())
                        stt(yc[:, :], yc[:, :], pc("lb", o), bo[:, :], ALU.add, ALU.add).then_inc(vector_steps, e.step())
                        eng.wait_ge(tensor_steps, e.at(f"fin_gate{o}"))
                        eng.wait_ge(vector_steps, e.mine())
                        tt(ot[:, :], yc[:, :], bank[b4 + 3][:, 0:CW], ALU.mult).then_inc(vector_steps, e.step(f"fin_out{o}"))
                        eng.wait_ge(scalar_steps, e.at(f"fin_high{o}"))
                        tt(hl[:, o, seg], ot[:, :], hh[:, o, seg].bitcast(F32), ALU.subtract).then_inc(vector_steps, e.step("fin_low3_all" if o == 3 else f"fin_low{o}"))

                for k in range(KT):
                    eng.wait_ge(x_back[k], e.at(f"x_back{k}"))
                    for c in range(NC3):
                        eng.wait_ge(tensor_steps, e.at(f"wo_mm{k}{c}"))
                        tt(x[:, k, cs(c)], bank[c][:, 0:CW], x[:, k, cs(c)], ALU.add).then_inc(vector_steps, e.step(f"wo_add{k}{c}"))
                e.also("wo_add_last")
                eng.wait_ge(vector_steps, e.mine())
                eng.sem_inc(vector_idle, 1)
                norm("n2", lambda k: pc("fn", k))
                with eng.Fori(0, NFF // 2) as i, e.rounds("ff", NFF // 2, i):
                    for j in range(2):
                        for c in range(NC3):
                            eng.wait_ge(tensor_steps, e.at(f"ff_u{j}{c}"))
                            eng.wait_ge(scalar_steps, e.at(f"ff_sil{j}{c}"))
                            eng.wait_ge(vector_steps, e.mine())
                            tt(midf[:, c, :], sil[:, c, :], bank[3 + c][:, 0:CW], ALU.mult).then_inc(vector_steps, e.step(f"ff_mid{j}{c}"))
                        for c in range(NC3):
                            eng.wait_ge(scalar_steps, e.at(f"ff_high{j}{c}"))
                            tt(ml[:, j, cs(c)], midf[:, c, :], mh[:, j, cs(c)].bitcast(F32), ALU.subtract).then_inc(vector_steps, e.step(f"ff_low{j}{c}"))
                    for c in range(NC3):
                        for k in range(KT):
                            eng.wait_ge(tensor_steps, e.at(f"ff_d{c * KT + k}"))
                            tt(x[:, k, cs(c)], bank[6 + k % 2][:, 0:CW], x[:, k, cs(c)], ALU.add).then_inc(vector_steps, e.step(f"ff_add{c * KT + k}"))
                    e.also("ff_add_last")
                    eng.wait_ge(vector_steps, e.mine())

            eng.sem_inc(vector_idle, 1)
            norm("nf", lambda k: fng[:, k:k + 1], last=True)

        @block.tensor
        def _(eng):
            e = Count(steps, "tensor")
            inv, state = Chunk(steps, "tensor_inv"), Chunk(steps, "tensor_state")
            eng.sem_inc(tensor_steps, CREDIT)
            eng.sem_inc(tensor_inv, CHUNK_CREDIT)
            eng.sem_inc(tensor_state, CHUNK_CREDIT)
            mm = eng.matmul

            def norm(p):
                with eng.Fori(0, NC3) as c, e.rounds(p, NC3, c):
                    eng.wait_ge(scalar_steps, e.at(p + "_std", back=1))
                    for k in range(KT):
                        eng.wait_ge(scalar_steps, e.at(f"{p}_sq{k}"))
                        last = mm(bank[7][:, 0:CW], ones, sq[:, k, :], start=(k == 0), stop=(k == KT - 1))
                    last.then_inc(tensor_steps, e.step(p + "_ss"))

            def unit(k, i=0, per=0):
                eng.wait_ge(w_low, layer[0] * UL + k + i * per + 1)
                return slot(k)

            def column(out, s, wcols, act_h, act_l, start, stop):
                mm(out, wh[s][:, wcols], act_h, start=start, stop=False)
                mm(out, wh[s][:, wcols], act_l, start=False, stop=False)
                return mm(out, wl[s][:, wcols], act_h, start=False, stop=stop)

            def tile(s, out, c):
                for k in range(KT):
                    last = column(out, s, slice(k * 128, k * 128 + 128), hh[:, k, cs(c)], hl[:, k, cs(c)], k == 0, k == KT - 1)
                return last

            layer = [0]
            eng.wait_ge(const_in, e.at("fin_in"))
            eng.sem_inc(tensor_idle, 1)
            with eng.Fori(0, L) as l, e.rounds("layer", L, l):
                layer[0] = l
                norm("n1")
                eng.wait_ge(vector_steps, e.at("n1_low7"))
                eng.sem_inc(tensor_idle, 1)
                with eng.Fori(0, 5) as i, e.rounds("wa", 5, i):
                    for j in range(3):
                        s = unit(j, i, 3)
                        for c in range(NC3):
                            if j:
                                eng.wait_ge(scalar_steps, e.at(f"wa_ev{j - 1}{c}"))
                            else:
                                eng.wait_ge(scalar_steps, e.at(f"wa_ev2{c}", back=1))
                            tile(s, bank[c][:, 0:CW], c).then_inc(tensor_steps, e.step(f"wa_mm{j}{c}"))
                for k in range(15, NIN):
                    s = unit(k)
                    for c in range(NC3):
                        eng.wait_ge(scalar_steps, e.at(f"wb_ev{k - 1}{c}" if k > 15 else f"wa_ev2{c}"))
                        tile(s, bank[c][:, 0:CW], c).then_inc(tensor_steps, e.step(f"wb_mm{k}{c}"))
                e.also("win_last")

                eng.wait_ge(rope_in, e.at("rope_in"))
                eng.wait_ge(scalar_steps, e.at(f"wb_ev{NIN - 1}2"))
                eng.sem_inc(tensor_idle, 1)
                with eng.Fori(0, 4) as p, e.rounds("rq", 4, p):
                    for c in range(NC3):
                        eng.wait_ge(vector_steps, e.at("rq_last" if c == 2 else f"rq_add{c}", back=1))
                        mm(bank[c][:, 0:CW], rotm, proj[:, bass.ds(15 + p, 1), cs(c)].rearrange("p a t -> p (a t)"),
                                  start=True, stop=True).then_inc(tensor_steps, e.step(f"rq_rot{c}"))
                eng.wait_ge(vector_steps, e.at("rq_last"))
                for g in range(2):
                    for c in range(NC3):
                        if g:
                            eng.wait_ge(vector_steps, e.at(f"kd0{c}"))
                        mm(bank[c][:, 0:CW], dup[:, 128 * g:128 * g + 128], proj[:, 19, cs(c)], start=True, stop=True)
                        mm(bank[3 + c][:, 0:CW], rdup[:, 128 * g:128 * g + 128], proj[:, 19, cs(c)], start=True, stop=True).then_inc(tensor_steps, e.step(f"rk{g}{c}"))
                eng.wait_ge(vector_steps, e.at("kd_last"))
                eng.wait_ge(pool_steps, e.at("att_zero"))
                eng.sem_inc(tensor_idle, 1)
                with eng.Fori(0, 4) as i, e.rounds("ab", 4, i):
                    for n in range(2):
                        o = f"ab{n}_"
                        eng.wait_ge(scalar_steps, e.at(o + "bdq1"))
                        if n == 0:
                            eng.wait_ge(vector_steps, e.at("ab1_low", back=1))
                        else:
                            eng.wait_ge(vector_steps, e.at("ab0_low"))
                        for p in range(4):
                            for h in range(2):
                                last = mm(bank[p][:, 256 * h:256 * h + 256], bdq[:, p, 128 * h:128 * h + 128],
                                          kd[:, p // 2, bass.ds(i * 256 + n * 128, 256)], start=True, stop=True)
                            last.then_inc(tensor_steps, e.step(f"{o}s{p}"))
                        e.also(o + "score")
                        eng.wait_ge(scalar_steps, e.at(o + "vblk"))
                        if n == 0:
                            eng.wait_ge(scalar_steps, e.at("ab1_ptc3", back=1))
                        else:
                            eng.wait_ge(scalar_steps, e.at("ab0_ptc3"))
                        mm(bank[7][:, 0:128], vblk[:, :], ident, is_transpose=True, start=True, stop=True).then_inc(tensor_steps, e.step(o + "vt"))
                        eng.wait_ge(scalar_steps, e.at(o + "vp"))
                        for q in range(4):
                            for w in range(4):
                                h, kt = (4 * q + w) // 2, w % 2
                                eng.wait_ge(vector_steps, e.at(f"{o}p{h}"))
                                last = mm(bank[4 + q][:, 128 * w:128 * w + 128], sm[:, h, 128 * kt:128 * kt + 128], ident,
                                          is_transpose=True, start=True, stop=True)
                            last.then_inc(tensor_steps, e.step(f"{o}pt{q}"))
                        for p in range(4):
                            eng.wait_ge(scalar_steps if p % 2 else vector_steps, e.at(f"{o}ptc{p}"))
                            for h in range(2):
                                for kt in range(2):
                                    v = vp[(n + 1 + kt) % 2][:, p // 2, (64 - 64 * h):(192 - 64 * h)]
                                    last = mm(bank[0][:, 128 * p:128 * p + 128], v, pT[:, 2 * (2 * p + h) + kt, :],
                                              start=(h, kt) == (0, 0), stop=(h, kt) == (1, 1))
                        last.then_inc(tensor_steps, e.step(o + "pv"))
                eng.wait_ge(vector_steps, e.at("ab1_low"))
                for h in range(8):
                    s2 = 2 * (h % 2) + h // 4
                    last = mm(bank[1][:, 8 * h:8 * h + 8], sel[:, 128 * s2:128 * s2 + 128], proj[:, 15 + h // 2, NP_:T],
                              start=True, stop=True)
                last.then_inc(tensor_steps, e.step("d_qz"))
                eng.wait_ge(scalar_steps, e.at("d_qz_c"))
                eng.wait_ge(scalar_steps, e.at("v_new"))
                eng.wait_ge(scalar_steps, e.at("k_new"))
                for q in range(2):
                    for b in range(4):
                        last = mm(bank[2 + q][0:8, 128 * b:128 * b + 128],
                                  qz[:, :].rearrange("p (h b) -> p h b", h=8)[:, :, 4 * q + b], Kw[:, 4 * q + b, :], start=True, stop=True)
                    last.then_inc(tensor_steps, e.step(f"d_s{q}"))
                for q in range(2):
                    for b in range(4):
                        last = mm(bank[5 + q][:, 128 * b:128 * b + 128], Vw[:, 4 * q + b, :], ident, is_transpose=True, start=True, stop=True)
                    last.then_inc(tensor_steps, e.step(f"d_vt{q}"))
                eng.wait_ge(vector_steps, e.at("d_p"))
                eng.sem_inc(tensor_idle, 1)
                for b in range(8):
                    last = mm(bank[4][:, 8 * b:8 * b + 8], smd[0:8, b, :], ident[0:8, 0:8], is_transpose=True, start=True, stop=True)
                last.then_inc(tensor_steps, e.step("d_pt"))
                eng.wait_ge(scalar_steps, e.at("d_ptc"))
                for b in range(8):
                    last = mm(bank[7][:, 8 * b:8 * b + 8], VwT[:, b, :], pTd[:, 8 * b:8 * b + 8], start=True, stop=True)
                last.then_inc(tensor_steps, e.step("d_pv"))
                eng.wait_ge(scalar_steps, e.at("d_ov"))
                ovh = ov[:, :].rearrange("p (b h) -> p b h", b=8)
                for p in range(4):
                    for h in range(2):
                        s2 = 2 * (p // 2) + h
                        last = mm(bank[0][:, 8 * p:8 * p + 8], sel[:, 128 * s2:128 * s2 + 128], ovh[:, :, 2 * p + h],
                                  start=(h == 0), stop=(h == 1))
                last.then_inc(tensor_steps, e.step("d_place"))

                eng.wait_ge(scalar_steps, e.at("tanh"))
                eng.wait_ge(lora_in, e.at("lora_in"))
                eng.wait_ge(vector_steps, e.at("att_low_dec"))
                for o in range(4):
                    if o:
                        eng.wait_ge(scalar_steps, e.at(f"lora_ev{o - 1}"))
                    oc = slice(128 * o, 128 * o + 128)
                    for w in range(2):
                        for q in range(2):
                            mm(bank[3 * w + q][:, :], wda[:, w, oc], proj[:, 12, 512 * q:512 * q + 512], start=True, stop=True)
                        last = mm(bank[2][:, 8 * w:8 * w + 8], wda[:, w, oc], proj[:, 12, NP_:T], start=True, stop=True)
                    last.then_inc(tensor_steps, e.step(f"lora{o}"))
                for o in range(4):
                    eng.wait_ge(scalar_steps, e.at(f"ksq{o}"))
                    if o:
                        eng.wait_ge(scalar_steps, e.at(f"knorm{o - 1}2"))
                    for c in range(NC3):
                        last = mm(bank[5 + c][:, 0:CW], bdones, ksq[:, cs(c)], start=True, stop=True)
                    last.then_inc(tensor_steps, e.step(f"kk_mm{o}"))

                eng.wait_ge(vector_steps, e.at("elem_last"))
                eng.wait_ge(pool_steps, e.at("chunk_zero"))

                def square(b, at0, spread, cur, step):
                    for m in range(4):
                        out = bank[b][:, at0 + step * m:at0 + step * (m + 1)]
                        last = mm(out, spread[:, (m + 2) % 4, :], cur(m), start=True, stop=True)
                    return last

                def chunk(c, q, B, A, P):
                    o = 1 - q
                    if B:
                        state.begin()
                        for g in range(2):
                            eng.wait_ge(vector_inv, at_chunk("vector_inv", f"m_{g}", l, c))
                            eng.wait_ge(scalar_inv, at_chunk("scalar_inv", f"vts_{g}", l, c))
                            eng.wait_ge(vector_state, at_chunk("vector_state", f"S_new{g}", l, c - 1))
                            eng.wait_ge(scalar_state, at_chunk("scalar_state", f"y{g}", l, c - 1))
                            for p in range(2):
                                out = bank[4 * g + 3][:, 64 * p:64 * p + 64]
                                mm(out, abd[q][:, 2 * g + p, :], Sc[g][:, p, :], start=True, stop=False)
                                last = mm(out, nm[q][g][:, 2 * p + 1, :], vc[q][g][:, p, :], start=False, stop=True)
                            last.then_inc(tensor_state, state.step(f"s1_{g}"))
                    if A:
                        inv.begin()
                        eng.wait_ge(vector_prep, at_chunk("vector_prep", "abd", l, c + 1))
                        eng.wait_ge(pool_prep, at_chunk("pool_prep", "bc", l, c + 1))
                        eng.wait_ge(scalar_prep, at_chunk("scalar_prep", "vbd1", l, c + 1))
                        for g in range(2):
                            eng.wait_ge(vector_inv, at_chunk("vector_inv", f"m4e_{g}", l, c))
                            eng.wait_ge(scalar_inv, at_chunk("scalar_inv", f"m4e_{g}", l, c))
                            for p in range(2):
                                k = 2 * g + p
                                ar = arc[o][:, k].rearrange("p w t -> p (w t)")
                                mm(bank[4 * g][:, 256 * p:256 * p + 128], bbd[:, k, :], ar, start=True, stop=True)
                                mm(bank[4 * g][:, 256 * p + 128:256 * p + 256], kbd[:, k, :], ar, start=True, stop=True)
                                mm(bank[4 * g + 1][:, 64 * p:64 * p + 64], abd[o][:, k, :], bc[:, k, :], start=True, stop=True)
                                last = mm(bank[4 * g + 2][:, 128 * p:128 * p + 128], vbd[:, k, :], ident, is_transpose=True, start=True, stop=True)
                            last.then_inc(tensor_inv, inv.step(f"g1_{g}"))
                    if B:
                        for g in range(2):
                            eng.wait_ge(scalar_state, at_chunk("scalar_state", f"sa0_{g}", l, c))
                            eng.wait_ge(vector_inv, at_chunk("vector_inv", f"m4e_{g}", l, c))
                            eng.wait_ge(scalar_inv, at_chunk("scalar_inv", f"m4e_{g}", l, c))
                            for p in range(2):
                                last = mm(bank[4 * g + 3][:, 128 + 64 * p:192 + 64 * p], Tt[q][g][:, p, :], sa0[g][:, p, :], start=True, stop=True)
                            last.then_inc(tensor_state, state.step(f"s2_{g}"))
                    if A:
                        for g in range(2):
                            eng.wait_ge(vector_inv, at_chunk("vector_inv", f"n16_{g}", l, c + 1))
                            square(4 * g + 1, 128, lb[g], lambda m: nr[0][g][:, m, 0], 64).then_inc(tensor_inv, inv.step(f"l2_{g}"))
                        for g in range(2):
                            eng.wait_ge(scalar_inv, at_chunk("scalar_inv", f"vts_{g}", l, c + 1))
                            for p in range(2):
                                k = 2 * g + p
                                mm(bank[4 * g + 2][:, 256 * p:256 * p + 128], bbd[:, k, :], ident, is_transpose=True, start=True, stop=True)
                                last = mm(bank[4 * g + 2][:, 256 * p + 128:256 * p + 256], kbd[:, k, :], ident, is_transpose=True,
                                          start=True, stop=True)
                            last.then_inc(tensor_inv, inv.step(f"bkt_{g}"))
                    if B:
                        for g in range(2):
                            eng.wait_ge(vector_state, at_chunk("vector_state", f"sa_{g}", l, c))
                            eng.wait_ge(scalar_state, at_chunk("scalar_state", f"sa_{g}", l, c))
                            eng.wait_ge(scalar_inv, at_chunk("scalar_inv", f"bks_{g}", l, c))
                            for p in range(2):
                                out = bank[4 * g + 3][:, 256 + 64 * p:320 + 64 * p]
                                mm(out, bks[q][g][:, 2 * p, :], sac[g][:, p, :], start=True, stop=False)
                                mm(out, bks[q][g][:, 2 * p + 1, :], vc[q][g][:, p, :], start=False, stop=True)
                            for p in range(2):
                                out = bank[4 * g + 3][:, 384 + 64 * p:448 + 64 * p]
                                mm(out, Ss[g][:, p, :], arc[q][:, 2 * g + p, 1, :], start=True, stop=False)
                                mm(out, sas[g][:, p, :], mr[q][g][:, 2 * p, :], start=False, stop=False)
                                last = mm(out, vts[q][g][:, p, :], mr[q][g][:, 2 * p + 1, :], start=False, stop=True)
                            last.then_inc(tensor_state, state.step(f"s3_{g}"))
                    if A:
                        both = lambda w, g: lambda m: nr[w][g][:, m].rearrange("p r t -> p (r t)")
                        for g in range(2):
                            eng.wait_ge(scalar_inv, at_chunk("scalar_inv", f"l2e_{g}", l, c + 1))
                            eng.wait_ge(vector_inv, at_chunk("vector_inv", f"l2e_{g}", l, c + 1))
                            square(4 * g, 0, la[g], both(1, g), 128).then_inc(tensor_inv, inv.step(f"l4_{g}"))
                        for g in range(2):
                            eng.wait_ge(vector_inv, at_chunk("vector_inv", f"l4e_{g}", l, c + 1))
                            square(4 * g + 1, 0, lb[g], both(0, g), 128).then_inc(tensor_inv, inv.step(f"l8_{g}"))
                        for g in range(2):
                            eng.wait_ge(vector_inv, at_chunk("vector_inv", f"l8e_{g}", l, c + 1))
                            square(4 * g, 0, la[g], lambda m: nr[1][g][:, m, 1], 64).then_inc(tensor_inv, inv.step(f"r8_{g}"))
                        for g in range(2):
                            eng.wait_ge(vector_inv, at_chunk("vector_inv", f"r8c_{g}", l, c + 1))
                            for p in range(2):
                                mm(bank[4 * g + 1][:, 64 * p:64 * p + 64], xb[g][:, p, :], nr[0][g][:, p, 1], start=True, stop=True)
                            for p in range(2):
                                last = mm(bank[4 * g + 1][:, 128 + 64 * p:192 + 64 * p], nm[o][g][:, 2 * p, :], nr[0][g][:, 2 + p, 1],
                                          start=True, stop=True)
                            last.then_inc(tensor_inv, inv.step(f"m1_{g}"))
                        for g in range(2):
                            eng.wait_ge(scalar_inv, at_chunk("scalar_inv", f"r8e_{g}", l, c + 1))
                            eng.wait_ge(vector_inv, at_chunk("vector_inv", f"m1e_{g}", l, c + 1))
                            square(4 * g, 256, lb[g], lambda m: nr[1][g][:, m, 0], 64).then_inc(tensor_inv, inv.step(f"m2_{g}"))
                        for g in range(2):
                            eng.wait_ge(vector_inv, at_chunk("vector_inv", f"m2c_{g}", l, c + 1))
                            for p in range(2):
                                last = mm(bank[4 * g + 1][:, 256 + 64 * p:320 + 64 * p], xb[g][:, p, :], nr[1][g][:, p, 1], start=True, stop=True)
                            last.then_inc(tensor_inv, inv.step(f"m3_{g}"))
                        for g in range(2):
                            eng.wait_ge(scalar_inv, at_chunk("scalar_inv", f"m2e_{g}", l, c + 1))
                            eng.wait_ge(vector_inv, at_chunk("vector_inv", f"m3e_{g}", l, c + 1))
                            for p in range(2):
                                last = mm(bank[4 * g][:, 64 * p:64 * p + 64], la[g][:, p, :], nr[0][g][:, p, 0], start=True, stop=True)
                            last.then_inc(tensor_inv, inv.step(f"m4_{g}"))

                chunk(-1, 1, B=False, A=True, P=True)
                with eng.Fori(0, NCH // 2 - 1) as i, e.rounds("rc", NCH // 2 - 1, i):
                    for q in range(2):
                        chunk(i * 2 + q, q, B=True, A=True, P=True)
                chunk(NCH - 2, 0, B=True, A=True, P=False)
                chunk(NCH - 1, 1, B=True, A=False, P=False)

                eng.wait_ge(vector_state, at_chunk("vector_state", "S_new1", l, NCH - 1))
                eng.wait_ge(scalar_state, at_chunk("scalar_state", "y1", l, NCH - 1))
                flat = lambda v: v.rearrange("p b i -> p (b i)")
                eng.sem_inc(tensor_idle, 1)
                with eng.Fori(0, 4) as p, e.rounds("dp", 4, p):
                    eng.wait_ge(vector_steps, e.at("dp_sa_in"))
                    mm(bank[0][:, :], bdones, flat(t1), start=True, stop=True).then_inc(tensor_steps, e.step("dp_sa"))
                    eng.wait_ge(vector_steps, e.at("dp_v_in"))
                    mm(bank[1][:, :], bdones, flat(t2), start=True, stop=True).then_inc(tensor_steps, e.step("dp_v"))
                    eng.wait_ge(vector_steps, e.at("dp_r_in"))
                    mm(bank[2][:, :], bdones, flat(t2), start=True, stop=True).then_inc(tensor_steps, e.step("dp_y"))
                eng.wait_ge(vector_steps, e.at("dec_y"))
                eng.wait_ge(wg_in, e.at("wg_in"))
                eng.wait_ge(scalar_steps, e.at("sig_gate"))
                eng.sem_inc(tensor_idle, 1)
                with eng.Fori(0, NC3) as c, e.rounds("fin", NC3, c):
                    seg = bass.ds(c * CW, CW)
                    for o in range(4):
                        b4 = 4 * (o % 2)
                        yc, q2, sd, rs, bo, ot = fb[o % 2]
                        if o >= 2:
                            eng.wait_ge(vector_steps, e.at(f"fin_out{o - 2}"))
                        else:
                            eng.wait_ge(vector_steps, e.at(f"fin_out{o + 2}", back=1))
                        mm(bank[b4][:, 0:CW], bdones, yar[:, o, seg], start=True, stop=True).then_inc(tensor_steps, e.step(f"fin_mean{o}"))
                        oc = slice(128 * o, 128 * o + 128)
                        mm(bank[b4 + 3][:, 0:CW], wg[:, 0, oc], proj[:, 13, seg], start=True, stop=False)
                        mm(bank[b4 + 3][:, 0:CW], wg[:, 1, oc], proj[:, 14, seg], start=False, stop=True).then_inc(tensor_steps, e.step(f"fin_gate{o}"))
                        eng.wait_ge(vector_steps, e.at(f"fin_rk{o}"))
                        mm(bank[b4 + 2][:, 0:CW], bdones, bo[:, :], start=True, stop=True).then_inc(tensor_steps, e.step(f"fin_bonus{o}"))
                        eng.wait_ge(scalar_steps, e.at(f"fin_sq{o}"))
                        mm(bank[b4 + 1][:, 0:CW], bdones, q2[:, :], start=True, stop=True).then_inc(tensor_steps, e.step(f"fin_var{o}"))

                eng.wait_ge(vector_steps, e.at("fin_low3_all"))
                eng.wait_ge(scalar_steps, e.at("fin_high3"))
                eng.wait_ge(pool_steps, e.at("att_low_back"))
                for k in range(KT):
                    s = unit(NIN + k)
                    for c in range(NC3):
                        if k:
                            eng.wait_ge(vector_steps, e.at(f"wo_add{k - 1}{c}"))
                        tile(s, bank[c][:, 0:CW], c).then_inc(tensor_steps, e.step(f"wo_mm{k}{c}"))
                norm("n2")
                eng.wait_ge(vector_steps, e.at("n2_low7"))
                eng.sem_inc(tensor_idle, 1)
                with eng.Fori(0, NFF // 2) as i, e.rounds("ff", NFF // 2, i):
                    for j in range(2):
                        for w, n in ((0, "g"), (1, "u")):
                            s = unit(NIN + KT + 2 * j + w, i, 6)
                            for c in range(NC3):
                                prev = "sil" if n == "g" else "mid"
                                if j:
                                    eng.wait_ge(scalar_steps if n == "g" else vector_steps, e.at(f"ff_{prev}0{c}"))
                                else:
                                    eng.wait_ge(scalar_steps if n == "g" else vector_steps, e.at(f"ff_{prev}1{c}", back=1))
                                tile(s, bank[3 * w + c][:, 0:CW], c).then_inc(tensor_steps, e.step(f"ff_{n}{j}{c}"))
                    s = [unit(NIN + KT + 4 + j, i, 6) for j in range(2)]
                    for c in range(NC3):
                        eng.wait_ge(vector_steps, e.at(f"ff_low1{c}"))
                        for k in range(KT):
                            n = c * KT + k
                            eng.wait_ge(vector_steps, e.at(f"ff_add{(n - 2) % (3 * KT)}", back=int(n < 2)))
                            for j in range(2):
                                last = column(bank[6 + k % 2][:, 0:CW], s[j], slice(128 * k, 128 * k + 128),
                                              mh[:, j, cs(c)], ml[:, j, cs(c)], j == 0, j == 1)
                            last.then_inc(tensor_steps, e.step(f"ff_d{n}"))
                    e.also("ff_down_last")
            norm("nf")


def _consts():
    C = np.zeros((128, NCST), np.float32)
    put = lambda n, v: C.__setitem__((slice(None), slice(CST[n][0], CST[n][0] + CST[n][1])), v)
    r = np.arange(128)
    s, h = r % 64, r // 64
    col = np.arange(64)
    put("ident", np.eye(128))
    put("ones", 1.0)
    put("bdones", (h[:, None] == h[None, :]))
    put("II", (s[:, None] == col[None, :]))
    half = np.repeat(np.arange(2), 64)
    sameh = h[:, None] == half[None, :]
    c2 = np.tile(col, 2)
    put("bd", sameh)
    up, low = s[:, None] < c2[None, :], s[:, None] > c2[None, :]
    b16 = (s[:, None] // 16) == (c2[None, :] // 16)
    put("up", sameh & up)
    put("low", sameh & low)
    put("d16", np.concatenate([sameh & up & b16, sameh & low & b16], 1))
    u, w = s[:, None] < col[None, :], s[:, None] > col[None, :]
    k16 = (s[:, None] // 16) == (col[None, :] // 16)
    k32 = (s[:, None] // 32) == (col[None, :] // 32)
    put("upi", s[:, None] <= col[None, :])
    put("d16c", np.concatenate([u & k16, w & k16], 1))
    put("o32", np.concatenate([u & k32 & ~k16, w & k32 & ~k16], 1))
    put("o64", u & ~k32)
    inv = (10000.0 ** (-np.arange(32) / 32)).astype(np.float32)
    pos = np.concatenate([np.arange(NP_), np.full(NS, 1024)]).astype(np.float32)
    ang = (pos[None, :] * inv[r % 32][:, None]).astype(np.float32)
    rope = np.concatenate([np.cos(ang), np.sin(ang)], 1).astype(np.float32)
    rot = np.zeros((128, 128), np.float32)
    for m in range(128):
        dd = m % 64
        if dd < 32:
            rot[m + 32, m] = -1.0
        else:
            rot[m - 32, m] = 1.0
    S = np.zeros((2, 2, 128, 128), np.float32)
    for a in range(2):
        for b in range(2):
            S[a, b, a * 64 + col, b * 64 + col] = 1.0
    dup = [S[g, 0] + S[g, 1] for g in range(2)]
    mats = np.concatenate([rot, dup[0], dup[1], rot @ dup[0], rot @ dup[1], S[0, 0], S[0, 1], S[1, 0], S[1, 1]], 1)
    j = np.arange(256)
    diff = r[:, None] - j[None, :] + 128
    ok = (diff >= 0) & (diff < WIN)
    m = np.where(ok, 0.0, -1e30).astype(np.float32)
    m0 = np.where(ok & (j[None, :] >= 128), 0.0, -1e30).astype(np.float32)
    amask = np.concatenate([m0, m, m, m, m], 1)
    smask = np.ones((128, NCH, 65), np.float32)
    smask[:, :, 0] = 0.0
    return {"cst": C, "rope": rope, "mats": mats.astype(np.float32), "amask": amask, "smask": smask.reshape(128, -1)}


def _chan(v, tiles):
    v = np.asarray(v)
    return np.moveaxis(v.reshape(v.shape[0], tiles, 128, *v.shape[2:]), 1, 2)


def _pad(v, n, axis):
    out = list(v.shape)
    out[axis] = n - v.shape[axis]
    return np.concatenate([v, np.zeros(out, v.dtype)], axis)


def _lay_out(i):
    A = {k: np.asarray(v) for k, v in i.items()}
    z = dict(_consts())
    xall = np.concatenate([A["x_prompt"][0], A["x_sample"][:, 0]], 0)
    z["x"] = np.ascontiguousarray(xall.T.reshape(KT, 128, T).transpose(1, 0, 2)).reshape(128, KT * T)
    w = A["w_in"]
    w = np.concatenate([_pad(w[:, :, :1824], 1920, 2), w[:, :, 1824:]], 2)

    def tiles(w):
        ll, ki, no = w.shape
        return w.reshape(ll, ki // 128, 128, no // 128, 128).transpose(0, 3, 2, 1, 4).reshape(ll, no // 128, 128, ki)

    g, u = tiles(A["w_gate"]), tiles(A["w_up"])
    dn = A["w_down"].reshape(L, NFF, 128, DM)
    ff = np.stack([g[:, 0::2], u[:, 0::2], g[:, 1::2], u[:, 1::2], dn[:, 0::2], dn[:, 1::2]], 2).reshape(L, 3 * NFF, 128, U)
    wts = np.concatenate([tiles(w), tiles(A["w_out"]), ff], 1).reshape(L * UL, 128, U)
    z["wts"] = _pad(wts, L * UL + 6, 0)
    par = np.zeros((L, 128, NPAR), np.float32)

    def put(n, v, tiles):
        par[:, :, PAR[n]:PAR[n] + tiles] = _chan(v, tiles)

    put("an", A["attn_norm"], 8)
    put("fn", A["ffn_norm"], 8)
    put("mu", _pad(A["mu"], 1920, 1), 15)
    for n, k in (("w0", "w0"), ("a0", "a0"), ("k_k", "k_k"), ("k_a", "k_a"), ("lg", "lnx_g"), ("lb", "lnx_b")):
        put(n, A[k], 4)
    put("r_k", A["r_k"].reshape(L, 512), 4)
    par[:, :, PAR["sink"]:PAR["sink"] + 8] = A["sinks"][:, None, :]
    par[:, 0:8, PAR["sinkcol"]] = A["sinks"]
    z["par"] = par
    z["fin"] = _chan(A["final_norm"][None], 8)[0]
    z["shift"] = _chan(_pad(A["state_shift"].transpose(0, 2, 1), 1920, 1), 15).reshape(L, 128, 15 * 8)
    win = lambda c: c[:, :, 1:].transpose(0, 3, 4, 1, 2).reshape(L, 128, 8 * 127)
    z["kwin"], z["vwin"] = win(A["cache_k_win"]), win(A["cache_v_win"])
    zero = np.zeros((L, 64, 512), np.float32)
    z["wda"] = np.stack([np.concatenate([A["w_decay_up"], zero], 1), np.concatenate([zero, A["w_a_up"]], 1)], 2).reshape(L, 128, 1024)
    z["wg"] = _pad(A["w_g_up"], 256, 1).reshape(L, 2, 128, 512).transpose(0, 2, 1, 3).reshape(L, 128, 1024)
    st = A["state_rwkv"].reshape(L, 8, 4, 2, 64, 64).transpose(0, 3, 5, 2, 1, 4)
    z["states"] = st.reshape(L, 128, 2048)
    return {k: np.ascontiguousarray(v) for k, v in z.items()}


_OUT = {"o_y": (128, KT * T), "o_ps": (L, 128, 256), "o_shift": (L, 128, 135), "o_pk": (L, 128, 128), "o_pv": (L, 128, 128),
        "o_ss": (L, 128, 2048), "o_sk": (L, 128, 1024), "o_sv": (L, 128, 1024)}


def _declare(nc, arrays):
    d = {n: nc.dram_tensor(n, a.shape, F32, kind="ExternalInput").ap() for n, a in arrays.items()}
    for n, s in _OUT.items():
        d[n] = nc.dram_tensor(n, s, F32, kind="ExternalOutput").ap()
    d["x_keep"] = nc.dram_tensor("x_keep", (128, KT * T), F32).ap()
    d["att_keep"] = nc.dram_tensor("att_keep", (128, 4 * T), F32).ap()
    return d


def kernel(**inputs):
    import concourse.bacc as bacc
    from concourse.bass_utils import run_bass_kernel_spmd

    arrays = _lay_out(inputs)
    known = None
    for _ in range(2):
        nc = bacc.Bacc("TRN2", target_bir_lowering=False, num_devices=1)
        steps = Steps(known)
        program(nc, _declare(nc, arrays), steps)
        known = (steps.at, steps.per_round)
    return _results(run_bass_kernel_spmd(nc, [arrays], core_ids=[0]).results[0])


def _results(r):
    y = np.asarray(r["o_y"]).reshape(128, KT, T).transpose(2, 1, 0).reshape(T, DM)
    ps = np.asarray(r["o_ps"]).reshape(L, 2, 64, 4, 64).transpose(0, 3, 1, 4, 2).reshape(L, 1, 8, 64, 64)
    ss = np.asarray(r["o_ss"]).reshape(L, 2, 64, 4, 8, 64).transpose(0, 4, 3, 1, 5, 2).reshape(L, 8, 8, 64, 64)
    sh = np.asarray(r["o_shift"]).reshape(L, 128, 15, 9).transpose(0, 3, 2, 1).reshape(L, 9, 1920)[:, :, :1824]
    pk = np.asarray(r["o_pk"]).transpose(0, 2, 1).reshape(L, 1, 128, 2, 64)
    pv = np.asarray(r["o_pv"]).transpose(0, 2, 1).reshape(L, 1, 128, 2, 64)
    sk = np.asarray(r["o_sk"]).reshape(L, 128, 8, 128).transpose(0, 2, 3, 1).reshape(L, 8, 128, 2, 64)
    sv = np.asarray(r["o_sv"]).reshape(L, 128, 8, 128).transpose(0, 2, 3, 1).reshape(L, 8, 128, 2, 64)
    c = np.ascontiguousarray
    return (c(y[None, :NP_]), c(y[NP_:, None]), c(ps), c(sh[:, 0:1]), c(pk), c(pv), c(ss), c(sh[:, 1:9]), c(sk), c(sv))
```

```python
from contextlib import ExitStack, contextmanager

import numpy as np

import concourse.bass as bass
from concourse import mybir

F32 = mybir.dt.float32
F32R = mybir.dt.float32r
ALU = mybir.AluOpType
ACT = mybir.ActivationFunctionType
AX = mybir.AxisListType

L = 2
DM = 1024
KT = DM // 128
NP_, NS = 1024, 8
T = NP_ + NS
NC3, CW = 3, T // 3
HD = 64
NPAIR = 4
CH = 64
NCH = NP_ // CH
FF = 2816
NFF = FF // 128
NIN = 21
UL = NIN + KT + 3 * NFF
U = 1024
WIN = 128
NBLK = NP_ // WIN
CDEC = float(np.exp(-0.5))
SCALE = HD ** -0.5
EPS, LNX_EPS = 1e-5, 64e-5
ENGINES = ("tensor", "vector", "scalar", "pool")
CREDIT = 6000

PAR = {}
_at = 0
for _n, _w in (("an", 8), ("fn", 8), ("mu", 15), ("w0", 4), ("a0", 4), ("k_k", 4), ("k_a", 4), ("r_k", 4),
               ("lg", 4), ("lb", 4), ("sink", 8), ("sinkcol", 1)):
    PAR[_n] = _at
    _at += _w
NPAR = _at

CST = {}
_at = 0
for _n, _w in (("ident", 128), ("ones", 128), ("bdones", 128), ("II", 64), ("bd", 128), ("up", 128), ("low", 128),
               ("d16", 256), ("upi", 64), ("d16c", 128), ("o32", 128), ("o64", 64)):
    CST[_n] = (_at, _w)
    _at += _w
NCST = _at


CHUNK_CREDIT = 200


class Steps:

    def __init__(self, known=None):
        self.known = known
        self.at, self.per_round = {}, {}


class Count:

    def __init__(self, steps, own):
        self.steps, self.own = steps, own
        self.scopes = [["", 1, {}, None]]
        self.last = None

    @contextmanager
    def rounds(self, name, n, i):
        self.scopes.append([name, n, {}, i])
        yield
        _, _, counts, _ = self.scopes.pop()
        for sem, k in counts.items():
            self.scopes[-1][2][sem] = self.scopes[-1][2].get(sem, 0) + n * k
            self.steps.per_round[sem, name] = k

    def load(self, sem, name=None):
        self.scopes[-1][2][sem] = self.scopes[-1][2].get(sem, 0) + 1
        place = (sem, tuple((s[0], s[1], s[2].get(sem, 0)) for s in self.scopes))
        if name is not None:
            assert name not in self.steps.at, name
            self.steps.at[name] = place
        if sem == self.own:
            self.last = place
        return 16

    def step(self, name=None):
        self.load(self.own, name)
        return 1

    def also(self, name):
        self.steps.at[name] = self.last

    def value(self, place, back):
        if self.steps.known is None:
            return 1
        sem, path = place
        known = self.steps.known[1]
        inc, start = (1, CREDIT) if sem in ENGINES else (16, 0)
        here = {s[0]: s[3] for s in self.scopes[1:]}
        v = inc * sum(off for _, _, off in path) + start
        inner = None
        for name, n, _ in path[1:]:
            k = known[sem, name]
            if name in here:
                v = v + here[name] * (inc * k)
                inner = k
            else:
                v = v + (n - 1) * inc * k
        if back:
            v = v - back * inc * inner
        return v

    def at(self, name, back=0):
        return self.value(self.steps.known[0][name] if self.steps.known else None, back)

    def mine(self):
        return self.value(self.last, 0)


class Chunk:

    def __init__(self, steps, own):
        self.steps, self.own, self.n = steps, own, 0

    def begin(self):
        self.n = 0

    def step(self, name=None):
        self.n += 1
        self.steps.at[self.own, self.n] = None
        self.steps.per_round[self.own] = max(self.n, self.steps.per_round.get(self.own, 0))
        if name is not None:
            self.steps.at[self.own, name] = self.n
        return 1


def chunk_at(steps, own, name, l, c, n=NCH):
    if steps.known is None:
        return 1
    at, per_round = steps.known
    off = name if isinstance(name, int) else at[own, name]
    return l * (n * per_round[own]) + (c * per_round[own] + (CHUNK_CREDIT + off))


def bcast(v, axis, n):
    v = v.unsqueeze(axis)
    shape = list(v.shape)
    shape[axis] = n
    return v.to_broadcast(shape)


class Space:

    def __init__(self, nc, tag, *free):
        self.nc, self.tag, self.free = nc, tag, [list(f) for f in free]

    def __call__(self, name, n, dt=F32):
        n8 = -(-n // 8) * 8
        for f in self.free:
            if f[1] - f[0] >= n8:
                at = f[0]
                f[0] += n8
                return self.nc.alloc_sbuf_tensor_at(self.tag + name, [128, n], dt, offset=BASE + 4 * at)
        raise ValueError(f"no room for {name}: {n} of {self.free}")


BASE = 16512
END = 229344
HH, HL, PJ = 0, KT * T, 2 * KT * T
EX = PJ + NIN * T
TOTAL = (END - BASE) // 4
RING = TOTAL - 9 * U
FIXED = RING - NCST - 160


def program(nc, d, steps):
    with ExitStack() as ctx:
        fence = ctx.enter_context(nc.sbuf_tensor("fence", [128, (nc.sbuf_bytes_remaining - 64) // 4], F32))
        del fence
        at = lambda name, n, off, dt=F32: nc.alloc_sbuf_tensor_at(name, [128, n], dt, offset=BASE + 4 * off)
        hh = at("act_high", KT * T, HH, F32R)[:, :].rearrange("p (k t) -> p k t", k=KT)
        hl = at("act_low", KT * T, HL, F32R)[:, :].rearrange("p (k t) -> p k t", k=KT)
        proj = at("proj", NIN * T, PJ)[:, :].rearrange("p (k t) -> p k t", k=NIN)
        x = at("resid", KT * T, PJ)[:, :].rearrange("p (k t) -> p k t", k=KT)
        cst = at("consts", NCST, FIXED)
        par = at("params", NPAR, FIXED + NCST)
        dpar = at("derived", 24, FIXED + NCST + 72)
        raw = [at(f"w_raw{s}", U, RING + s * U) for s in range(3)]
        wh = [at(f"w_high{s}", U, RING + (3 + s) * U, F32R) for s in range(3)]
        wl = [at(f"w_low{s}", U, RING + (6 + s) * U, F32R) for s in range(3)]
        bank = [ctx.enter_context(nc.psum_tensor(f"bank{i}", [128, 512], F32)) for i in range(8)]

        c_ = lambda n: cst[:, CST[n][0]:CST[n][0] + CST[n][1]]
        ident, ones, bdones, II = c_("ident"), c_("ones"), c_("bdones"), c_("II")
        pc = lambda n, i=0: par[:, PAR[n] + i:PAR[n] + i + 1]
        negkk, omka, fng = dpar[:, 0:4], dpar[:, 4:8], dpar[:, 8:16]
        eps_rms, eps_lnx = dpar[:, 16:17], dpar[:, 17:18]

        sp = Space(nc, "n_", (PJ + KT * T, EX))
        sq = sp("squares", KT * CW)[:, :].rearrange("p (k t) -> p k t", k=KT)
        hn = sp("normed", KT * CW)[:, :].rearrange("p (k t) -> p k t", k=KT)
        std, rstd = sp("std", CW), sp("rstd", CW)
        sp = Space(nc, "f_", (PJ + KT * T, EX))
        mh = sp("mid_high", 2 * T, F32R)[:, :].rearrange("p (j t) -> p j t", j=2)
        ml = sp("mid_low", 2 * T, F32R)[:, :].rearrange("p (j t) -> p j t", j=2)
        sil = sp("silu", 3 * CW)[:, :].rearrange("p (c t) -> p c t", c=3)
        midf = sp("mid", 3 * CW)[:, :].rearrange("p (c t) -> p c t", c=3)
        sp = Space(nc, "s_", (EX, FIXED))
        raw9 = sp("raw_last", 15 * 9)[:, :].rearrange("p (k t) -> p k t", k=15)
        shd = sp("shift_in", 15 * 8)[:, :].rearrange("p (k t) -> p k t", k=15)
        edge = sp("edge", 15 * 8)[:, :].rearrange("p (k t) -> p k t", k=15)
        dif = sp("diff", T)
        lo_h, lo_l = (HH, HH + 4 * T), (HL, HL + 4 * T)
        sp = Space(nc, "a_", lo_h, lo_l, (EX + 384, FIXED), (RING, TOTAL))
        cos, sin = sp("cos", T), sp("sin", T)
        amask = sp("amask", 2 * 256)
        vp = [sp(f"v_padded{e}", 2 * 192)[:, :].rearrange("p (g d) -> p g d", g=2) for e in range(2)]
        kd = sp("k_twice", 2 * (WIN + T))[:, :].rearrange("p (g t) -> p g t", g=2)
        bdq = sp("q_spread", 4 * 256)[:, :].rearrange("p (k t) -> p k t", k=4)
        sm = [v[:, :].rearrange("p (h t) -> p h t", h=8) for v in (sp("scores", 8 * 256), at("a_scores_odd", 8 * 256, HH))]
        stat = sp("stats", 128)
        mats = sp("rope_mats", 5 * 128)
        sel = sp("select", 4 * 128)
        pT = sp("probs_t", 16 * 128)[:, :].rearrange("p (h t) -> p h t", h=16)
        vblk = sp("v_block", 128)
        rt = sp("rope_tmp", 3 * CW)[:, :].rearrange("p (c t) -> p c t", c=3)
        kro = sp("k_tail", 136)
        Kw = sp("k_window", 8 * 128)[:, :].rearrange("p (b t) -> p b t", b=8)
        Vw = sp("v_window", 8 * 128)[:, :].rearrange("p (b t) -> p b t", b=8)
        VwT = sp("v_window_t", 8 * 128)[:, :].rearrange("p (b t) -> p b t", b=8)
        qz, pTd, ov = sp("q_dec", 64), sp("probs_dec_t", 64), sp("o_dec", 64)
        smd = sp("scores_dec", 1024)[:, :].rearrange("p (b t) -> p b t", b=8)
        rotm, dup, rdup = mats[:, 0:128], mats[:, 128:384], mats[:, 384:640]
        q_tiles = (PJ + 15 * T, PJ + 21 * T)
        nkk = at("neg_kk", 4 * T, HH)[:, :].rearrange("p (k t) -> p k t", k=4)
        yar = at("y_heads", 4 * T, HH)[:, :].rearrange("p (k t) -> p k t", k=4)
        bb = at("b_heads", 4 * T, HL)[:, :].rearrange("p (k t) -> p k t", k=4)
        sp = Space(nc, "w_", q_tiles)
        lw_t = sp("log_decay", 4 * NCH * 65)
        lw = lw_t[:, :].rearrange("p (k n t) -> p k n t", k=4, n=NCH)
        lw_flat = lw_t[:, :].rearrange("p (k m) -> p k m", k=4)
        lwd = sp("log_decay_dec", 32)[:, :].rearrange("p (k t) -> p k t", k=4)
        rest = tuple(sp.free[0])
        sp = Space(nc, "e_", (RING, TOTAL))
        wda = sp("w_decay_a", 1024)[:, :].rearrange("p (w n) -> p w n", w=2)
        smask = sp("scan_mask", NCH * 65)
        ksq = sp("k_squared", T)
        nrm = sp("k_norm", T)
        at_ = sp("a_term", T)
        tile12 = (PJ + 12 * T, PJ + 13 * T)
        sp = Space(nc, "c_", (RING, TOTAL), rest, (EX + 384, FIXED), tile12, (HL + 4 * T, HL + 8 * T))
        k4 = lambda name: sp(name, 512)[:, :].rearrange("p (k t) -> p k t", k=4)
        k2 = lambda name: sp(name, 256)[:, :].rearrange("p (k t) -> p k t", k=2)
        k2c = lambda name: sp(name, 128)[:, :].rearrange("p (k t) -> p k t", k=2)
        par_grp = lambda f, name: [[f(f"{name}{q}{g}") for g in range(2)] for q in range(2)]
        grp = lambda f, name: [f(f"{name}{g}") for g in range(2)]
        abd = [k4(f"A_spread{q}") for q in range(2)]
        arc = [sp(f"AR{q}", 512)[:, :].rearrange("p (k w t) -> p k w t", k=4, w=2) for q in range(2)]
        pend = [sp(f"P_end{q}", 4) for q in range(2)]
        bbd, kbd, vbd = k4("B_spread"), k4("K_spread"), k4("Vt_spread")
        bc = sp("B", 256)[:, :].rearrange("p (k t) -> p k t", k=4)
        nm = par_grp(k4, "N_Mak_spread")
        mr = par_grp(lambda n: sp(n, 256)[:, :].rearrange("p (k t) -> p k t", k=4), "M_r")
        vc, vts = par_grp(k2c, "V"), par_grp(k2, "V_spread")
        bks = par_grp(k4, "BK_spread")
        Tt = par_grp(k2, "Tt_spread")
        xb = grp(k2, "X_spread")
        nr = [grp(lambda n: sp(n, 512)[:, :].rearrange("p (m r t) -> p m r t", m=4, r=2), f"NR_{w}") for w in range(2)]
        la, lb = grp(k4, "NX_spread_a"), grp(k4, "NX_spread_b")
        sa0, sac, sas = grp(k2c, "SA0"), grp(k2c, "SA"), grp(k2, "SA_spread")
        Sc, Ss = grp(k2c, "S"), grp(k2, "S_spread")
        att_low = at("att_low_back", 4 * T, HL + 4 * T)[:, :].rearrange("p (k t) -> p k t", k=4)
        sp = Space(nc, "d_", (RING, TOTAL))
        SD = sp("states", 2048)[:, :].rearrange("p (k b i) -> p k b i", k=4, b=8)
        t1a, t2a, t3a = (sp(f"t{n}_a", 512)[:, :].rearrange("p (b i) -> p b i", b=8) for n in (1, 2, 3))
        wdec = sp("decay", 32)[:, :].rearrange("p (k t) -> p k t", k=4)
        wg = sp("w_gate_up", 1024)[:, :].rearrange("p (w n) -> p w n", w=2)
        odd = Space(nc, "d_", tuple(sp.free[0]))
        t1b, t2b, t3b = (odd(f"t{n}_b", 512)[:, :].rearrange("p (b i) -> p b i", b=8) for n in (1, 2, 3))
        t1, t2, t3 = (t1a, t1b), (t2a, t2b), (t3a, t3b)
        fyc, fbo = ([sp(f"fin_{n}{o}", CW) for o in range(4)] for n in ("centred", "bonus"))
        fsq, fsd = ([sp(f"fin_{n}{o}", CW) for o in range(2)] for n in ("squares", "root"))

        sem = lambda n: ctx.enter_context(nc.semaphore(n))
        tensor_steps, vector_steps, scalar_steps, pool_steps = (sem(n + "_steps") for n in ENGINES)
        x_in, const_in, par_in, shift_in, rope_in, window_in, lora_in, state_in, wg_in = (sem(n) for n in (
            "x_in", "const_in", "par_in", "shift_in", "rope_in", "window_in", "lora_in", "state_in", "wg_in"))
        x_back = [sem(f"x_back{k}") for k in range(KT)]
        spill, shift_out, k_out, window_out, state_out, sample_out, y_out = (sem(n) for n in (
            "spill", "shift_out", "k_out", "window_out", "state_out", "sample_out", "y_out"))
        pool_prep, scalar_prep, vector_prep = (sem(n) for n in ("pool_prep", "scalar_prep", "vector_prep"))
        tensor_inv, scalar_inv, vector_inv = (sem(n) for n in ("tensor_inv", "scalar_inv", "vector_inv"))
        tensor_att, scalar_att, vector_att = (sem(n) for n in ("tensor_scores", "scalar_scores", "vector_scores"))
        scalar_soft, vector_soft = sem("scalar_softmax"), sem("vector_softmax")
        tensor_val, scalar_val, vector_val = (sem(n) for n in ("tensor_values", "scalar_values", "vector_values"))
        tensor_state, scalar_state, vector_state = (sem(n) for n in ("tensor_state", "scalar_state", "vector_state"))
        att_out, att_back = sem("att_out"), sem("att_back")
        sync_idle, tensor_idle, vector_idle, scalar_idle, pool_idle = (sem(n + "_idle") for n in ("sync", *ENGINES))
        raw_in = [sem(f"w_raw_in{s}") for s in range(3)]
        w_high = sem("w_high_ready")
        w_low = sem("w_low_ready")

        PER_SLOT = (32, 32, 31)

        def slot(k):
            return (k + 2) % 3 if k < NIN else (k - NIN) % 3

        def loads(l, k, i=0, per=0):
            base = k // 3 if k < NIN else NIN // 3 + (k - NIN) // 3
            return (l * PER_SLOT[slot(k)] + base + 1 + i * (per // 3)) * 16

        def after(k):
            return (1, k - UL) if k >= UL else (0, k)

        def at_chunk(own, name, l, c):
            return chunk_at(steps, own, name, l, c)

        def at_block(own, name, l, n):
            return chunk_at(steps, own, name, l, n, NBLK)

        block = ctx.enter_context(nc.Block())
        cs = lambda c: slice(c * CW, (c + 1) * CW)

        @block.sync
        def _(eng):
            e = Count(steps, "x_in")

            def fill_dma(l, k, i=0, per=0, wait=True):
                dl, kk = after(k)
                g = (l + dl) * UL + kk + i * per
                if wait:
                    eng.wait_ge(w_low, g - 3 + 1)
                eng.dma_start(raw[slot(kk)][:, :], d["wts"][bass.ds(g, 1)].rearrange("a p n -> p (a n)")
                              ).then_inc(raw_in[slot(kk)], 16)

            eng.dma_start(x[:, :, :], d["x"].rearrange("p (k t) -> p k t", k=KT)).then_inc(x_in, e.load("x_in", "x_in"))
            eng.dma_start(cst[:, :], d["cst"]).then_inc(const_in, e.load("const_in", "const_in"))
            eng.dma_start(fng, d["fin"]).then_inc(const_in, e.load("const_in", "fin_in"))
            for k in range(3):
                fill_dma(0, k, wait=False)
            for k in range(3, 6):
                fill_dma(0, k)
            with eng.Fori(0, L) as l, e.rounds("layer", L, l):
                row = lambda n: d[n][bass.ds(l, 1)].rearrange("a p n -> p (a n)")
                eng.wait_ge(vector_steps, e.at("ff_add_last", back=1))
                eng.wait_ge(x_in, e.at("x_in"))
                eng.dma_start(par[:, :], row("par")).then_inc(par_in, e.load("par_in", "par_in"))
                eng.dma_start(d["x_keep"].rearrange("p (k t) -> p k t", k=KT), x[:, :, :]).then_inc(spill, e.load("spill", "spill"))
                eng.wait_ge(vector_steps, e.at("edge_put", back=1))
                eng.dma_start(shd, row("shift").rearrange("p (k t) -> p k t", k=15)).then_inc(shift_in, e.load("shift_in", "shift_in"))
                with eng.Fori(0, 5) as i, e.rounds("wa", 5, i):
                    for j in range(3):
                        fill_dma(l, 6 + j, i, 3)
                eng.wait_ge(tensor_steps, e.at("win_last"))
                eng.dma_start(cos[:, :], d["rope"][:, 0:T]).then_inc(rope_in, e.load("rope_in"))
                eng.dma_start(sin[:, :], d["rope"][:, T:2 * T]).then_inc(rope_in, e.load("rope_in"))
                eng.dma_start(mats[:, :], d["mats"][:, 0:640]).then_inc(rope_in, e.load("rope_in"))
                eng.dma_start(sel[:, :], d["mats"][:, 640:1152]).then_inc(rope_in, e.load("rope_in"))
                eng.dma_start(amask[:, :], d["amask"]).then_inc(rope_in, e.load("rope_in", "rope_in"))
                eng.dma_start(Kw[:, :, 0:127], row("kwin").rearrange("p (b t) -> p b t", b=8)).then_inc(window_in, e.load("window_in"))
                eng.dma_start(Vw[:, :, 0:127], row("vwin").rearrange("p (b t) -> p b t", b=8)).then_inc(window_in, e.load("window_in", "window_in"))
                eng.wait_ge(scalar_steps, e.at("raw9_last"))
                eng.dma_start(row("o_shift").rearrange("p (k t) -> p k t", k=15), raw9).then_inc(shift_out, e.load("shift_out", "shift_out"))
                eng.wait_ge(scalar_steps, e.at("k_tail1"))
                eng.dma_start(row("o_pk"), kro[:, 0:128]).then_inc(k_out, e.load("k_out"))
                eng.dma_start(row("o_pv"), proj[:, 20, NP_ - WIN:NP_]).then_inc(k_out, e.load("k_out", "k_out"))
                eng.wait_ge(scalar_steps, e.at("v_new"))
                eng.dma_start(row("o_sk").rearrange("p (b t) -> p b t", b=8), Kw).then_inc(window_out, e.load("window_out"))
                eng.dma_start(row("o_sv").rearrange("p (b t) -> p b t", b=8), Vw).then_inc(window_out, e.load("window_out", "window_out"))
                eng.wait_ge(vector_steps, e.at("att_low_dec"))
                eng.wait_ge(window_out, e.at("window_out"))
                eng.wait_ge(k_out, e.at("k_out"))
                eng.dma_start(wda, row("wda").rearrange("p (w n) -> p w n", w=2)).then_inc(lora_in, e.load("lora_in"))
                eng.dma_start(smask[:, :], d["smask"]).then_inc(lora_in, e.load("lora_in", "lora_in"))
                eng.dma_start(d["att_keep"].rearrange("p (k t) -> p k t", k=4), hl[:, 4:8, :].bitcast(F32)).then_inc(att_out, e.load("att_out", "att_out"))
                eng.wait_ge(vector_state, at_chunk("vector_state", "S_new1", l, NCH - 1))
                eng.sem_inc(sync_idle, 1)
                for g in range(2):
                    eng.dma_start(row("o_ps").rearrange("p (k t) -> p k t", k=4)[:, 2 * g:2 * g + 2, :], Sc[g]).then_inc(state_out, e.load("state_out", f"state_out{g}"))
                eng.wait_ge(scalar_state, at_chunk("scalar_state", "y1", l, NCH - 1))
                eng.wait_ge(state_out, e.at("state_out1"))
                eng.dma_start(SD, row("states").rearrange("p (k b i) -> p k b i", k=4, b=8)).then_inc(state_in, e.load("state_in", "state_in"))
                eng.dma_start(wg, row("wg").rearrange("p (w n) -> p w n", w=2)).then_inc(wg_in, e.load("wg_in", "wg_in"))
                eng.wait_ge(att_out, e.at("att_out"))
                eng.dma_start(att_low, d["att_keep"].rearrange("p (k t) -> p k t", k=4)).then_inc(att_back, e.load("att_back", "att_back"))
                eng.wait_ge(vector_steps, e.at("dec_y"))
                eng.dma_start(row("o_ss").rearrange("p (k b i) -> p k b i", k=4, b=8), SD).then_inc(sample_out, e.load("sample_out", "sample_out"))
                eng.wait_ge(sample_out, e.at("sample_out"))
                for k in range(NIN, NIN + 3):
                    eng.sem_inc(sync_idle, 1)
                    fill_dma(l, k, wait=False)
                eng.wait_ge(pool_steps, e.at("fin_low3_all"))
                eng.wait_ge(shift_out, e.at("shift_out"))
                eng.wait_ge(spill, e.at("spill"))
                for k in range(KT):
                    eng.dma_start(x[:, k, :], d["x_keep"][:, k * T:(k + 1) * T]).then_inc(x_back[k], e.load(f"x_back{k}", f"x_back{k}"))
                for k in range(NIN + 3, NIN + KT + 6):
                    fill_dma(l, k)
                with eng.Fori(0, NFF // 2) as i, e.rounds("ff", NFF // 2, i):
                    for j in range(6):
                        fill_dma(l, NIN + KT + 6 + j, i, 6)
            for c in range(NC3):
                eng.wait_ge(vector_steps, e.at(f"nf{c}_n{KT - 1}"))
                eng.dma_start(d["o_y"].rearrange("p (k t) -> p k t", k=KT)[:, :, cs(c)], x[:, :, cs(c)]
                              ).then_inc(y_out, e.load("y_out", "y_out" if c == NC3 - 1 else None))
            eng.wait_ge(y_out, e.at("y_out"))
            eng.wait_ge(state_out, e.at("state_out1"))
            eng.wait_ge(sample_out, e.at("sample_out"))
            eng.wait_ge(shift_out, e.at("shift_out"))
            eng.wait_ge(k_out, e.at("k_out"))
            eng.wait_ge(window_out, e.at("window_out"))
            for s in range(3):
                eng.wait_ge(raw_in[s], (L * PER_SLOT[s] + 2) * 16)

        @block.gpsimd
        def _(eng):
            e = Count(steps, "pool")
            prep = Chunk(steps, "pool_prep")
            eng.sem_inc(pool_steps, CREDIT)
            eng.sem_inc(pool_prep, CHUNK_CREDIT)

            def fill_low(l, k, i=0, per=0):
                dl, kk = after(k)
                g = (l + dl) * UL + kk + i * per
                eng.wait_ge(w_high, g + 1)
                eng.tensor_tensor(wl[slot(kk)][:, :], raw[slot(kk)][:, :], wh[slot(kk)][:, :].bitcast(F32),
                                  ALU.subtract).then_inc(w_low, 1)

            for k in range(3):
                fill_low(0, k)
            with eng.Fori(0, L) as l, e.rounds("layer", L, l):
                with eng.Fori(0, 5) as i, e.rounds("wa", 5, i):
                    for j in range(3):
                        fill_low(l, 3 + j, i, 3)
                for k in range(18, NIN):
                    fill_low(l, k)
                eng.wait_ge(tensor_steps, e.at("win_last"))
                eng.sem_inc(pool_idle, 1)
                for v in (kd[:, :, 0:WIN], vp[0], vp[1], bdq):
                    eng.memset(v, 0.0).then_inc(pool_steps, e.step())
                eng.memset(stat[:, :], 0.0).then_inc(pool_steps, e.step("att_zero"))
                eng.wait_ge(scalar_steps, e.at("att_high_dec"))
                eng.wait_ge(vector_steps, e.at("att_low_dec"))
                eng.wait_ge(k_out, e.at("k_out"))
                eng.sem_inc(pool_idle, 1)
                eng.memset(lw[:, :, :, 0], 0.0).then_inc(pool_steps, e.step("lw_zero"))
                eng.wait_ge(att_out, e.at("att_out"))
                eng.wait_ge(window_out, e.at("window_out"))
                eng.wait_ge(tensor_steps, e.at("lora3"))
                eng.sem_inc(pool_idle, 1)
                for v in (*Sc, *la, *Tt[0], *Tt[1], *sas, *Ss):
                    eng.memset(v, 0.0).then_inc(pool_steps, e.step())
                eng.wait_ge(vector_steps, e.at("elem_last"))
                eng.sem_inc(pool_idle, 1)
                for v in (*abd, bbd):
                    eng.memset(v, 0.0).then_inc(pool_steps, e.step())
                eng.memset(vbd, 0.0).then_inc(pool_steps, e.step("chunk_zero"))

                def chunk(c, q, P):
                    if P:
                        prep.begin()
                        tok = bass.ds((c + 2) * CH, CH)
                        eng.wait_ge(scalar_prep, at_chunk("scalar_prep", "exp_b", l, c + 2))
                        eng.sem_inc(pool_idle, 1)
                        eng.tensor_tensor(bc, bb[:, :, tok], bc, ALU.mult).then_inc(pool_prep, prep.step("bc"))
                        eng.wait_ge(scalar_prep, at_chunk("scalar_prep", "exp_ar", l, c + 2))
                        eng.sem_inc(pool_idle, 1)
                        eng.tensor_tensor(arc[q][:, :, 0, :], nkk[:, :, tok], arc[q][:, :, 0, :], ALU.mult).then_inc(pool_prep, prep.step())
                        eng.tensor_tensor(arc[q][:, :, 1, :], proj[:, 0:4, tok], arc[q][:, :, 1, :], ALU.mult).then_inc(pool_prep, prep.step("ar"))

                chunk(-2, 0, True)
                chunk(-1, 1, True)
                with eng.Fori(0, NCH // 2 - 1) as i, e.rounds("rc", NCH // 2 - 1, i):
                    for q in range(2):
                        chunk(i * 2 + q, q, True)
                eng.wait_ge(att_back, e.at("att_back"))
                eng.sem_inc(pool_idle, 1)
                eng.tensor_copy(hl[:, 4:8, :], att_low).then_inc(pool_steps, e.step("att_low_back"))
                with eng.Fori(0, NC3) as c, e.rounds("fin", NC3, c):
                    seg = bass.ds(c * CW, CW)
                    for o in range(4):
                        eng.wait_ge(scalar_steps, e.at(f"fin_high{o}"))
                        eng.sem_inc(pool_idle, 1)
                        eng.tensor_tensor(hl[:, o, seg], fyc[o][:, :], hh[:, o, seg].bitcast(F32), ALU.subtract).then_inc(pool_steps, e.step(f"fin_low{o}"))
                    e.also("fin_low3_all")
                for k in range(NIN, NIN + KT + 3):
                    fill_low(l, k)
                with eng.Fori(0, NFF // 2) as i, e.rounds("ff", NFF // 2, i):
                    for j in range(6):
                        fill_low(l, NIN + KT + 3 + j, i, 6)

        @block.scalar
        def _(eng):
            e = Count(steps, "scalar")
            prep, inv, state = Chunk(steps, "scalar_prep"), Chunk(steps, "scalar_inv"), Chunk(steps, "scalar_state")
            eng.sem_inc(scalar_steps, CREDIT)
            eng.sem_inc(scalar_prep, CHUNK_CREDIT)
            eng.sem_inc(scalar_inv, CHUNK_CREDIT)
            eng.sem_inc(scalar_state, CHUNK_CREDIT)
            eng.sem_inc(scalar_att, CHUNK_CREDIT)
            att = Chunk(steps, "scalar_att")
            eng.sem_inc(scalar_val, CHUNK_CREDIT)
            val = Chunk(steps, "scalar_val")
            eng.sem_inc(scalar_soft, CHUNK_CREDIT)
            soft = Chunk(steps, "scalar_soft")
            a = eng.activation

            def fill_high(l, k, i=0, per=0, used=None):
                dl, kk = after(k)
                g = (l + dl) * UL + kk + i * per
                eng.wait_ge(raw_in[slot(kk)], loads(l + dl, kk, i, per))
                if used:
                    eng.wait_ge(tensor_steps, e.at(used))
                eng.copy(wh[slot(kk)][:, :], raw[slot(kk)][:, :]).then_inc(w_high, 1)

            def norm(p, last, ready):
                def squares(c):
                    ready(c)
                    if c:
                        eng.wait_ge(tensor_steps, e.at(f"{p}{c - 1}_ss"))
                    for k in range(KT):
                        a(sq[:, k, :], x[:, k, cs(c)], ACT.Square).then_inc(scalar_steps, e.step(f"{p}{c}_sq{k}"))

                squares(0)
                for c in range(NC3):
                    eng.wait_ge(tensor_steps, e.at(f"{p}{c}_ss"))
                    if c:
                        eng.wait_ge(vector_steps, e.at(f"{p}{c - 1}_recip"))
                    a(std[:, :], bank[5][:, 0:CW], ACT.Sqrt, bias=eps_rms, scale=1.0 / DM).then_inc(scalar_steps, e.step(f"{p}{c}_std"))
                    if c < NC3 - 1:
                        squares(c + 1)
                    if not last:
                        for k in range(KT):
                            eng.wait_ge(vector_steps, e.at(f"{p}{c}_n{k}"))
                            eng.copy(hh[:, k, cs(c)], hn[:, k, :]).then_inc(scalar_steps, e.step(f"{p}{c}_high{k}"))

            for k in range(3):
                fill_high(0, k)
            eng.wait_ge(x_in, e.at("x_in"))
            eng.wait_ge(vector_steps, e.at("eps"))
            with eng.Fori(0, L) as l, e.rounds("layer", L, l):
                norm("n1", False, lambda c: eng.wait_ge(vector_steps, e.at(f"ff_add{(c + 1) * KT - 1}", back=1)))
                eng.wait_ge(spill, e.at("spill"))
                eng.wait_ge(vector_steps, e.at("n12_low7"))
                with eng.Fori(0, 5) as i, e.rounds("wa", 5, i):
                    for j in range(3):
                        for c in range(NC3):
                            eng.wait_ge(tensor_steps, e.at(f"wa_mm{j}{c}"))
                            eng.copy(proj[:, bass.ds(3 * i + j, 1), cs(c)].rearrange("p a t -> p (a t)"),
                                            bank[c][:, 0:CW]).then_inc(scalar_steps, e.step(f"wa_ev{j}{c}"))
                        eng.wait_ge(scalar_steps, e.mine())
                        eng.copy(raw9[:, bass.ds(3 * i + j, 1), :].rearrange("p a t -> p (a t)"),
                                        proj[:, bass.ds(3 * i + j, 1), NP_ - 1:T].rearrange("p a t -> p (a t)")).then_inc(scalar_steps, e.step("raw9_last" if j == 2 else f"raw9_{j}"))
                        fill_high(l, 3 + j, i, 3, f"wa_mm{j}2")
                for k in range(15, NIN):
                    for c in range(NC3):
                        eng.wait_ge(tensor_steps, e.at(f"wb_mm{k}{c}"))
                        eng.copy(proj[:, k, cs(c)], bank[c][:, 0:CW]).then_inc(scalar_steps, e.step(f"wb_ev{k}{c}"))
                    if k + 3 < NIN:
                        fill_high(l, k + 3, used=f"wb_mm{k}2")

                for g in range(2):
                    eng.wait_ge(vector_steps, e.at("kd_last"))
                    eng.copy(kro[64 * g:64 * g + 64, :], kd[64 * g:64 * g + 64, g, NP_:NP_ + 136]).then_inc(scalar_steps, e.step(f"k_tail{g}"))
                eng.wait_ge(scalar_steps, e.mine())
                eng.wait_ge(window_in, e.at("window_in"))
                eng.copy(Kw[:, :, 127], kro[:, 128:136]).then_inc(scalar_steps, e.step("k_new"))
                eng.copy(Vw[:, :, 127], proj[:, 20, NP_:T]).then_inc(scalar_steps, e.step("v_new"))
                eng.wait_ge(pool_steps, e.at("att_zero"))
                eng.wait_ge(vector_steps, e.at("rq_last"))

                def blocks(n, q, S, M, V):
                    o = 1 - q
                    st = lambda w, h, k=8: stat[:, 64 * q + 8 * w + h:64 * q + 8 * w + h + k]
                    if S:
                        att.begin()
                        blk = bass.ds((n + 1) * WIN, WIN)
                        eng.wait_ge(tensor_att, at_block("tensor_att", "s3", l, n))
                        for h in range(2):
                            rows = slice(64 * h, 64 * h + 64)
                            eng.copy(bdq[rows, :, 128 * h:128 * h + 128], proj[rows, 15:19, blk]).then_inc(scalar_att, att.step(f"bdq{h}"))
                    if V:
                        val.begin()
                        eng.wait_ge(tensor_val, at_block("tensor_val", "vt", l, n - 1))
                        eng.wait_ge(tensor_val, at_block("tensor_val", "pv", l, n - 2))
                        eng.copy(vp[o][:, :, 64:128], bank[7][:, 0:128].rearrange("p (g t) -> p g t", g=2)).then_inc(scalar_val, val.step("vp"))
                        eng.wait_ge(tensor_val, at_block("tensor_val", "pt1", l, n - 1))
                        eng.copy(pT[:, 4:8, :], bank[5][:, :].rearrange("p (h t) -> p h t", h=4)).then_inc(scalar_val, val.step("ptc1"))
                    if M:
                        soft.begin()
                        eng.wait_ge(vector_att, at_block("vector_att", "negmax", l, n))
                        for h in range(4):
                            a(sm[q][:, h, :], sm[q][:, h, :], ACT.Exp, bias=st(2, h, 1), accum_out=st(3, h, 1)).then_inc(scalar_soft, soft.step(f"exp{h}"))
                    if V:
                        eng.wait_ge(tensor_val, at_block("tensor_val", "pt3", l, n - 1))
                        eng.copy(pT[:, 12:16, :], bank[5][:, :].rearrange("p (h t) -> p h t", h=4)).then_inc(scalar_val, val.step("ptc3"))
                    if M:
                        for h in range(4, 8):
                            a(sm[q][:, h, :], sm[q][:, h, :], ACT.Exp, bias=st(2, h, 1), accum_out=st(3, h, 1)).then_inc(scalar_soft, soft.step(f"exp{h}"))
                        a(st(5, 0), st(4, 0), ACT.Exp).then_inc(scalar_soft, soft.step("sinkexp"))
                        if V:
                            eng.wait_ge(tensor_val, at_block("tensor_val", "vt", l, n - 1))
                        eng.copy(vblk[:, :], proj[:, 20, bass.ds(n * WIN, WIN)]).then_inc(scalar_soft, soft.step("vblk"))
                    if V:
                        eng.wait_ge(tensor_val, at_block("tensor_val", "pv", l, n - 1))
                        eng.copy(hh[:, 4:8, bass.ds((n - 1) * WIN, WIN)], bank[6][:, :].rearrange("p (k t) -> p k t", k=4)
                                 ).then_inc(scalar_val, val.step("high"))
                    if M:
                        eng.wait_ge(vector_soft, at_block("vector_soft", "recip", l, n))
                        for h in range(5, 8):
                            a(sm[q][:, h, :], sm[q][:, h, :], ACT.Copy, scale=st(6, h, 1)).then_inc(scalar_soft, soft.step("p_last" if h == 7 else None))

                blocks(-1, 1, S=True, M=False, V=False)
                blocks(0, 0, S=True, M=True, V=False)
                with eng.Fori(0, NBLK // 2 - 1) as i, e.rounds("ab", NBLK // 2 - 1, i):
                    for q in range(2):
                        blocks(i * 2 + (1 + q), 1 - q, S=True, M=True, V=True)
                blocks(NBLK - 1, 1, S=False, M=True, V=True)
                blocks(NBLK, 0, S=False, M=False, V=True)
                eng.wait_ge(tensor_steps, e.at("d_qz"))
                eng.copy(qz[:, :], bank[1][:, 0:64]).then_inc(scalar_steps, e.step("d_qz_c"))
                eng.wait_ge(vector_steps, e.at("d_sub"))
                a(smd[0:8, :, :], smd[0:8, :, :], ACT.Exp).then_inc(scalar_steps, e.step("d_exp"))
                a(stat[0:8, 8:16], stat[0:8, 0:8], ACT.Exp, bias=par[0:8, PAR["sinkcol"]:PAR["sinkcol"] + 1],
                         scale=-1.0).then_inc(scalar_steps, e.step("d_sinkexp"))
                for q in range(2):
                    eng.wait_ge(tensor_steps, e.at(f"d_vt{q}"))
                    eng.copy(VwT[:, 4 * q:4 * q + 4, :], bank[5 + q][:, :].rearrange("p (b t) -> p b t", b=4)).then_inc(scalar_steps, e.step(f"d_vtc{q}"))
                eng.wait_ge(tensor_steps, e.at("d_pt"))
                eng.copy(pTd[:, :], bank[4][:, 0:64]).then_inc(scalar_steps, e.step("d_ptc"))
                eng.wait_ge(tensor_steps, e.at("d_pv"))
                eng.copy(ov[:, :], bank[7][:, 0:64]).then_inc(scalar_steps, e.step("d_ov"))
                eng.wait_ge(tensor_steps, e.at("d_place"))
                eng.copy(hh[:, 4:8, NP_:T], bank[0][:, 0:32].rearrange("p (k t) -> p k t", k=4)).then_inc(scalar_steps, e.step("att_high_dec"))

                eng.wait_ge(vector_steps, e.at("edge_put"))
                a(proj[0:64, 12, :], proj[0:64, 12, :], ACT.Tanh).then_inc(scalar_steps, e.step("tanh"))
                eng.wait_ge(pool_steps, e.at("lw_zero"))
                eng.wait_ge(vector_steps, e.at("att_low_dec"))
                eng.wait_ge(k_out, e.at("k_out"))
                eng.wait_ge(window_out, e.at("window_out"))
                a(ksq[:, :], proj[:, 4, :], ACT.Square, scale=pc("k_k", 0)).then_inc(scalar_steps, e.step("ksq0"))
                for o in range(4):
                    eng.wait_ge(tensor_steps, e.at(f"kk_mm{o}"))
                    if o:
                        eng.wait_ge(vector_steps, e.at(f"kk_recip{o - 1}"))
                    for c in range(NC3):
                        a(nrm[:, cs(c)], bank[5 + c][:, 0:CW], ACT.Sqrt).then_inc(scalar_steps, e.step(f"knorm{o}{c}"))
                    if o < 3:
                        a(ksq[:, :], proj[:, 5 + o, :], ACT.Square, scale=pc("k_k", o + 1)).then_inc(scalar_steps, e.step(f"ksq{o + 1}"))
                    for q in range(2):
                        eng.wait_ge(tensor_steps, e.at(f"lora{o}"))
                        a(lw[:, o, 8 * q:8 * q + 8, 1:65], bank[q][:, :].rearrange("p (n t) -> p n t", n=8),
                                 ACT.Sigmoid, bias=pc("w0", o)).then_inc(scalar_steps, e.step(f"lw{o}{q}"))
                        a(bb[:, o, 512 * q:512 * q + 512], bank[3 + q][:, :], ACT.Sigmoid, bias=pc("a0", o)).then_inc(scalar_steps, e.step(f"a{o}{q}"))
                    a(lwd[:, o, :], bank[2][:, 0:8], ACT.Sigmoid, bias=pc("w0", o)).then_inc(scalar_steps, e.step())
                    a(bb[:, o, NP_:T], bank[2][:, 8:16], ACT.Sigmoid, bias=pc("a0", o)).then_inc(scalar_steps, e.step(f"lora_ev{o}"))
                a(proj[:, 13:15, :], proj[:, 13:15, :], ACT.Sigmoid).then_inc(scalar_steps, e.step("sig_gate"))

                eng.wait_ge(vector_steps, e.at("elem_last"))
                eng.wait_ge(pool_steps, e.at("chunk_zero"))

                def chunk(c, q, B, A, P):
                    o = 1 - q
                    ps = lambda b, lo, hi, k: bank[b][:, lo:hi].rearrange("p (k t) -> p k t", k=k)
                    low, lc = slice(64, 128), slice(64, 128)
                    lwi = lambda rows, lo: lw[rows, :, bass.ds(c + 2, 1), lo:lo + 64].rearrange("p k a t -> p k (a t)")
                    allp = slice(0, 128)
                    if B:
                        state.begin()
                        for g in range(2):
                            eng.wait_ge(tensor_state, at_chunk("tensor_state", f"s1_{g}", l, c))
                            eng.copy(sa0[g], ps(4 * g + 3, 0, 128, 2)).then_inc(scalar_state, state.step(f"sa0_{g}"))
                    if A:
                        inv.begin()
                        for g in range(2):
                            eng.wait_ge(tensor_inv, at_chunk("tensor_inv", f"g1_{g}", l, c + 1))
                            vt = ps(4 * g + 2, 0, 256, 2)
                            for h in range(2):
                                rows = slice(64 * h, 64 * h + 64)
                                eng.copy(vc[o][g][rows], vt[rows, :, rows]).then_inc(scalar_inv, inv.step())
                            eng.copy(vts[o][g], vt).then_inc(scalar_inv, inv.step(f"vts_{g}"))
                    if B:
                        for g in range(2):
                            eng.wait_ge(tensor_state, at_chunk("tensor_state", f"s2_{g}", l, c))
                            eng.copy(sac[g][low], ps(4 * g + 3, 128, 256, 2)[low]).then_inc(scalar_state, state.step())
                            eng.copy(sas[g][low, :, lc], ps(4 * g + 3, 128, 256, 2)[low]).then_inc(scalar_state, state.step(f"sa_{g}"))
                    if A:
                        for g in range(2):
                            eng.wait_ge(tensor_inv, at_chunk("tensor_inv", f"bkt_{g}", l, c + 1))
                            eng.copy(bks[o][g], ps(4 * g + 2, 0, 512, 4)).then_inc(scalar_inv, inv.step(f"bks_{g}"))
                        for g in range(2):
                            eng.wait_ge(tensor_inv, at_chunk("tensor_inv", f"l2_{g}", l, c + 1))
                            eng.copy(nr[1][g][low, :, 0], ps(4 * g + 1, 128, 384, 4)[low]).then_inc(scalar_inv, inv.step())
                            eng.copy(la[g][low, :, lc], ps(4 * g + 1, 128, 384, 4)[low]).then_inc(scalar_inv, inv.step(f"l2e_{g}"))
                    if A:
                        for g in range(2):
                            v = bank[4 * g][:, :].rearrange("p (m r t) -> p m r t", m=4, r=2)
                            eng.wait_ge(tensor_inv, at_chunk("tensor_inv", f"l4_{g}", l, c + 1))
                            eng.copy(nr[0][g][low, :, 0], v[low, :, 0]).then_inc(scalar_inv, inv.step())
                            eng.copy(lb[g][low, :, lc], v[low, :, 0]).then_inc(scalar_inv, inv.step(f"l4e_{g}"))
                    if P:
                        prep.begin()
                        eng.wait_ge(tensor_inv, at_chunk("tensor_inv", "bkt_1", l, c + 1))
                        eng.sem_inc(scalar_idle, 1)
                        a(bc, lwi(allp, 1), ACT.Exp, scale=CDEC).then_inc(scalar_prep, prep.step("exp_b"))
                    if A:
                        for g in range(2):
                            v = bank[4 * g + 1][:, :].rearrange("p (m r t) -> p m r t", m=4, r=2)
                            eng.wait_ge(tensor_inv, at_chunk("tensor_inv", f"l8_{g}", l, c + 1))
                            eng.copy(la[g][low, :, lc], v[low, :, 0]).then_inc(scalar_inv, inv.step(f"l8e_{g}"))
                    if P:
                        for h in range(2):
                            rows = slice(64 * h, 64 * h + 64)
                            a(bbd[rows, :, rows], lwi(rows, 1), ACT.Exp, scale=CDEC).then_inc(scalar_prep, prep.step(f"exp_bbd{h}"))
                    if A:
                        for g in range(2):
                            eng.wait_ge(vector_inv, at_chunk("vector_inv", f"r8c_{g}", l, c + 1))
                            eng.copy(lb[g][low, :, lc], nr[0][g][low, :, 1]).then_inc(scalar_inv, inv.step(f"r8e_{g}"))
                    if B:
                        for g in range(2):
                            eng.wait_ge(tensor_state, at_chunk("tensor_state", f"y_{g}", l, c))
                            eng.copy(yar[:, 2 * g:2 * g + 2, bass.ds(c * CH, CH)], ps(4 * g + 3, 384, 512, 2)
                                     ).then_inc(scalar_state, state.step(f"y{g}"))
                    if P:
                        eng.wait_ge(tensor_state, at_chunk("tensor_state", "y_1", l, c))
                        eng.sem_inc(scalar_idle, 1)
                        a(arc[q][:, :, 0, :], lwi(allp, 0), ACT.Exp, scale=-CDEC).then_inc(scalar_prep, prep.step())
                        a(arc[q][:, :, 1, :], lwi(allp, 1), ACT.Exp, scale=-CDEC).then_inc(scalar_prep, prep.step("exp_ar"))
                    if P:
                        eng.wait_ge(vector_state, at_chunk("vector_state", "S_dec1", l, c))
                        eng.sem_inc(scalar_idle, 1)
                        a(pend[q][:, :].unsqueeze(2), lw[:, :, bass.ds(c + 2, 1), 64:65].rearrange("p k a t -> p k (a t)"), ACT.Exp, scale=-CDEC
                          ).then_inc(scalar_prep, prep.step("exp_end"))
                        for h in range(2):
                            rows = slice(64 * h, 64 * h + 64)
                            a(abd[q][rows, :, rows], lwi(rows, 0), ACT.Exp, scale=-CDEC).then_inc(scalar_prep, prep.step(f"exp_abd{h}"))
                    if A:
                        for g in range(2):
                            eng.wait_ge(vector_inv, at_chunk("vector_inv", f"m2c_{g}", l, c + 1))
                            eng.copy(la[g][low, 0:2, lc], nr[1][g][low, 2:4, 1]).then_inc(scalar_inv, inv.step(f"m2e_{g}"))
                    if P:
                        for h in range(2):
                            rows = slice(64 * h, 64 * h + 64)
                            eng.copy(vbd[rows, :, rows], proj[rows, 8:12, bass.ds((c + 2) * CH, CH)]).then_inc(scalar_prep, prep.step(f"vbd{h}"))
                    if A:
                        for g in range(2):
                            eng.wait_ge(vector_inv, at_chunk("vector_inv", f"m4c_{g}", l, c + 1))
                            eng.copy(Tt[o][g][low, :, lc], nr[0][g][low, 0:2, 1]).then_inc(scalar_inv, inv.step(f"m4e_{g}"))

                chunk(-2, 0, B=False, A=False, P=True)
                chunk(-1, 1, B=False, A=True, P=True)
                with eng.Fori(0, NCH // 2 - 1) as i, e.rounds("rc", NCH // 2 - 1, i):
                    for q in range(2):
                        chunk(i * 2 + q, q, B=True, A=True, P=True)
                chunk(NCH - 2, 0, B=True, A=True, P=False)
                chunk(NCH - 1, 1, B=True, A=False, P=False)

                eng.wait_ge(vector_state, at_chunk("vector_state", "S_new1", l, NCH - 1))
                eng.wait_ge(tensor_state, at_chunk("tensor_state", "y_1", l, NCH - 1))
                eng.wait_ge(state_out, e.at("state_out1"))
                a(wdec, lwd, ACT.Exp, scale=-CDEC).then_inc(scalar_steps, e.step("wdec"))
                with eng.Fori(0, NC3) as c, e.rounds("fin", NC3, c):
                    seg = bass.ds(c * CW, CW)

                    def root(o):
                        eng.wait_ge(tensor_steps, e.at(f"fin_var{o}"))
                        eng.wait_ge(vector_steps, e.at(f"fin_lg{(o + 2) % 4}", back=int(o < 2)))
                        a(fsd[o % 2][:, :], bank[o][:, 0:CW], ACT.Sqrt, bias=eps_lnx, scale=1.0 / HD).then_inc(scalar_steps, e.step(f"fin_sd{o}"))

                    for o in range(4):
                        eng.wait_ge(vector_steps, e.at(f"fin_yc{o}"))
                        if o < 2:
                            eng.wait_ge(tensor_steps, e.at(f"fin_var{o + 2}", back=1))
                        a(fsq[o % 2][:, :], fyc[o][:, :], ACT.Square).then_inc(scalar_steps, e.step(f"fin_sq{o}"))
                        if o:
                            root(o - 1)
                    root(3)
                    for o in range(4):
                        eng.wait_ge(vector_steps, e.at(f"fin_out{o}"))
                        eng.copy(hh[:, o, seg], fyc[o][:, :]).then_inc(scalar_steps, e.step(f"fin_high{o}"))

                eng.wait_ge(pool_steps, e.at("fin_low3_all"))
                for k in range(NIN, NIN + 3):
                    fill_high(l, k)
                for k in range(NIN, NIN + KT):
                    fill_high(l, k + 3, used=f"wo_mm{k - NIN}2")
                norm("n2", False, lambda c: eng.wait_ge(vector_steps, e.at(f"wo_add{KT - 1}{c}")))
                eng.wait_ge(vector_steps, e.at("n22_low7"))
                with eng.Fori(0, NFF // 2) as i, e.rounds("ff", NFF // 2, i):
                    for j in range(2):
                        for c in range(NC3):
                            eng.wait_ge(tensor_steps, e.at(f"ff_g{j}{c}"))
                            if j:
                                eng.wait_ge(vector_steps, e.at(f"ff_mid{j - 1}{c}"))
                            else:
                                eng.wait_ge(vector_steps, e.at(f"ff_mid1{c}", back=1))
                            a(sil[:, c, :], bank[c][:, 0:CW], ACT.Silu).then_inc(scalar_steps, e.step(f"ff_sil{j}{c}"))
                        fill_high(l, NIN + KT + 3 + 2 * j, i, 6, f"ff_g{j}2")
                        for c in range(NC3):
                            eng.wait_ge(vector_steps, e.at(f"ff_mid{j}{c}"))
                            if j == 0 and c == 0:
                                eng.wait_ge(tensor_steps, e.at("ff_down_last", back=1))
                            eng.copy(mh[:, j, cs(c)], midf[:, c, :]).then_inc(scalar_steps, e.step(f"ff_high{j}{c}"))
                        fill_high(l, NIN + KT + 3 + 2 * j + 1, i, 6, f"ff_u{j}2")
                    for j in (4, 5):
                        fill_high(l, NIN + KT + 3 + j, i, 6, "ff_down_last")
            norm("nf", True, lambda c: eng.wait_ge(vector_steps, e.at(f"ff_add{(c + 1) * KT - 1}")))

        @block.vector
        def _(eng):
            e = Count(steps, "vector")
            prep, inv, state = Chunk(steps, "vector_prep"), Chunk(steps, "vector_inv"), Chunk(steps, "vector_state")
            eng.sem_inc(vector_steps, CREDIT)
            eng.sem_inc(vector_prep, CHUNK_CREDIT)
            eng.sem_inc(vector_inv, CHUNK_CREDIT)
            eng.sem_inc(vector_state, CHUNK_CREDIT)
            eng.sem_inc(vector_att, CHUNK_CREDIT)
            att = Chunk(steps, "vector_att")
            eng.sem_inc(vector_val, CHUNK_CREDIT)
            val = Chunk(steps, "vector_val")
            eng.sem_inc(vector_soft, CHUNK_CREDIT)
            soft = Chunk(steps, "vector_soft")
            tt, ts, stt = eng.tensor_tensor, eng.tensor_scalar, eng.scalar_tensor_tensor
            two = lambda v: v.rearrange("p k (a t) -> p k a t", a=2)
            wide = lambda v: bcast(v, 2, 2)
            mask2 = lambda m, k: bcast(m.rearrange("p (a t) -> p a t", a=2), 1, k)

            def norm(p, gain, last=False):
                for c in range(NC3):
                    eng.wait_ge(scalar_steps, e.at(f"{p}{c}_std"))
                    eng.wait_ge(vector_steps, e.mine())
                    eng.reciprocal(rstd[:, :], std[:, :]).then_inc(vector_steps, e.step(f"{p}{c}_recip"))
                    eng.wait_ge(vector_steps, e.mine())
                    for k in range(KT):
                        out = x[:, k, cs(c)] if last else hn[:, k, :]
                        stt(out, x[:, k, cs(c)], gain(k), rstd[:, :], ALU.mult, ALU.mult).then_inc(vector_steps, e.step(f"{p}{c}_n{k}"))
                    if not last:
                        for k in range(KT):
                            eng.wait_ge(scalar_steps, e.at(f"{p}{c}_high{k}"))
                            tt(hl[:, k, cs(c)], hn[:, k, :], hh[:, k, cs(c)].bitcast(F32), ALU.subtract).then_inc(vector_steps, e.step(f"{p}{c}_low{k}"))

            eng.memset(eps_rms, EPS).then_inc(vector_steps, e.step())
            eng.memset(eps_lnx, LNX_EPS).then_inc(vector_steps, e.step("eps"))
            eng.wait_ge(x_in, e.at("x_in"))
            eng.wait_ge(const_in, e.at("fin_in"))
            eng.sem_inc(vector_idle, 1)
            with eng.Fori(0, L) as l, e.rounds("layer", L, l):
                eng.wait_ge(par_in, e.at("par_in"))
                ts(negkk, par[:, PAR["k_k"]:PAR["k_k"] + 4], -1.0, None, ALU.mult).then_inc(vector_steps, e.step())
                ts(omka, par[:, PAR["k_a"]:PAR["k_a"] + 4], -1.0, 1.0, ALU.mult, ALU.add).then_inc(vector_steps, e.step())
                norm("n1", lambda k: pc("an", k))
                with eng.Fori(0, 5) as i, e.rounds("wa", 5, i):
                    for j in range(3):
                        tile = lambda lo, hi: proj[:, bass.ds(3 * i + j, 1), lo:hi].rearrange("p a t -> p (a t)")
                        eng.wait_ge(scalar_steps, e.at("raw9_last" if j == 2 else f"raw9_{j}"))
                        if j:
                            eng.wait_ge(vector_steps, e.at(f"shifted{j - 1}"))
                        else:
                            eng.wait_ge(vector_steps, e.at("shifted2", back=1))
                        tt(dif[:, 0:NP_ - 1], tile(0, NP_ - 1), tile(1, NP_), ALU.subtract).then_inc(vector_steps, e.step())
                        eng.wait_ge(vector_steps, e.mine())
                        stt(tile(1, NP_), dif[:, 0:NP_ - 1], par[:, bass.ds(3 * i + (PAR["mu"] + j), 1)], tile(1, NP_),
                                   ALU.mult, ALU.add).then_inc(vector_steps, e.step(f"shifted{j}"))
                mu = par[:, PAR["mu"]:PAR["mu"] + 15]
                eng.wait_ge(vector_steps, e.mine())
                tt(dif[:, 0:15], proj[:, 0:15, 0], mu, ALU.mult).then_inc(vector_steps, e.step())
                eng.wait_ge(shift_in, e.at("shift_in"))
                tt(edge, shd, raw9[:, :, 1:9], ALU.subtract).then_inc(vector_steps, e.step())
                eng.wait_ge(vector_steps, e.mine())
                tt(proj[:, 0:15, 0], proj[:, 0:15, 0], dif[:, 0:15], ALU.subtract).then_inc(vector_steps, e.step())
                tt(edge, edge, bcast(mu, 2, 8), ALU.mult).then_inc(vector_steps, e.step())
                eng.wait_ge(vector_steps, e.mine())
                tt(proj[:, 0:15, NP_:T], raw9[:, :, 1:9], edge, ALU.add).then_inc(vector_steps, e.step("edge_put"))

                eng.wait_ge(rope_in, e.at("rope_in"))
                eng.sem_inc(vector_idle, 1)
                with eng.Fori(0, 4) as p, e.rounds("rq", 4, p):
                    for c in range(NC3):
                        qt = proj[:, bass.ds(15 + p, 1), cs(c)].rearrange("p a t -> p (a t)")
                        eng.wait_ge(vector_steps, e.mine())
                        eng.wait_ge(tensor_steps, e.at(f"rq_rot{c}"))
                        tt(rt[:, c, :], bank[c][:, 0:CW], sin[:, cs(c)], ALU.mult).then_inc(vector_steps, e.step())
                        tt(qt, qt, cos[:, cs(c)], ALU.mult).then_inc(vector_steps, e.step())
                        eng.wait_ge(vector_steps, e.mine())
                        tt(qt, qt, rt[:, c, :], ALU.add).then_inc(vector_steps, e.step("rq_last" if c == 2 else f"rq_add{c}"))
                for g in range(2):
                    for c in range(NC3):
                        kt = kd[:, g, WIN + c * CW:WIN + (c + 1) * CW]
                        eng.wait_ge(tensor_steps, e.at(f"rk{g}{c}"))
                        eng.wait_ge(vector_steps, e.mine())
                        tt(rt[:, c, :], bank[3 + c][:, 0:CW], sin[:, cs(c)], ALU.mult).then_inc(vector_steps, e.step())
                        tt(kt, bank[c][:, 0:CW], cos[:, cs(c)], ALU.mult).then_inc(vector_steps, e.step())
                        eng.wait_ge(vector_steps, e.mine())
                        tt(kt, kt, rt[:, c, :], ALU.add).then_inc(vector_steps, e.step("kd_last" if (g, c) == (1, 2) else f"kd{g}{c}"))
                sink = par[:, PAR["sink"]:PAR["sink"] + 8]
                eng.wait_ge(pool_steps, e.at("att_zero"))

                def blocks(n, q, S, M, V):
                    o = 1 - q
                    st = lambda w, q: stat[:, 64 * q + 8 * w:64 * q + 8 * w + 8]
                    mine = lambda: eng.wait_ge(vector_att, at_block("vector_att", att.n, l, n + 1))
                    if V:
                        val.begin()
                        eng.wait_ge(tensor_val, at_block("tensor_val", "pt0", l, n - 1))
                        eng.wait_ge(tensor_val, at_block("tensor_val", "pv", l, n - 2))
                        eng.tensor_copy(pT[:, 0:4, :], bank[4][:, :].rearrange("p (h t) -> p h t", h=4)).then_inc(vector_val, val.step("ptc0"))
                    if S:
                        att.begin()
                        mk = amask[:, 256:512] if V or M else amask[:, 0:256]
                        if V:
                            eng.wait_ge(tensor_val, at_block("tensor_val", "pt3", l, n - 1))
                        for p in range(4):
                            eng.wait_ge(tensor_att, at_block("tensor_att", f"s{p}", l, n + 1))
                            stt(sm[o][:, 2 * p:2 * p + 2, :], bank[p][:, :].rearrange("p (h t) -> p h t", h=2), SCALE,
                                bcast(mk, 1, 2), ALU.mult, ALU.add).then_inc(vector_att, att.step(f"sc{p}"))
                            if p == 0 and V:
                                eng.wait_ge(tensor_val, at_block("tensor_val", "pt2", l, n - 1))
                                eng.tensor_copy(pT[:, 8:12, :], bank[4][:, :].rearrange("p (h t) -> p h t", h=4)).then_inc(vector_val, val.step("ptc2"))
                        mine()
                        mx, nmx, sk = st(0, o), st(2, o), st(4, o)
                        eng.tensor_reduce(mx, sm[o], AX.X, ALU.max).then_inc(vector_att, att.step())
                        mine()
                        tt(mx, mx, sink, ALU.max).then_inc(vector_att, att.step())
                        mine()
                        tt(sk, sink, mx, ALU.subtract).then_inc(vector_att, att.step())
                        ts(nmx, mx, -1.0, None, ALU.mult).then_inc(vector_att, att.step("negmax"))
                    if V and not S:
                        eng.wait_ge(tensor_val, at_block("tensor_val", "pt2", l, n - 1))
                        eng.tensor_copy(pT[:, 8:12, :], bank[4][:, :].rearrange("p (h t) -> p h t", h=4)).then_inc(vector_val, val.step("ptc2"))
                    if M:
                        soft.begin()
                        den, se, rd = st(3, q), st(5, q), st(6, q)
                        eng.wait_ge(scalar_soft, at_block("scalar_soft", "sinkexp", l, n))
                        tt(den, den, se, ALU.add).then_inc(vector_soft, soft.step("den"))
                        eng.wait_ge(vector_soft, at_block("vector_soft", "den", l, n))
                        eng.reciprocal(rd, den).then_inc(vector_soft, soft.step("recip"))
                        eng.wait_ge(vector_soft, at_block("vector_soft", "recip", l, n))
                        for h in range(5):
                            ts(sm[q][:, h, :], sm[q][:, h, :], rd[:, h:h + 1], None, ALU.mult).then_inc(vector_soft, soft.step("p_last" if h == 4 else None))
                    if V:
                        blk = bass.ds((n - 1) * WIN, WIN)
                        eng.wait_ge(scalar_val, at_block("scalar_val", "high", l, n - 1))
                        tt(hl[:, 4:8, blk], bank[6][:, :].rearrange("p (k t) -> p k t", k=4), hh[:, 4:8, blk].bitcast(F32),
                           ALU.subtract).then_inc(vector_val, val.step("low"))

                blocks(-1, 1, S=True, M=False, V=False)
                blocks(0, 0, S=True, M=True, V=False)
                with eng.Fori(0, NBLK // 2 - 1) as i, e.rounds("ab", NBLK // 2 - 1, i):
                    for q in range(2):
                        blocks(i * 2 + (1 + q), 1 - q, S=True, M=True, V=True)
                blocks(NBLK - 1, 1, S=False, M=True, V=True)
                blocks(NBLK, 0, S=False, M=False, V=True)
                eng.wait_ge(vector_steps, e.mine())
                for q in range(2):
                    eng.wait_ge(tensor_steps, e.at(f"d_s{q}"))
                    ts(smd[0:8, 4 * q:4 * q + 4, :], bank[2 + q][0:8, :].rearrange("p (b t) -> p b t", b=4), SCALE, None, ALU.mult).then_inc(vector_steps, e.step())
                eng.wait_ge(vector_steps, e.mine())
                dm, dd, dr = stat[0:8, 0:8], stat[0:8, 48:56], stat[0:8, 56:64]
                bcol = lambda v: bcast(v, 2, 128)
                eng.tensor_reduce(dm, smd[0:8], AX.X, ALU.max).then_inc(vector_steps, e.step())
                eng.wait_ge(vector_steps, e.mine())
                ts(dm, dm, par[0:8, PAR["sinkcol"]:PAR["sinkcol"] + 1], None, ALU.max).then_inc(vector_steps, e.step())
                eng.wait_ge(vector_steps, e.mine())
                tt(smd[0:8], smd[0:8], bcol(dm), ALU.subtract).then_inc(vector_steps, e.step("d_sub"))
                eng.wait_ge(scalar_steps, e.at("d_exp"))
                eng.tensor_reduce(dd, smd[0:8], AX.X, ALU.add).then_inc(vector_steps, e.step())
                eng.wait_ge(scalar_steps, e.at("d_sinkexp"))
                eng.wait_ge(vector_steps, e.mine())
                tt(dd, dd, stat[0:8, 8:16], ALU.add).then_inc(vector_steps, e.step())
                eng.wait_ge(vector_steps, e.mine())
                eng.reciprocal(dr, dd).then_inc(vector_steps, e.step())
                eng.wait_ge(vector_steps, e.mine())
                tt(smd[0:8], smd[0:8], bcol(dr), ALU.mult).then_inc(vector_steps, e.step("d_p"))
                eng.wait_ge(scalar_steps, e.at("att_high_dec"))
                tt(hl[:, 4:8, NP_:T], bank[0][:, 0:32].rearrange("p (k t) -> p k t", k=4), hh[:, 4:8, NP_:T].bitcast(F32),
                          ALU.subtract).then_inc(vector_steps, e.step("att_low_dec"))

                for o in range(4):
                    kt = proj[:, 4 + o, :]
                    eng.wait_ge(scalar_steps, e.at(f"knorm{o}2"))
                    eng.wait_ge(vector_steps, e.mine())
                    ts(nrm[:, :], nrm[:, :], 1e-12, None, ALU.max).then_inc(vector_steps, e.step())
                    eng.wait_ge(vector_steps, e.mine())
                    eng.reciprocal(at_[:, :], nrm[:, :]).then_inc(vector_steps, e.step(f"kk_recip{o}"))
                    eng.wait_ge(vector_steps, e.mine())
                    stt(nkk[:, o, :], kt, negkk[:, o:o + 1], at_[:, :], ALU.mult, ALU.mult).then_inc(vector_steps, e.step())
                    eng.wait_ge(scalar_steps, e.at(f"lw{o}1"))
                    eng.wait_ge(lora_in, e.at("lora_in"))
                    eng.tensor_tensor_scan(lw_flat[:, o, :], smask[:, :], lw_flat[:, o, :], 0.0, ALU.mult, ALU.add).then_inc(vector_steps, e.step())
                    eng.wait_ge(scalar_steps, e.at(f"lora_ev{o}"))
                    eng.wait_ge(vector_steps, e.mine())
                    ts(at_[:, :], bb[:, o, :], pc("k_a", o), omka[:, o:o + 1], ALU.mult, ALU.add).then_inc(vector_steps, e.step())
                    eng.wait_ge(vector_steps, e.mine())
                    tt(kt, kt, at_[:, :], ALU.mult).then_inc(vector_steps, e.step())
                    stt(bb[:, o, :], nkk[:, o, :], -1.0, bb[:, o, :], ALU.mult, ALU.mult).then_inc(vector_steps, e.step("elem_last" if o == 3 else None))

                eng.wait_ge(pool_steps, e.at("chunk_zero"))
                m16 = CST["d16"][0]
                o32 = bcast(c_("o32").rearrange("p (w t) -> p w t", w=2), 2, 2)
                k22 = lambda v: v.rearrange("p (w k) t -> p w k t", w=2)

                def chunk(c, q, B, A, P):
                    o = 1 - q
                    ps = lambda b, lo, hi, k: bank[b][:, lo:hi].rearrange("p (k t) -> p k t", k=k)
                    pr = lambda b: bank[b][:, :].rearrange("p (m r t) -> p m r t", m=4, r=2)
                    top = slice(0, 64)
                    tok = bass.ds((c + 2) * CH, CH)
                    mine = lambda: eng.wait_ge(vector_inv, at_chunk("vector_inv", inv.n, l, c + 1))
                    if A:
                        inv.begin()
                        for g in range(2):
                            eng.wait_ge(tensor_inv, at_chunk("tensor_inv", f"g1_{g}", l, c + 1))
                            X = ps(4 * g + 1, 0, 128, 2)
                            Gn = bank[4 * g][:, :].rearrange("p (k w t) -> p k w t", k=2, w=2)[:, :, 0, 0:64]
                            tt(two(lb[g][:, 2:4, :]), wide(X), mask2(cst[:, m16 + 128:m16 + 256], 2), ALU.mult).then_inc(vector_inv, inv.step())
                            tt(nr[0][g][:, 2:4, 0], X, bcast(c_("d16c")[:, 64:128], 1, 2), ALU.mult).then_inc(vector_inv, inv.step())
                            tt(two(xb[g]), wide(X), mask2(c_("low"), 2), ALU.mult).then_inc(vector_inv, inv.step())
                            tt(two(lb[g][:, 0:2, :]), wide(Gn), mask2(cst[:, m16:m16 + 128], 2), ALU.mult).then_inc(vector_inv, inv.step())
                            tt(nr[0][g][:, 0:2, 0], Gn, bcast(c_("d16c")[:, 0:64], 1, 2), ALU.mult).then_inc(vector_inv, inv.step(f"n16_{g}"))
                    if B:
                        state.begin()
                        for g in range(2):
                            eng.wait_ge(tensor_state, at_chunk("tensor_state", f"s2_{g}", l, c))
                            eng.tensor_copy(sac[g][top], ps(4 * g + 3, 128, 256, 2)[top]).then_inc(vector_state, state.step())
                            eng.tensor_copy(sas[g][top, :, 0:64], ps(4 * g + 3, 128, 256, 2)[top]).then_inc(vector_state, state.step(f"sa_{g}"))
                    if A:
                        for g in range(2):
                            G = ps(4 * g, 0, 512, 4)
                            mine()
                            tt(two(nm[o][g]), wide(G[:, :, 0:64]), mask2(c_("up"), 4), ALU.mult).then_inc(vector_inv, inv.step())
                            tt(mr[o][g], G[:, :, 64:128], bcast(c_("upi"), 1, 4), ALU.mult).then_inc(vector_inv, inv.step())
                            tt(nr[1][g][:, :, 1], nr[0][g][:, :, 0], bcast(II, 1, 4), ALU.add).then_inc(vector_inv, inv.step(f"m_{g}"))
                            eng.wait_ge(tensor_inv, at_chunk("tensor_inv", f"l2_{g}", l, c + 1))
                            eng.tensor_copy(nr[1][g][top, :, 0], ps(4 * g + 1, 128, 384, 4)[top]).then_inc(vector_inv, inv.step())
                            eng.tensor_copy(la[g][top, :, 0:64], ps(4 * g + 1, 128, 384, 4)[top]).then_inc(vector_inv, inv.step(f"l2e_{g}"))
                    for g in range(2):
                        if B:
                            eng.wait_ge(tensor_state, at_chunk("tensor_state", f"s3_{g}", l, c))
                            tt(Sc[g], ps(4 * g + 3, 256, 384, 2), Sc[g], ALU.add).then_inc(vector_state, state.step(f"S_add{g}"))
                        if A:
                            eng.wait_ge(tensor_inv, at_chunk("tensor_inv", f"l4_{g}", l, c + 1))
                            eng.tensor_copy(nr[0][g][top, :, 0], pr(4 * g)[top, :, 0]).then_inc(vector_inv, inv.step())
                            eng.tensor_copy(lb[g][top, :, 0:64], pr(4 * g)[top, :, 0]).then_inc(vector_inv, inv.step())
                            eng.wait_ge(scalar_inv, at_chunk("scalar_inv", f"l4e_{g}", l, c + 1))
                            tt(nr[0][g][:, :, 1], pr(4 * g)[:, :, 1], nr[1][g][:, :, 1], ALU.add).then_inc(vector_inv, inv.step(f"l4e_{g}"))
                    for g in range(2):
                        if A:
                            eng.wait_ge(tensor_inv, at_chunk("tensor_inv", f"l8_{g}", l, c + 1))
                            eng.tensor_copy(la[g][top, :, 0:64], pr(4 * g + 1)[top, :, 0]).then_inc(vector_inv, inv.step())
                            eng.wait_ge(scalar_inv, at_chunk("scalar_inv", f"l8e_{g}", l, c + 1))
                            tt(nr[1][g][:, :, 1], pr(4 * g + 1)[:, :, 1], nr[0][g][:, :, 1], ALU.add).then_inc(vector_inv, inv.step(f"l8e_{g}"))
                    if B:
                        for g in range(2):
                            eng.wait_ge(scalar_prep, at_chunk("scalar_prep", "exp_end", l, c))
                            eng.wait_ge(vector_state, at_chunk("vector_state", f"S_add{g}", l, c))
                            tt(Sc[g], Sc[g], bcast(pend[q][:, 2 * g:2 * g + 2], 2, 64), ALU.mult).then_inc(vector_state, state.step(f"S_dec{g}"))
                    if P:
                        prep.begin()
                        eng.wait_ge(scalar_prep, at_chunk("scalar_prep", "exp_bbd1", l, c + 2))
                        tt(two(kbd), wide(proj[:, 4:8, tok]), two(bbd), ALU.mult).then_inc(vector_prep, prep.step("kbd"))
                    if A:
                        for g in range(2):
                            eng.wait_ge(tensor_inv, at_chunk("tensor_inv", f"r8_{g}", l, c + 1))
                            tt(nr[0][g][:, :, 1], pr(4 * g)[:, :, 1], nr[1][g][:, :, 1], ALU.add).then_inc(vector_inv, inv.step(f"r8c_{g}"))
                            mine()
                            eng.tensor_copy(lb[g][top, :, 0:64], nr[0][g][top, :, 1]).then_inc(vector_inv, inv.step(f"r8e_{g}"))
                    if P:
                        eng.wait_ge(vector_prep, at_chunk("vector_prep", "kbd", l, c + 2))
                        tt(two(bbd), wide(bb[:, :, tok]), two(bbd), ALU.mult).then_inc(vector_prep, prep.step("bbd"))
                    if A:
                        for g in range(2):
                            eng.wait_ge(tensor_inv, at_chunk("tensor_inv", f"m1_{g}", l, c + 1))
                            tt(k22(nr[1][g][:, :, 0]), k22(pr(4 * g + 1)[:, :, 1]), o32, ALU.mult).then_inc(vector_inv, inv.step(f"m1e_{g}"))
                    if B:
                        for g in range(2):
                            eng.wait_ge(vector_state, at_chunk("vector_state", f"S_dec{g}", l, c))
                            eng.wait_ge(tensor_state, at_chunk("tensor_state", f"y_{g}", l, c))
                            tt(two(Ss[g]), wide(Sc[g]), mask2(c_("bd"), 2), ALU.mult).then_inc(vector_state, state.step(f"S_new{g}"))
                    if A:
                        for g in range(2):
                            eng.wait_ge(tensor_inv, at_chunk("tensor_inv", f"m2_{g}", l, c + 1))
                            tt(nr[1][g][:, :, 1], pr(4 * g)[:, :, 0], nr[0][g][:, :, 1], ALU.add).then_inc(vector_inv, inv.step(f"m2c_{g}"))
                            mine()
                            eng.tensor_copy(la[g][top, 0:2, 0:64], nr[1][g][top, 2:4, 1]).then_inc(vector_inv, inv.step(f"m2e_{g}"))
                    if P:
                        eng.wait_ge(scalar_prep, at_chunk("scalar_prep", "exp_abd1", l, c + 2))
                        tt(two(abd[q]), wide(nkk[:, :, tok]), two(abd[q]), ALU.mult).then_inc(vector_prep, prep.step("abd"))
                    if A:
                        for g in range(2):
                            eng.wait_ge(tensor_inv, at_chunk("tensor_inv", f"m3_{g}", l, c + 1))
                            tt(nr[0][g][:, 0:2, 0], pr(4 * g + 1)[:, 0:2, 1], bcast(c_("o64"), 1, 2), ALU.mult).then_inc(vector_inv, inv.step(f"m3e_{g}"))
                        for g in range(2):
                            eng.wait_ge(tensor_inv, at_chunk("tensor_inv", f"m4_{g}", l, c + 1))
                            tt(nr[0][g][:, 0:2, 1], pr(4 * g)[:, 0:2, 0], nr[1][g][:, 0:2, 1], ALU.add).then_inc(vector_inv, inv.step(f"m4c_{g}"))
                            mine()
                            eng.tensor_copy(Tt[o][g][top, :, 0:64], nr[0][g][top, 0:2, 1]).then_inc(vector_inv, inv.step(f"m4e_{g}"))

                chunk(-2, 0, B=False, A=False, P=True)
                chunk(-1, 1, B=False, A=True, P=True)
                with eng.Fori(0, NCH // 2 - 1) as i, e.rounds("rc", NCH // 2 - 1, i):
                    for q in range(2):
                        chunk(i * 2 + q, q, B=True, A=True, P=True)
                chunk(NCH - 2, 0, B=True, A=True, P=False)
                chunk(NCH - 1, 1, B=True, A=False, P=False)

                eng.wait_ge(state_in, e.at("state_in"))
                eng.wait_ge(scalar_steps, e.at("wdec"))
                eng.wait_ge(scalar_state, at_chunk("scalar_state", "y1", l, NCH - 1))
                eng.sem_inc(vector_idle, 1)
                with eng.Fori(0, 2) as i, e.rounds("dp", 2, i):
                    col = lambda v: bcast(v.rearrange("p a t -> p (a t)"), 2, 64)
                    tile = lambda t, q: col(t[:, bass.ds(i * 2 + q, 1), NP_:T])
                    S = [SD[:, bass.ds(i * 2 + j, 1)].rearrange("p a b i -> p (a b) i") for j in range(2)]
                    banked = lambda b: bank[b][:, :].rearrange("p (b i) -> p b i", b=8)
                    iib = bcast(II, 1, 8)
                    for j in range(2):
                        eng.wait_ge(vector_steps, e.at(f"dec_y{j}", back=1))
                        tt(t1[j], S[j], tile(nkk, j), ALU.mult).then_inc(vector_steps, e.step(f"dp_sa_in{j}"))
                        tt(t2[j], iib, tile(proj, j + 8), ALU.mult).then_inc(vector_steps, e.step(f"dp_v_in{j}"))
                        tt(S[j], S[j], col(wdec[:, bass.ds(i * 2 + j, 1), :]), ALU.mult).then_inc(vector_steps, e.step(f"dp_decayed{j}"))
                    for j in range(2):
                        eng.wait_ge(tensor_steps, e.at(f"dp_sa{j}"))
                        tt(t3[j], banked(3 * j), tile(bb, j), ALU.mult).then_inc(vector_steps, e.step(f"dp_sab{j}"))
                        eng.wait_ge(tensor_steps, e.at(f"dp_v{j}"))
                        tt(t1[j], banked(3 * j + 1), tile(proj, j + 4), ALU.mult).then_inc(vector_steps, e.step(f"dp_vk{j}"))
                    for j in range(2):
                        eng.wait_ge(vector_steps, e.at(f"dp_sab{j}"))
                        tt(S[j], S[j], t3[j], ALU.add).then_inc(vector_steps, e.step(f"dp_half{j}"))
                    for j in range(2):
                        eng.wait_ge(vector_steps, e.at(f"dp_half{j}"))
                        tt(S[j], S[j], t1[j], ALU.add).then_inc(vector_steps, e.step(f"dp_new{j}"))
                    for j in range(2):
                        eng.wait_ge(vector_steps, e.at(f"dp_new{j}"))
                        tt(t2[j], S[j], tile(proj, j), ALU.mult).then_inc(vector_steps, e.step(f"dp_r_in{j}"))
                    for j in range(2):
                        eng.wait_ge(tensor_steps, e.at(f"dp_y{j}"))
                        tt(t3[j], banked(3 * j + 2), iib, ALU.mult).then_inc(vector_steps, e.step(f"dp_y_of{j}"))
                    for j in range(2):
                        eng.wait_ge(vector_steps, e.at(f"dp_y_of{j}"))
                        eng.sem_inc(vector_idle, 1)
                        eng.tensor_reduce(yar[:, bass.ds(i * 2 + j, 1), NP_:T].rearrange("p a t -> p (a t)"), t3[j], AX.X, ALU.add).then_inc(vector_steps, e.step(f"dec_y{j}"))
                    e.also("dec_y")

                eng.wait_ge(vector_steps, e.mine())
                eng.sem_inc(vector_idle, 1)
                with eng.Fori(0, NC3) as c, e.rounds("fin", NC3, c):
                    seg = bass.ds(c * CW, CW)
                    eng.wait_ge(wg_in, e.at("wg_in"))
                    for o in range(4):
                        eng.wait_ge(vector_steps, e.at(f"fin_lb{o}", back=1))
                        stt(fbo[o][:, :], proj[:, o, seg], pc("r_k", o), proj[:, 4 + o, seg], ALU.mult, ALU.mult).then_inc(vector_steps, e.step(f"fin_rk{o}"))
                    for o in range(4):
                        eng.wait_ge(tensor_steps, e.at(f"fin_mean{o}"))
                        eng.wait_ge(pool_steps, e.at(f"fin_low{o}", back=1))
                        stt(fyc[o][:, :], bank[o][:, 0:CW], -1.0 / HD, yar[:, o, seg], ALU.mult, ALU.add).then_inc(vector_steps, e.step(f"fin_yc{o}"))
                    for o in range(4):
                        rs = fsd[o % 2]
                        eng.wait_ge(tensor_steps, e.at(f"fin_bonus{o}"))
                        tt(fbo[o][:, :], bank[4 + o][:, 0:CW], proj[:, 8 + o, seg], ALU.mult).then_inc(vector_steps, e.step(f"fin_bo{o}"))
                        eng.wait_ge(scalar_steps, e.at(f"fin_sd{o}"))
                        eng.reciprocal(rs[:, :], rs[:, :]).then_inc(vector_steps, e.step(f"fin_rs{o}"))
                        eng.wait_ge(vector_steps, e.at(f"fin_rs{o}"))
                        stt(fyc[o][:, :], fyc[o][:, :], pc("lg", o), rs[:, :], ALU.mult, ALU.mult).then_inc(vector_steps, e.step(f"fin_lg{o}"))
                        eng.wait_ge(vector_steps, e.at(f"fin_lg{o}"))
                        stt(fyc[o][:, :], fyc[o][:, :], pc("lb", o), fbo[o][:, :], ALU.add, ALU.add).then_inc(vector_steps, e.step(f"fin_lb{o}"))
                        eng.wait_ge(tensor_steps, e.at(f"fin_gate{o}"))
                        eng.wait_ge(vector_steps, e.at(f"fin_lb{o}"))
                        tt(fyc[o][:, :], fyc[o][:, :], bank[4 + o][:, 0:CW], ALU.mult).then_inc(vector_steps, e.step(f"fin_out{o}"))

                for k in range(KT):
                    eng.wait_ge(x_back[k], e.at(f"x_back{k}"))
                    for c in range(NC3):
                        eng.wait_ge(tensor_steps, e.at(f"wo_mm{k}{c}"))
                        tt(x[:, k, cs(c)], bank[c][:, 0:CW], x[:, k, cs(c)], ALU.add).then_inc(vector_steps, e.step(f"wo_add{k}{c}"))
                e.also("wo_add_last")
                eng.wait_ge(vector_steps, e.mine())
                eng.sem_inc(vector_idle, 1)
                norm("n2", lambda k: pc("fn", k))
                with eng.Fori(0, NFF // 2) as i, e.rounds("ff", NFF // 2, i):
                    for j in range(2):
                        for c in range(NC3):
                            eng.wait_ge(tensor_steps, e.at(f"ff_u{j}{c}"))
                            eng.wait_ge(scalar_steps, e.at(f"ff_sil{j}{c}"))
                            eng.wait_ge(vector_steps, e.mine())
                            tt(midf[:, c, :], sil[:, c, :], bank[3 + c][:, 0:CW], ALU.mult).then_inc(vector_steps, e.step(f"ff_mid{j}{c}"))
                        for c in range(NC3):
                            eng.wait_ge(scalar_steps, e.at(f"ff_high{j}{c}"))
                            tt(ml[:, j, cs(c)], midf[:, c, :], mh[:, j, cs(c)].bitcast(F32), ALU.subtract).then_inc(vector_steps, e.step(f"ff_low{j}{c}"))
                    for c in range(NC3):
                        for k in range(KT):
                            eng.wait_ge(tensor_steps, e.at(f"ff_d{c * KT + k}"))
                            tt(x[:, k, cs(c)], bank[6 + k % 2][:, 0:CW], x[:, k, cs(c)], ALU.add).then_inc(vector_steps, e.step(f"ff_add{c * KT + k}"))
                    e.also("ff_add_last")
                    eng.wait_ge(vector_steps, e.mine())

            eng.sem_inc(vector_idle, 1)
            norm("nf", lambda k: fng[:, k:k + 1], last=True)

        @block.tensor
        def _(eng):
            e = Count(steps, "tensor")
            inv, state = Chunk(steps, "tensor_inv"), Chunk(steps, "tensor_state")
            eng.sem_inc(tensor_steps, CREDIT)
            eng.sem_inc(tensor_inv, CHUNK_CREDIT)
            eng.sem_inc(tensor_state, CHUNK_CREDIT)
            eng.sem_inc(tensor_att, CHUNK_CREDIT)
            att = Chunk(steps, "tensor_att")
            eng.sem_inc(tensor_val, CHUNK_CREDIT)
            val = Chunk(steps, "tensor_val")
            mm = eng.matmul

            def norm(p):
                for c in range(NC3):
                    if c:
                        eng.wait_ge(scalar_steps, e.at(f"{p}{c - 1}_std"))
                    for k in range(KT):
                        eng.wait_ge(scalar_steps, e.at(f"{p}{c}_sq{k}"))
                        last = mm(bank[5][:, 0:CW], ones, sq[:, k, :], start=(k == 0), stop=(k == KT - 1))
                    last.then_inc(tensor_steps, e.step(f"{p}{c}_ss"))

            def unit(k, i=0, per=0):
                eng.wait_ge(w_low, layer[0] * UL + k + i * per + 1)
                return slot(k)

            def column(out, s, wcols, act_h, act_l, start, stop):
                mm(out, wh[s][:, wcols], act_h, start=start, stop=False)
                mm(out, wh[s][:, wcols], act_l, start=False, stop=False)
                return mm(out, wl[s][:, wcols], act_h, start=False, stop=stop)

            def tile(s, out, c):
                for k in range(KT):
                    last = column(out, s, slice(k * 128, k * 128 + 128), hh[:, k, cs(c)], hl[:, k, cs(c)], k == 0, k == KT - 1)
                return last

            layer = [0]
            eng.wait_ge(const_in, e.at("fin_in"))
            eng.sem_inc(tensor_idle, 1)
            with eng.Fori(0, L) as l, e.rounds("layer", L, l):
                layer[0] = l
                norm("n1")
                with eng.Fori(0, 5) as i, e.rounds("wa", 5, i):
                    for j in range(3):
                        s = unit(j, i, 3)
                        for c in range(NC3):
                            if j == 0:
                                eng.wait_ge(vector_steps, e.at(f"n1{c}_low7"))
                            if j:
                                eng.wait_ge(scalar_steps, e.at(f"wa_ev{j - 1}{c}"))
                            else:
                                eng.wait_ge(scalar_steps, e.at(f"wa_ev2{c}", back=1))
                            tile(s, bank[c][:, 0:CW], c).then_inc(tensor_steps, e.step(f"wa_mm{j}{c}"))
                for k in range(15, NIN):
                    s = unit(k)
                    for c in range(NC3):
                        eng.wait_ge(scalar_steps, e.at(f"wb_ev{k - 1}{c}" if k > 15 else f"wa_ev2{c}"))
                        tile(s, bank[c][:, 0:CW], c).then_inc(tensor_steps, e.step(f"wb_mm{k}{c}"))
                e.also("win_last")

                eng.wait_ge(rope_in, e.at("rope_in"))
                eng.wait_ge(scalar_steps, e.at(f"wb_ev{NIN - 1}2"))
                eng.sem_inc(tensor_idle, 1)
                with eng.Fori(0, 4) as p, e.rounds("rq", 4, p):
                    for c in range(NC3):
                        eng.wait_ge(vector_steps, e.at("rq_last" if c == 2 else f"rq_add{c}", back=1))
                        mm(bank[c][:, 0:CW], rotm, proj[:, bass.ds(15 + p, 1), cs(c)].rearrange("p a t -> p (a t)"),
                                  start=True, stop=True).then_inc(tensor_steps, e.step(f"rq_rot{c}"))
                eng.wait_ge(vector_steps, e.at("rq_last"))
                for g in range(2):
                    for c in range(NC3):
                        if g:
                            eng.wait_ge(vector_steps, e.at(f"kd0{c}"))
                        mm(bank[c][:, 0:CW], dup[:, 128 * g:128 * g + 128], proj[:, 19, cs(c)], start=True, stop=True)
                        mm(bank[3 + c][:, 0:CW], rdup[:, 128 * g:128 * g + 128], proj[:, 19, cs(c)], start=True, stop=True).then_inc(tensor_steps, e.step(f"rk{g}{c}"))
                eng.wait_ge(vector_steps, e.at("kd_last"))
                eng.wait_ge(pool_steps, e.at("att_zero"))
                eng.sem_inc(tensor_idle, 1)

                def blocks(n, q, S, M, V):
                    o = 1 - q
                    if S:
                        att.begin()
                    if V:
                        val.begin()

                    def probs_t(w):
                        if w == 0:
                            eng.wait_ge(vector_val, at_block("vector_val", "ptc2", l, n - 2))
                        elif w == 1:
                            eng.wait_ge(scalar_val, at_block("scalar_val", "ptc3", l, n - 2))
                        elif w == 2:
                            eng.wait_ge(vector_val, at_block("vector_val", "ptc0", l, n - 1))
                        else:
                            eng.wait_ge(scalar_val, at_block("scalar_val", "ptc1", l, n - 1))
                        for k in range(4):
                            h, kt = (4 * w + k) // 2, k % 2
                            last = mm(bank[4 + w % 2][:, 128 * k:128 * k + 128], sm[o][:, h, 128 * kt:128 * kt + 128], ident,
                                      is_transpose=True, start=True, stop=True)
                        last.then_inc(tensor_val, val.step(f"pt{w}"))

                    def scores(p):
                        eng.wait_ge(vector_att, at_block("vector_att", f"sc{p}", l, n))
                        for h in range(2):
                            last = mm(bank[p][:, 256 * h:256 * h + 256], bdq[:, p, 128 * h:128 * h + 128],
                                      kd[:, p // 2, bass.ds((n + 1) * WIN, 2 * WIN)], start=True, stop=True)
                        last.then_inc(tensor_att, att.step(f"s{p}"))

                    if V:
                        eng.wait_ge(scalar_soft, at_block("scalar_soft", "vblk", l, n - 1))
                        eng.wait_ge(scalar_val, at_block("scalar_val", "vp", l, n - 2))
                        mm(bank[7][:, 0:128], vblk[:, :], ident, is_transpose=True, start=True, stop=True).then_inc(tensor_val, val.step("vt"))
                        eng.wait_ge(vector_soft, at_block("vector_soft", "p_last", l, n - 1))
                        eng.wait_ge(scalar_soft, at_block("scalar_soft", "p_last", l, n - 1))
                        probs_t(0)
                        probs_t(1)
                    if S:
                        eng.wait_ge(scalar_att, at_block("scalar_att", "bdq1", l, n + 1))
                        scores(0)
                        if not V:
                            scores(1)
                    if V:
                        probs_t(2)
                        probs_t(3)
                    if S:
                        for p in range(1 if V else 2, 4):
                            scores(p)
                    if V:
                        eng.wait_ge(vector_val, at_block("vector_val", "low", l, n - 2))
                        eng.wait_ge(scalar_val, at_block("scalar_val", "vp", l, n - 1))
                        eng.wait_ge(vector_val, at_block("vector_val", "ptc2", l, n - 1))
                        eng.wait_ge(scalar_val, at_block("scalar_val", "ptc3", l, n - 1))
                        for p in range(4):
                            for h in range(2):
                                for kt in range(2):
                                    v = vp[(q + kt) % 2][:, p // 2, (64 - 64 * h):(192 - 64 * h)]
                                    last = mm(bank[6][:, 128 * p:128 * p + 128], v, pT[:, 2 * (2 * p + h) + kt, :],
                                              start=(h, kt) == (0, 0), stop=(h, kt) == (1, 1))
                        last.then_inc(tensor_val, val.step("pv"))

                blocks(-1, 1, S=True, M=False, V=False)
                blocks(0, 0, S=True, M=True, V=False)
                with eng.Fori(0, NBLK // 2 - 1) as i, e.rounds("ab", NBLK // 2 - 1, i):
                    for q in range(2):
                        blocks(i * 2 + (1 + q), 1 - q, S=True, M=True, V=True)
                blocks(NBLK - 1, 1, S=False, M=True, V=True)
                blocks(NBLK, 0, S=False, M=False, V=True)
                eng.wait_ge(vector_val, at_block("vector_val", "low", l, NBLK - 1))
                for h in range(8):
                    s2 = 2 * (h % 2) + h // 4
                    last = mm(bank[1][:, 8 * h:8 * h + 8], sel[:, 128 * s2:128 * s2 + 128], proj[:, 15 + h // 2, NP_:T],
                              start=True, stop=True)
                last.then_inc(tensor_steps, e.step("d_qz"))
                eng.wait_ge(scalar_steps, e.at("d_qz_c"))
                eng.wait_ge(scalar_steps, e.at("v_new"))
                eng.wait_ge(scalar_steps, e.at("k_new"))
                for q in range(2):
                    for b in range(4):
                        last = mm(bank[2 + q][0:8, 128 * b:128 * b + 128],
                                  qz[:, :].rearrange("p (h b) -> p h b", h=8)[:, :, 4 * q + b], Kw[:, 4 * q + b, :], start=True, stop=True)
                    last.then_inc(tensor_steps, e.step(f"d_s{q}"))
                for q in range(2):
                    for b in range(4):
                        last = mm(bank[5 + q][:, 128 * b:128 * b + 128], Vw[:, 4 * q + b, :], ident, is_transpose=True, start=True, stop=True)
                    last.then_inc(tensor_steps, e.step(f"d_vt{q}"))
                eng.wait_ge(vector_steps, e.at("d_p"))
                eng.sem_inc(tensor_idle, 1)
                for b in range(8):
                    last = mm(bank[4][:, 8 * b:8 * b + 8], smd[0:8, b, :], ident[0:8, 0:8], is_transpose=True, start=True, stop=True)
                last.then_inc(tensor_steps, e.step("d_pt"))
                eng.wait_ge(scalar_steps, e.at("d_ptc"))
                for b in range(8):
                    last = mm(bank[7][:, 8 * b:8 * b + 8], VwT[:, b, :], pTd[:, 8 * b:8 * b + 8], start=True, stop=True)
                last.then_inc(tensor_steps, e.step("d_pv"))
                eng.wait_ge(scalar_steps, e.at("d_ov"))
                ovh = ov[:, :].rearrange("p (b h) -> p b h", b=8)
                for p in range(4):
                    for h in range(2):
                        s2 = 2 * (p // 2) + h
                        last = mm(bank[0][:, 8 * p:8 * p + 8], sel[:, 128 * s2:128 * s2 + 128], ovh[:, :, 2 * p + h],
                                  start=(h == 0), stop=(h == 1))
                last.then_inc(tensor_steps, e.step("d_place"))

                eng.wait_ge(vector_steps, e.at("att_low_dec"))
                for o in range(4):
                    eng.wait_ge(scalar_steps, e.at(f"ksq{o}"))
                    if o:
                        eng.wait_ge(scalar_steps, e.at(f"knorm{o - 1}2"))
                    for c in range(NC3):
                        last = mm(bank[5 + c][:, 0:CW], bdones, ksq[:, cs(c)], start=True, stop=True)
                    last.then_inc(tensor_steps, e.step(f"kk_mm{o}"))
                    if o == 0:
                        eng.wait_ge(scalar_steps, e.at("tanh"))
                        eng.wait_ge(lora_in, e.at("lora_in"))
                    else:
                        eng.wait_ge(scalar_steps, e.at(f"lora_ev{o - 1}"))
                    oc = slice(128 * o, 128 * o + 128)
                    for w in range(2):
                        for q in range(2):
                            mm(bank[3 * w + q][:, :], wda[:, w, oc], proj[:, 12, 512 * q:512 * q + 512], start=True, stop=True)
                        last = mm(bank[2][:, 8 * w:8 * w + 8], wda[:, w, oc], proj[:, 12, NP_:T], start=True, stop=True)
                    last.then_inc(tensor_steps, e.step(f"lora{o}"))

                eng.wait_ge(vector_steps, e.at("elem_last"))
                eng.wait_ge(pool_steps, e.at("chunk_zero"))

                def square(b, at0, spread, cur, step):
                    for m in range(4):
                        out = bank[b][:, at0 + step * m:at0 + step * (m + 1)]
                        last = mm(out, spread[:, (m + 2) % 4, :], cur(m), start=True, stop=True)
                    return last

                def chunk(c, q, B, A, P):
                    o = 1 - q
                    if B:
                        state.begin()
                        for g in range(2):
                            eng.wait_ge(vector_inv, at_chunk("vector_inv", f"m_{g}", l, c))
                            eng.wait_ge(scalar_inv, at_chunk("scalar_inv", f"vts_{g}", l, c))
                            eng.wait_ge(vector_state, at_chunk("vector_state", f"S_new{g}", l, c - 1))
                            eng.wait_ge(scalar_state, at_chunk("scalar_state", f"y{g}", l, c - 1))
                            for p in range(2):
                                out = bank[4 * g + 3][:, 64 * p:64 * p + 64]
                                mm(out, abd[q][:, 2 * g + p, :], Sc[g][:, p, :], start=True, stop=False)
                                last = mm(out, nm[q][g][:, 2 * p + 1, :], vc[q][g][:, p, :], start=False, stop=True)
                            last.then_inc(tensor_state, state.step(f"s1_{g}"))
                    if A:
                        inv.begin()
                        eng.wait_ge(vector_prep, at_chunk("vector_prep", "abd", l, c + 1))
                        eng.wait_ge(pool_prep, at_chunk("pool_prep", "ar", l, c + 1))
                        eng.wait_ge(scalar_prep, at_chunk("scalar_prep", "vbd1", l, c + 1))
                        for g in range(2):
                            eng.wait_ge(vector_inv, at_chunk("vector_inv", f"m4e_{g}", l, c))
                            eng.wait_ge(scalar_inv, at_chunk("scalar_inv", f"m4e_{g}", l, c))
                            for p in range(2):
                                k = 2 * g + p
                                ar = arc[o][:, k].rearrange("p w t -> p (w t)")
                                mm(bank[4 * g][:, 256 * p:256 * p + 128], bbd[:, k, :], ar, start=True, stop=True)
                                mm(bank[4 * g][:, 256 * p + 128:256 * p + 256], kbd[:, k, :], ar, start=True, stop=True)
                                mm(bank[4 * g + 1][:, 64 * p:64 * p + 64], abd[o][:, k, :], bc[:, k, :], start=True, stop=True)
                                last = mm(bank[4 * g + 2][:, 128 * p:128 * p + 128], vbd[:, k, :], ident, is_transpose=True, start=True, stop=True)
                            last.then_inc(tensor_inv, inv.step(f"g1_{g}"))
                    if B:
                        for g in range(2):
                            eng.wait_ge(scalar_state, at_chunk("scalar_state", f"sa0_{g}", l, c))
                            eng.wait_ge(vector_inv, at_chunk("vector_inv", f"m4e_{g}", l, c))
                            eng.wait_ge(scalar_inv, at_chunk("scalar_inv", f"m4e_{g}", l, c))
                            for p in range(2):
                                last = mm(bank[4 * g + 3][:, 128 + 64 * p:192 + 64 * p], Tt[q][g][:, p, :], sa0[g][:, p, :], start=True, stop=True)
                            last.then_inc(tensor_state, state.step(f"s2_{g}"))
                    if A:
                        for g in range(2):
                            eng.wait_ge(scalar_inv, at_chunk("scalar_inv", f"vts_{g}", l, c + 1))
                            for p in range(2):
                                k = 2 * g + p
                                mm(bank[4 * g + 2][:, 256 * p:256 * p + 128], bbd[:, k, :], ident, is_transpose=True, start=True, stop=True)
                                last = mm(bank[4 * g + 2][:, 256 * p + 128:256 * p + 256], kbd[:, k, :], ident, is_transpose=True,
                                          start=True, stop=True)
                            last.then_inc(tensor_inv, inv.step(f"bkt_{g}"))
                        for g in range(2):
                            eng.wait_ge(vector_inv, at_chunk("vector_inv", f"n16_{g}", l, c + 1))
                            square(4 * g + 1, 128, lb[g], lambda m: nr[0][g][:, m, 0], 64).then_inc(tensor_inv, inv.step(f"l2_{g}"))

                    def new_state(g):
                        eng.wait_ge(vector_state, at_chunk("vector_state", f"sa_{g}", l, c))
                        eng.wait_ge(scalar_state, at_chunk("scalar_state", f"sa_{g}", l, c))
                        eng.wait_ge(scalar_inv, at_chunk("scalar_inv", f"bks_{g}", l, c))
                        for p in range(2):
                            out = bank[4 * g + 3][:, 256 + 64 * p:320 + 64 * p]
                            mm(out, bks[q][g][:, 2 * p, :], sac[g][:, p, :], start=True, stop=False)
                            last = mm(out, bks[q][g][:, 2 * p + 1, :], vc[q][g][:, p, :], start=False, stop=True)
                        last.then_inc(tensor_state, state.step(f"s3_{g}"))

                    def heads_out(g):
                        eng.wait_ge(vector_state, at_chunk("vector_state", f"S_add{g}", l, c))
                        for p in range(2):
                            out = bank[4 * g + 3][:, 384 + 64 * p:448 + 64 * p]
                            mm(out, Ss[g][:, p, :], arc[q][:, 2 * g + p, 1, :], start=True, stop=False)
                            mm(out, sas[g][:, p, :], mr[q][g][:, 2 * p, :], start=False, stop=False)
                            last = mm(out, vts[q][g][:, p, :], mr[q][g][:, 2 * p + 1, :], start=False, stop=True)
                        last.then_inc(tensor_state, state.step(f"y_{g}"))

                    if A:
                        both = lambda w, g: lambda m: nr[w][g][:, m].rearrange("p r t -> p (r t)")
                        for g in range(2):
                            if B:
                                new_state(g)
                            eng.wait_ge(scalar_inv, at_chunk("scalar_inv", f"l2e_{g}", l, c + 1))
                            eng.wait_ge(vector_inv, at_chunk("vector_inv", f"l2e_{g}", l, c + 1))
                            square(4 * g, 0, la[g], both(1, g), 128).then_inc(tensor_inv, inv.step(f"l4_{g}"))
                    if B and not A:
                        new_state(0)
                        new_state(1)
                    if A:
                        for g in range(2):
                            eng.wait_ge(vector_inv, at_chunk("vector_inv", f"l4e_{g}", l, c + 1))
                            square(4 * g + 1, 0, lb[g], both(0, g), 128).then_inc(tensor_inv, inv.step(f"l8_{g}"))
                            if B:
                                heads_out(g)
                        for g in range(2):
                            eng.wait_ge(vector_inv, at_chunk("vector_inv", f"l8e_{g}", l, c + 1))
                            square(4 * g, 0, la[g], both(1, g), 128).then_inc(tensor_inv, inv.step(f"r8_{g}"))
                    if B and not A:
                        heads_out(0)
                        heads_out(1)
                    if A:
                        for g in range(2):
                            eng.wait_ge(vector_inv, at_chunk("vector_inv", f"r8c_{g}", l, c + 1))
                            for p in range(2):
                                mm(bank[4 * g + 1][:, 128 * p:128 * p + 128], xb[g][:, p, :], both(0, g)(p), start=True, stop=True)
                            for p in range(2):
                                last = mm(bank[4 * g + 1][:, 256 + 128 * p:384 + 128 * p], nm[o][g][:, 2 * p, :], both(0, g)(2 + p),
                                          start=True, stop=True)
                            last.then_inc(tensor_inv, inv.step(f"m1_{g}"))
                        for g in range(2):
                            eng.wait_ge(scalar_inv, at_chunk("scalar_inv", f"r8e_{g}", l, c + 1))
                            eng.wait_ge(vector_inv, at_chunk("vector_inv", f"m1e_{g}", l, c + 1))
                            square(4 * g, 0, lb[g], both(1, g), 128).then_inc(tensor_inv, inv.step(f"m2_{g}"))
                        for g in range(2):
                            eng.wait_ge(vector_inv, at_chunk("vector_inv", f"m2c_{g}", l, c + 1))
                            for p in range(2):
                                last = mm(bank[4 * g + 1][:, 128 * p:128 * p + 128], xb[g][:, p, :], both(1, g)(p), start=True, stop=True)
                            last.then_inc(tensor_inv, inv.step(f"m3_{g}"))
                        for g in range(2):
                            eng.wait_ge(scalar_inv, at_chunk("scalar_inv", f"m2e_{g}", l, c + 1))
                            eng.wait_ge(vector_inv, at_chunk("vector_inv", f"m3e_{g}", l, c + 1))
                            for p in range(2):
                                last = mm(bank[4 * g][:, 128 * p:128 * p + 128], la[g][:, p, :], both(0, g)(p), start=True, stop=True)
                            last.then_inc(tensor_inv, inv.step(f"m4_{g}"))

                chunk(-1, 1, B=False, A=True, P=True)
                with eng.Fori(0, NCH // 2 - 1) as i, e.rounds("rc", NCH // 2 - 1, i):
                    for q in range(2):
                        chunk(i * 2 + q, q, B=True, A=True, P=True)
                chunk(NCH - 2, 0, B=True, A=True, P=False)
                chunk(NCH - 1, 1, B=True, A=False, P=False)

                eng.wait_ge(vector_state, at_chunk("vector_state", "S_new1", l, NCH - 1))
                eng.wait_ge(scalar_state, at_chunk("scalar_state", "y1", l, NCH - 1))
                flat = lambda v: v.rearrange("p b i -> p (b i)")
                eng.sem_inc(tensor_idle, 1)
                with eng.Fori(0, 2) as i, e.rounds("dp", 2, i):
                    for j in range(2):
                        eng.wait_ge(vector_steps, e.at(f"dp_sa_in{j}"))
                        mm(bank[3 * j][:, :], bdones, flat(t1[j]), start=True, stop=True).then_inc(tensor_steps, e.step(f"dp_sa{j}"))
                        eng.wait_ge(vector_steps, e.at(f"dp_v_in{j}"))
                        mm(bank[3 * j + 1][:, :], bdones, flat(t2[j]), start=True, stop=True).then_inc(tensor_steps, e.step(f"dp_v{j}"))
                    for j in range(2):
                        eng.wait_ge(vector_steps, e.at(f"dp_r_in{j}"))
                        mm(bank[3 * j + 2][:, :], bdones, flat(t2[j]), start=True, stop=True).then_inc(tensor_steps, e.step(f"dp_y{j}"))
                eng.wait_ge(vector_steps, e.at("dec_y"))
                eng.wait_ge(wg_in, e.at("wg_in"))
                eng.wait_ge(scalar_steps, e.at("sig_gate"))
                eng.sem_inc(tensor_idle, 1)
                with eng.Fori(0, NC3) as c, e.rounds("fin", NC3, c):
                    seg = bass.ds(c * CW, CW)
                    for o in range(4):
                        eng.wait_ge(scalar_steps, e.at(f"fin_sd{o}", back=1))
                        mm(bank[o][:, 0:CW], bdones, yar[:, o, seg], start=True, stop=True).then_inc(tensor_steps, e.step(f"fin_mean{o}"))
                    for o in range(4):
                        eng.wait_ge(vector_steps, e.at(f"fin_out{o}", back=1))
                        eng.wait_ge(vector_steps, e.at(f"fin_rk{o}"))
                        mm(bank[4 + o][:, 0:CW], bdones, fbo[o][:, :], start=True, stop=True).then_inc(tensor_steps, e.step(f"fin_bonus{o}"))
                    for o in range(4):
                        oc = slice(128 * o, 128 * o + 128)
                        eng.wait_ge(scalar_steps, e.at(f"fin_sq{o}"))
                        mm(bank[o][:, 0:CW], bdones, fsq[o % 2][:, :], start=True, stop=True).then_inc(tensor_steps, e.step(f"fin_var{o}"))
                        eng.wait_ge(vector_steps, e.at(f"fin_bo{o}"))
                        mm(bank[4 + o][:, 0:CW], wg[:, 0, oc], proj[:, 13, seg], start=True, stop=False)
                        mm(bank[4 + o][:, 0:CW], wg[:, 1, oc], proj[:, 14, seg], start=False, stop=True).then_inc(tensor_steps, e.step(f"fin_gate{o}"))

                eng.wait_ge(pool_steps, e.at("fin_low3_all"))
                eng.wait_ge(scalar_steps, e.at("fin_high3"))
                eng.wait_ge(pool_steps, e.at("att_low_back"))
                for k in range(KT):
                    s = unit(NIN + k)
                    for c in range(NC3):
                        if k:
                            eng.wait_ge(vector_steps, e.at(f"wo_add{k - 1}{c}"))
                        tile(s, bank[c][:, 0:CW], c).then_inc(tensor_steps, e.step(f"wo_mm{k}{c}"))
                norm("n2")
                eng.sem_inc(tensor_idle, 1)
                with eng.Fori(0, NFF // 2) as i, e.rounds("ff", NFF // 2, i):
                    for j in range(2):
                        for w, n in ((0, "g"), (1, "u")):
                            s = unit(NIN + KT + 2 * j + w, i, 6)
                            for c in range(NC3):
                                prev = "sil" if n == "g" else "mid"
                                if j == w == 0:
                                    eng.wait_ge(vector_steps, e.at(f"n2{c}_low7"))
                                if j:
                                    eng.wait_ge(scalar_steps if n == "g" else vector_steps, e.at(f"ff_{prev}0{c}"))
                                else:
                                    eng.wait_ge(scalar_steps if n == "g" else vector_steps, e.at(f"ff_{prev}1{c}", back=1))
                                tile(s, bank[3 * w + c][:, 0:CW], c).then_inc(tensor_steps, e.step(f"ff_{n}{j}{c}"))
                    s = [unit(NIN + KT + 4 + j, i, 6) for j in range(2)]
                    for c in range(NC3):
                        eng.wait_ge(vector_steps, e.at(f"ff_low1{c}"))
                        for k in range(KT):
                            n = c * KT + k
                            eng.wait_ge(vector_steps, e.at(f"ff_add{(n - 2) % (3 * KT)}", back=int(n < 2)))
                            for j in range(2):
                                last = column(bank[6 + k % 2][:, 0:CW], s[j], slice(128 * k, 128 * k + 128),
                                              mh[:, j, cs(c)], ml[:, j, cs(c)], j == 0, j == 1)
                            last.then_inc(tensor_steps, e.step(f"ff_d{n}"))
                    e.also("ff_down_last")
            norm("nf")


def _consts():
    C = np.zeros((128, NCST), np.float32)
    put = lambda n, v: C.__setitem__((slice(None), slice(CST[n][0], CST[n][0] + CST[n][1])), v)
    r = np.arange(128)
    s, h = r % 64, r // 64
    col = np.arange(64)
    put("ident", np.eye(128))
    put("ones", 1.0)
    put("bdones", (h[:, None] == h[None, :]))
    put("II", (s[:, None] == col[None, :]))
    half = np.repeat(np.arange(2), 64)
    sameh = h[:, None] == half[None, :]
    c2 = np.tile(col, 2)
    put("bd", sameh)
    up, low = s[:, None] < c2[None, :], s[:, None] > c2[None, :]
    b16 = (s[:, None] // 16) == (c2[None, :] // 16)
    put("up", sameh & up)
    put("low", sameh & low)
    put("d16", np.concatenate([sameh & up & b16, sameh & low & b16], 1))
    u, w = s[:, None] < col[None, :], s[:, None] > col[None, :]
    k16 = (s[:, None] // 16) == (col[None, :] // 16)
    k32 = (s[:, None] // 32) == (col[None, :] // 32)
    put("upi", s[:, None] <= col[None, :])
    put("d16c", np.concatenate([u & k16, w & k16], 1))
    put("o32", np.concatenate([u & k32 & ~k16, w & k32 & ~k16], 1))
    put("o64", u & ~k32)
    inv = (10000.0 ** (-np.arange(32) / 32)).astype(np.float32)
    pos = np.concatenate([np.arange(NP_), np.full(NS, 1024)]).astype(np.float32)
    ang = (pos[None, :] * inv[r % 32][:, None]).astype(np.float32)
    rope = np.concatenate([np.cos(ang), np.sin(ang)], 1).astype(np.float32)
    rot = np.zeros((128, 128), np.float32)
    for m in range(128):
        dd = m % 64
        if dd < 32:
            rot[m + 32, m] = -1.0
        else:
            rot[m - 32, m] = 1.0
    S = np.zeros((2, 2, 128, 128), np.float32)
    for a in range(2):
        for b in range(2):
            S[a, b, a * 64 + col, b * 64 + col] = 1.0
    dup = [S[g, 0] + S[g, 1] for g in range(2)]
    mats = np.concatenate([rot, dup[0], dup[1], rot @ dup[0], rot @ dup[1], S[0, 0], S[0, 1], S[1, 0], S[1, 1]], 1)
    j = np.arange(256)
    diff = r[:, None] - j[None, :] + 128
    ok = (diff >= 0) & (diff < WIN)
    m = np.where(ok, 0.0, -1e30).astype(np.float32)
    m0 = np.where(ok & (j[None, :] >= 128), 0.0, -1e30).astype(np.float32)
    amask = np.concatenate([m0, m], 1)
    smask = np.ones((128, NCH, 65), np.float32)
    smask[:, :, 0] = 0.0
    return {"cst": C, "rope": rope, "mats": mats.astype(np.float32), "amask": amask, "smask": smask.reshape(128, -1)}


def _chan(v, tiles):
    v = np.asarray(v)
    return np.moveaxis(v.reshape(v.shape[0], tiles, 128, *v.shape[2:]), 1, 2)


def _pad(v, n, axis):
    out = list(v.shape)
    out[axis] = n - v.shape[axis]
    return np.concatenate([v, np.zeros(out, v.dtype)], axis)


def _lay_out(i):
    A = {k: np.asarray(v) for k, v in i.items()}
    z = dict(_consts())
    xall = np.concatenate([A["x_prompt"][0], A["x_sample"][:, 0]], 0)
    z["x"] = np.ascontiguousarray(xall.T.reshape(KT, 128, T).transpose(1, 0, 2)).reshape(128, KT * T)
    w = A["w_in"]
    w = np.concatenate([_pad(w[:, :, :1824], 1920, 2), w[:, :, 1824:]], 2)

    def tiles(w):
        ll, ki, no = w.shape
        return w.reshape(ll, ki // 128, 128, no // 128, 128).transpose(0, 3, 2, 1, 4).reshape(ll, no // 128, 128, ki)

    g, u = tiles(A["w_gate"]), tiles(A["w_up"])
    dn = A["w_down"].reshape(L, NFF, 128, DM)
    ff = np.stack([g[:, 0::2], u[:, 0::2], g[:, 1::2], u[:, 1::2], dn[:, 0::2], dn[:, 1::2]], 2).reshape(L, 3 * NFF, 128, U)
    wts = np.concatenate([tiles(w), tiles(A["w_out"]), ff], 1).reshape(L * UL, 128, U)
    z["wts"] = _pad(wts, L * UL + 6, 0)
    par = np.zeros((L, 128, NPAR), np.float32)

    def put(n, v, tiles):
        par[:, :, PAR[n]:PAR[n] + tiles] = _chan(v, tiles)

    put("an", A["attn_norm"], 8)
    put("fn", A["ffn_norm"], 8)
    put("mu", _pad(A["mu"], 1920, 1), 15)
    for n, k in (("w0", "w0"), ("a0", "a0"), ("k_k", "k_k"), ("k_a", "k_a"), ("lg", "lnx_g"), ("lb", "lnx_b")):
        put(n, A[k], 4)
    put("r_k", A["r_k"].reshape(L, 512), 4)
    par[:, :, PAR["sink"]:PAR["sink"] + 8] = A["sinks"][:, None, :]
    par[:, 0:8, PAR["sinkcol"]] = A["sinks"]
    z["par"] = par
    z["fin"] = _chan(A["final_norm"][None], 8)[0]
    z["shift"] = _chan(_pad(A["state_shift"].transpose(0, 2, 1), 1920, 1), 15).reshape(L, 128, 15 * 8)
    win = lambda c: c[:, :, 1:].transpose(0, 3, 4, 1, 2).reshape(L, 128, 8 * 127)
    z["kwin"], z["vwin"] = win(A["cache_k_win"]), win(A["cache_v_win"])
    zero = np.zeros((L, 64, 512), np.float32)
    z["wda"] = np.stack([np.concatenate([A["w_decay_up"], zero], 1), np.concatenate([zero, A["w_a_up"]], 1)], 2).reshape(L, 128, 1024)
    z["wg"] = _pad(A["w_g_up"], 256, 1).reshape(L, 2, 128, 512).transpose(0, 2, 1, 3).reshape(L, 128, 1024)
    st = A["state_rwkv"].reshape(L, 8, 4, 2, 64, 64).transpose(0, 3, 5, 2, 1, 4)
    z["states"] = st.reshape(L, 128, 2048)
    return {k: np.ascontiguousarray(v) for k, v in z.items()}


_OUT = {"o_y": (128, KT * T), "o_ps": (L, 128, 256), "o_shift": (L, 128, 135), "o_pk": (L, 128, 128), "o_pv": (L, 128, 128),
        "o_ss": (L, 128, 2048), "o_sk": (L, 128, 1024), "o_sv": (L, 128, 1024)}


def _declare(nc, arrays):
    d = {n: nc.dram_tensor(n, a.shape, F32, kind="ExternalInput").ap() for n, a in arrays.items()}
    for n, s in _OUT.items():
        d[n] = nc.dram_tensor(n, s, F32, kind="ExternalOutput").ap()
    d["x_keep"] = nc.dram_tensor("x_keep", (128, KT * T), F32).ap()
    d["att_keep"] = nc.dram_tensor("att_keep", (128, 4 * T), F32).ap()
    return d


def kernel(**inputs):
    import concourse.bacc as bacc
    from concourse.bass_utils import run_bass_kernel_spmd

    arrays = _lay_out(inputs)
    known = None
    for _ in range(2):
        nc = bacc.Bacc("TRN2", target_bir_lowering=False, num_devices=1)
        steps = Steps(known)
        program(nc, _declare(nc, arrays), steps)
        known = (steps.at, steps.per_round)
    return _results(run_bass_kernel_spmd(nc, [arrays], core_ids=[0]).results[0])


def _results(r):
    y = np.asarray(r["o_y"]).reshape(128, KT, T).transpose(2, 1, 0).reshape(T, DM)
    ps = np.asarray(r["o_ps"]).reshape(L, 2, 64, 4, 64).transpose(0, 3, 1, 4, 2).reshape(L, 1, 8, 64, 64)
    ss = np.asarray(r["o_ss"]).reshape(L, 2, 64, 4, 8, 64).transpose(0, 4, 3, 1, 5, 2).reshape(L, 8, 8, 64, 64)
    sh = np.asarray(r["o_shift"]).reshape(L, 128, 15, 9).transpose(0, 3, 2, 1).reshape(L, 9, 1920)[:, :, :1824]
    pk = np.asarray(r["o_pk"]).transpose(0, 2, 1).reshape(L, 1, 128, 2, 64)
    pv = np.asarray(r["o_pv"]).transpose(0, 2, 1).reshape(L, 1, 128, 2, 64)
    sk = np.asarray(r["o_sk"]).reshape(L, 128, 8, 128).transpose(0, 2, 3, 1).reshape(L, 8, 128, 2, 64)
    sv = np.asarray(r["o_sv"]).reshape(L, 128, 8, 128).transpose(0, 2, 3, 1).reshape(L, 8, 128, 2, 64)
    c = np.ascontiguousarray
    return (c(y[None, :NP_]), c(y[NP_:, None]), c(ps), c(sh[:, 0:1]), c(pk), c(pv), c(ss), c(sh[:, 1:9]), c(sk), c(sv))
```
